# Optimizing a Trainium2 kernel written in Bass

```python
import math
import jax, jax.numpy as jnp
from jax import lax
import numpy as np

D_MODEL = 1024
BATCH = 1
SEQ = 256
DEPTH = 2

CTX_LEN = 256
GRID_W = 64

MLA_HEADS = 4
QK_NOPE = 64
QK_ROPE = 32
V_DIM = 64
Q_LORA = 256
KV_LORA = 128
ATTN_W = MLA_HEADS * V_DIM
Q_BLOCK = 128
ROPE_BASE = 10000.0
AXIS_DIM = QK_ROPE // 2
AXIS_FREQS = AXIS_DIM // 2

CONV_W = 256
CONV_K = 31

FOURIER_W = 256
FOURIER_GROUPS = 4
FOURIER_GDIM = FOURIER_W // FOURIER_GROUPS

SGU_W = 256
SGU_GROUPS = 4
SGU_GDIM = SGU_W // SGU_GROUPS
CHUNK = 128

MIX_W = ATTN_W + CONV_W + FOURIER_W + SGU_W

Q_OFF = 0
KV_OFF = Q_OFF + Q_LORA
ROPE_OFF = KV_OFF + KV_LORA
CONV_OFF = ROPE_OFF + QK_ROPE
FOUR_OFF = CONV_OFF + 2 * CONV_W
SGU_OFF = FOUR_OFF + FOURIER_W
GATE_OFF = SGU_OFF + 2 * SGU_W
IN_DIM = GATE_OFF + MIX_W

RMS_EPS = 1e-6
LN_EPS = 1e-5


def _rmsnorm(x, g):
    xf = x.astype(jnp.float32)
    y = xf * lax.rsqrt(jnp.mean(xf * xf, axis=-1, keepdims=True) + RMS_EPS)
    return (y * g.astype(jnp.float32)).astype(x.dtype)

def _layernorm(x, g, b):
    xf = x.astype(jnp.float32)
    mu = jnp.mean(xf, axis=-1, keepdims=True)
    var = jnp.mean(jnp.square(xf - mu), axis=-1, keepdims=True)
    y = (xf - mu) * lax.rsqrt(var + LN_EPS)
    return (y * g.astype(jnp.float32) + b.astype(jnp.float32)).astype(x.dtype)

def _axial_tables(n_tokens):
    rows = n_tokens // GRID_W
    row = jnp.broadcast_to(jnp.arange(rows)[:, None], (rows, GRID_W)).reshape(-1).astype(jnp.float32)
    col = jnp.broadcast_to(jnp.arange(GRID_W)[None, :], (rows, GRID_W)).reshape(-1).astype(jnp.float32)
    inv = ROPE_BASE ** (-jnp.arange(0, AXIS_DIM, 2, dtype=jnp.float32) / AXIS_DIM)
    ang = jnp.stack([row[:, None] * inv, col[:, None] * inv], axis=1)
    return jnp.cos(ang), jnp.sin(ang)

def _rope2d(x, cos, sin):
    shp = (1, cos.shape[0]) + (1,) * (x.ndim - 3) + (2, AXIS_FREQS)
    c = cos.reshape(shp)
    s = sin.reshape(shp)
    xr = x.astype(jnp.float32).reshape(x.shape[:-1] + (2, 2, AXIS_FREQS))
    x1, x2 = xr[..., 0, :], xr[..., 1, :]
    out = jnp.stack([x1 * c - x2 * s, x1 * s + x2 * c], axis=-2)
    return out.reshape(x.shape).astype(x.dtype)

def _mla_q(q_part, p):
    b, n, _ = q_part.shape
    c_q = _rmsnorm(q_part, p["q_norm_g"])
    return (c_q @ p["w_uq"]).reshape(b, n, MLA_HEADS, QK_NOPE + QK_ROPE)

def _mla_kv(kv_part, p):
    b, n, _ = kv_part.shape
    c_kv = _rmsnorm(kv_part[..., :KV_LORA], p["kv_norm_g"])
    kv = (c_kv @ p["w_ukv"]).reshape(b, n, MLA_HEADS, QK_NOPE + V_DIM)
    return kv[..., :QK_NOPE], kv_part[..., KV_LORA:], kv[..., QK_NOPE:]

def _assemble_k(k_nope, k_rope):
    k_r = jnp.broadcast_to(k_rope[:, :, None, :], k_nope.shape[:3] + (QK_ROPE,))
    return jnp.concatenate([k_nope, k_r], axis=-1)

def _attend(q, k, v):
    scale = 1.0 / math.sqrt(QK_NOPE + QK_ROPE)
    s = jnp.einsum("bqhd,bkhd->bhqk", q, k, preferred_element_type=jnp.float32) * scale
    pr = jax.nn.softmax(s, axis=-1)
    return jnp.einsum("bhqk,bkhd->bqhd", pr.astype(v.dtype), v)

def _block_attention(q, k, v):
    b, n, h, dk = q.shape
    nb = n // Q_BLOCK
    qb = q.reshape(b, nb, Q_BLOCK, h, dk).swapaxes(0, 1)
    ob = lax.map(lambda qq: _attend(qq, k, v), qb)
    return ob.swapaxes(0, 1).reshape(b, n, h * V_DIM)

def _conv_module(a, p):
    glu = a[..., :CONV_W] * jax.nn.sigmoid(a[..., CONV_W:])
    y = lax.conv_general_dilated(
        glu, p["conv_w"][:, None, :].astype(glu.dtype), window_strides=(1,),
        padding=[(CONV_K // 2, CONV_K // 2)], dimension_numbers=("NWC", "WIO", "NWC"),
        feature_group_count=CONV_W)
    y = y + p["conv_b"]
    y = jax.nn.silu(_layernorm(y, p["conv_ln_g"], p["conv_ln_b"]))
    return y @ p["w_pw"] + p["b_pw"]

def _fourier(f, p):
    b, n, _ = f.shape
    fg = f.astype(jnp.float32).reshape(b, n, FOURIER_GROUPS, FOURIER_GDIM)
    mixed = jnp.fft.fft2(fg, axes=(1, 3), norm="ortho").real.reshape(b, n, FOURIER_W).astype(f.dtype)
    return mixed @ p["w_fourier"] + p["b_fourier"]

def _spatial_gating(uv, p):
    u, v = uv[..., :SGU_W], uv[..., SGU_W:]
    v = _layernorm(v, p["sgu_ln_g"], p["sgu_ln_b"])
    b, n, _ = v.shape
    vc = v.reshape(b, n // CHUNK, CHUNK, SGU_GROUPS, SGU_GDIM)
    mixed = jnp.einsum("gij,bnjgc->bnigc", p["w_s"], vc) + p["b_s"].T[None, None, :, :, None]
    return u * mixed.reshape(b, n, SGU_W)

def _branches(hp, attn, p):
    conv = _conv_module(hp[..., CONV_OFF:FOUR_OFF], p)
    four = _fourier(hp[..., FOUR_OFF:SGU_OFF], p)
    sgu = _spatial_gating(hp[..., SGU_OFF:GATE_OFF], p)
    y = jnp.concatenate([attn, conv, four, sgu], axis=-1) * jax.nn.silu(hp[..., GATE_OFF:])
    return y @ p["w_out"]

def _layer(x, xc, c, c_ctx, p, cos, sin, need_ctx_out):
    shift, scale, gate = jnp.split(jax.nn.silu(c) @ p["w_ada"] + p["b_ada"], 3, axis=-1)
    shift_c, scale_c, gate_c = jnp.split(jax.nn.silu(c_ctx) @ p["w_ada"] + p["b_ada"], 3, axis=-1)
    h = _rmsnorm(x, p["norm_g"]) * (1.0 + scale[:, None, :]) + shift[:, None, :]
    hc = _rmsnorm(xc, p["norm_g"]) * (1.0 + scale_c) + shift_c

    hp = h @ p["w_in"]
    if need_ctx_out:
        hpc = hc @ p["w_in"]
        ctx_kv = hpc[..., KV_OFF:CONV_OFF]
    else:
        ctx_kv = hc @ p["w_in"][:, KV_OFF:CONV_OFF]

    kn_c, kr_c, v_c = _mla_kv(ctx_kv, p)
    k_c = _assemble_k(kn_c, kr_c)

    q = _mla_q(hp[..., Q_OFF:KV_OFF], p)
    q = jnp.concatenate([q[..., :QK_NOPE], _rope2d(q[..., QK_NOPE:], cos, sin)], axis=-1)
    kn, kr, v = _mla_kv(hp[..., KV_OFF:CONV_OFF], p)
    k = _assemble_k(kn, _rope2d(kr, cos, sin))
    k_all = jnp.concatenate([k, k_c], axis=1)
    v_all = jnp.concatenate([v, v_c], axis=1)
    attn = _block_attention(q, k_all, v_all)

    x = x + gate[:, None, :] * _branches(hp, attn, p)

    if need_ctx_out:
        q_c = _mla_q(hpc[..., Q_OFF:KV_OFF], p)
        b, l = xc.shape[0], xc.shape[1]
        attn_c = _attend(q_c, k_c, v_c).reshape(b, l, ATTN_W)
        xc = xc + gate_c * _branches(hpc, attn_c, p)
    return x, xc

def first_inputs(seed: int = 0) -> dict:
    key = jax.random.key(seed)
    ks = iter(jax.random.split(key, 40))
    f32 = jnp.float32

    def nrm(shape, s):
        return jax.random.normal(next(ks), shape, f32) * s

    def gain(shape):
        return 1.0 + 0.02 * jax.random.normal(next(ks), shape, f32)

    L = DEPTH
    return {
        "x": nrm((BATCH, SEQ, D_MODEL), 1.0),
        "c": nrm((BATCH, D_MODEL), 1.0),
        "ctx": nrm((BATCH, CTX_LEN, D_MODEL), 1.0),
        "c_ctx": nrm((D_MODEL,), 1.0),
        "w_ada": nrm((L, D_MODEL, 3 * D_MODEL), 0.5 * D_MODEL ** -0.5),
        "b_ada": nrm((L, 3 * D_MODEL), 0.01),
        "norm_g": gain((L, D_MODEL)),
        "w_in": nrm((L, D_MODEL, IN_DIM), D_MODEL ** -0.5),
        "q_norm_g": gain((L, Q_LORA)),
        "w_uq": nrm((L, Q_LORA, MLA_HEADS * (QK_NOPE + QK_ROPE)), Q_LORA ** -0.5),
        "kv_norm_g": gain((L, KV_LORA)),
        "w_ukv": nrm((L, KV_LORA, MLA_HEADS * (QK_NOPE + V_DIM)), KV_LORA ** -0.5),
        "conv_w": nrm((L, CONV_K, CONV_W), CONV_K ** -0.5),
        "conv_b": nrm((L, CONV_W), 0.01),
        "conv_ln_g": gain((L, CONV_W)),
        "conv_ln_b": nrm((L, CONV_W), 0.01),
        "w_pw": nrm((L, CONV_W, CONV_W), CONV_W ** -0.5),
        "b_pw": nrm((L, CONV_W), 0.01),
        "w_fourier": nrm((L, FOURIER_W, FOURIER_W), FOURIER_W ** -0.5),
        "b_fourier": nrm((L, FOURIER_W), 0.01),
        "sgu_ln_g": gain((L, SGU_W)),
        "sgu_ln_b": nrm((L, SGU_W), 0.01),
        "w_s": nrm((L, SGU_GROUPS, CHUNK, CHUNK), 0.5 * CHUNK ** -0.5),
        "b_s": 1.0 + nrm((L, SGU_GROUPS, CHUNK), 0.1),
        "w_out": nrm((L, MIX_W, D_MODEL), MIX_W ** -0.5),
        "final_g": gain((D_MODEL,)),
    }

def first_block(x, c, ctx, c_ctx, w_ada, b_ada, norm_g, w_in, q_norm_g, w_uq, kv_norm_g, w_ukv,
              conv_w, conv_b, conv_ln_g, conv_ln_b, w_pw, b_pw, w_fourier, b_fourier,
              sgu_ln_g, sgu_ln_b, w_s, b_s, w_out, final_g):
    n_tokens = x.shape[1]
    cos, sin = _axial_tables(n_tokens)
    xc = ctx
    for i in range(DEPTH):
        p = {
            "w_ada": w_ada[i], "b_ada": b_ada[i], "norm_g": norm_g[i], "w_in": w_in[i],
            "q_norm_g": q_norm_g[i], "w_uq": w_uq[i], "kv_norm_g": kv_norm_g[i], "w_ukv": w_ukv[i],
            "conv_w": conv_w[i], "conv_b": conv_b[i], "conv_ln_g": conv_ln_g[i], "conv_ln_b": conv_ln_b[i],
            "w_pw": w_pw[i], "b_pw": b_pw[i], "w_fourier": w_fourier[i], "b_fourier": b_fourier[i],
            "sgu_ln_g": sgu_ln_g[i], "sgu_ln_b": sgu_ln_b[i], "w_s": w_s[i], "b_s": b_s[i],
            "w_out": w_out[i],
        }
        x, xc = _layer(x, xc, c, c_ctx, p, cos, sin, need_ctx_out=(i < DEPTH - 1))
    return _rmsnorm(x, final_g)


N_MIX_HEADS = 16
HEAD_DIM = D_MODEL // N_MIX_HEADS
N_HEADS_DIL = 6
DILATED_PAIRS = ((128, 1), (512, 4), (2048, 16))
N_HEADS_DIFF = 4
DIFF_QK_DIM = HEAD_DIM // 2
N_HEADS_SB = 6
D_MIX = (N_HEADS_DIL + N_HEADS_DIFF + N_HEADS_SB) * HEAD_DIM
IN_SIZES = (N_HEADS_DIL * HEAD_DIM,) * 3 + (N_HEADS_DIFF * 2 * DIFF_QK_DIM,) * 2 + (N_HEADS_DIFF * HEAD_DIM,) + (N_HEADS_SB * HEAD_DIM,) * 3
D_IN = sum(IN_SIZES)
D_FF = 2816
NORM_EPS = 1e-6
N_NORMS = 6


def rmsnorm(x, g):
    xf = x.astype(jnp.float32)
    y = xf * lax.rsqrt(jnp.mean(xf * xf, axis=-1, keepdims=True) + NORM_EPS)
    return (y * g.astype(jnp.float32)).astype(x.dtype)

def swiglu(h, w_gate, w_up, w_down):
    return (jax.nn.silu(h @ w_gate) * (h @ w_up)) @ w_down

def alibi_slopes(n):
    return 2.0 ** (-8.0 * jnp.arange(1, n + 1, dtype=jnp.float32) / n)

def to_heads(t, n_heads):
    b, s, _ = t.shape
    return t.reshape(b, s, n_heads, -1).transpose(0, 2, 1, 3)

def from_heads(t):
    b, h, s, dh = t.shape
    return t.transpose(0, 2, 1, 3).reshape(b, s, h * dh)

def query_blocks(t):
    b, h, s, dh = t.shape
    return t.reshape(b, h, s // Q_BLOCK, Q_BLOCK, dh).transpose(2, 0, 1, 3, 4)

def merge_blocks(t):
    nq, b, h, q, dh = t.shape
    return t.transpose(1, 2, 0, 3, 4).reshape(b, h, nq * q, dh)

def dilated_branch(q, k, v, slopes, window, dilation):
    b, h, s, dh = q.shape
    n_back = window // dilation
    chunk = dilation * n_back
    sp = -(-s // chunk) * chunk
    seg = sp // dilation
    nb = seg // n_back

    def split(t):
        t = jnp.pad(t, ((0, 0), (0, 0), (0, sp - s), (0, 0)))
        t = t.reshape(b, h, seg, dilation, dh).transpose(0, 1, 3, 2, 4)
        return t.reshape(b, h, dilation, nb, n_back, dh)

    def with_prev(t):
        prev = jnp.concatenate([jnp.zeros_like(t[:, :, :, :1]), t[:, :, :, :-1]], axis=3)
        return jnp.concatenate([prev, t], axis=4)

    qb = split(q)
    kk = with_prev(split(k))
    vv = with_prev(split(v))
    sc = jnp.einsum('bhrnqd,bhrnkd->bhrnqk', qb, kk, preferred_element_type=jnp.float32)
    qi = jnp.arange(n_back)[:, None]
    ki = jnp.arange(2 * n_back)[None, :]
    dist = n_back + qi - ki
    band = (dist >= 0) & (dist <= n_back)
    first = (jnp.arange(nb) == 0)[:, None, None] & (ki < n_back)[None]
    valid = band[None] & ~first
    sc = sc - slopes[None, :, None, None, None, None] * (dilation * dist).astype(jnp.float32)
    sc = jnp.where(valid, sc, -jnp.inf)
    m = jnp.max(sc, axis=-1, keepdims=True)
    p = jnp.exp(sc - m)
    den = jnp.sum(p, axis=-1)
    o = jnp.einsum('bhrnqk,bhrnkd->bhrnqd', p, vv, preferred_element_type=jnp.float32) / den[..., None]
    lse = m[..., 0] + jnp.log(den)
    o = o.reshape(b, h, dilation, seg, dh).transpose(0, 1, 3, 2, 4).reshape(b, h, sp, dh)[:, :, :s]
    lse = lse.reshape(b, h, dilation, seg).transpose(0, 1, 3, 2).reshape(b, h, sp)[:, :, :s]
    return o, lse

def dilated_attention(q, k, v):
    slopes = alibi_slopes(q.shape[1])
    outs, lses = zip(*[dilated_branch(q, k, v, slopes, w, d) for (w, d) in DILATED_PAIRS])
    wts = jax.nn.softmax(jnp.stack(lses), axis=0)
    return jnp.sum(wts[..., None] * jnp.stack(outs), axis=0)

def differential_attention(q1, q2, k1, k2, v, lam):
    s = q1.shape[2]
    slopes = alibi_slopes(q1.shape[1])
    kpos = jnp.arange(s)
    starts = jnp.arange(s // Q_BLOCK) * Q_BLOCK

    def block(args):
        start, a, c = args
        rel = (start + jnp.arange(Q_BLOCK))[:, None] - kpos[None, :]
        bias = jnp.where(rel >= 0, -slopes[:, None, None] * rel.astype(jnp.float32), -jnp.inf)
        a1 = jax.nn.softmax(jnp.einsum('bhqd,bhkd->bhqk', a, k1, preferred_element_type=jnp.float32) + bias, axis=-1)
        a2 = jax.nn.softmax(jnp.einsum('bhqd,bhkd->bhqk', c, k2, preferred_element_type=jnp.float32) + bias, axis=-1)
        return jnp.einsum('bhqk,bhkd->bhqd', a1 - lam * a2, v, preferred_element_type=jnp.float32)

    return merge_blocks(lax.map(block, (starts, query_blocks(q1), query_blocks(q2))))

def stick_breaking_attention(q, k, v):
    s = q.shape[2]
    kpos = jnp.arange(s)
    starts = jnp.arange(s // Q_BLOCK) * Q_BLOCK

    def block(args):
        start, a = args
        valid = kpos[None, :] < (start + jnp.arange(Q_BLOCK))[:, None]
        z = jnp.einsum('bhqd,bhkd->bhqk', a, k, preferred_element_type=jnp.float32)
        log_fail = jnp.where(valid, jax.nn.log_sigmoid(-z), 0.0)
        after = lax.cumsum(log_fail, axis=3, reverse=True) - log_fail
        wts = jnp.where(valid, jnp.exp(jax.nn.log_sigmoid(z) + after), 0.0)
        return jnp.einsum('bhqk,bhkd->bhqd', wts, v, preferred_element_type=jnp.float32)

    return merge_blocks(lax.map(block, (starts, query_blocks(q))))

def token_mixer(h, w_in, w_out, lam_params, subln_gain, layer):
    proj = h @ w_in
    idx = [int(i) for i in np.cumsum(IN_SIZES)[:-1]]
    qa, ka, va, qb, kb, vb, qc, kc, vc = jnp.split(proj, idx, axis=-1)
    b, s, _ = h.shape
    o_a = dilated_attention(to_heads(qa, N_HEADS_DIL) * (HEAD_DIM ** -0.5), to_heads(ka, N_HEADS_DIL), to_heads(va, N_HEADS_DIL))
    qb = qb.reshape(b, s, N_HEADS_DIFF, 2, DIFF_QK_DIM).transpose(0, 2, 3, 1, 4) * (DIFF_QK_DIM ** -0.5)
    kb = kb.reshape(b, s, N_HEADS_DIFF, 2, DIFF_QK_DIM).transpose(0, 2, 3, 1, 4)
    lam_init = 0.8 - 0.6 * math.exp(-0.3 * layer)
    lam = jnp.exp(jnp.sum(lam_params[0] * lam_params[1])) - jnp.exp(jnp.sum(lam_params[2] * lam_params[3])) + lam_init
    o_b = differential_attention(qb[:, :, 0], qb[:, :, 1], kb[:, :, 0], kb[:, :, 1], to_heads(vb, N_HEADS_DIFF), lam.astype(jnp.float32))
    o_b = rmsnorm(o_b, subln_gain) * (1.0 - lam_init)
    o_c = stick_breaking_attention(to_heads(qc, N_HEADS_SB) * (HEAD_DIM ** -0.5), to_heads(kc, N_HEADS_SB), to_heads(vc, N_HEADS_SB))
    mixed = jnp.concatenate([from_heads(o_a), from_heads(o_b), from_heads(o_c)], axis=-1).astype(h.dtype)
    return mixed @ w_out

def second_inputs(seed: int = 0) -> dict:
    key = jax.random.key(seed)
    ks = jax.random.split(key, 10)
    f32 = jnp.float32
    x = jax.random.normal(ks[0], (BATCH, SEQ, D_MODEL), f32)
    norm_gains = 1.0 + 0.02 * jax.random.normal(ks[1], (DEPTH, N_NORMS, D_MODEL), f32)
    w_ffn_gate = jax.random.normal(ks[2], (DEPTH, 2, D_MODEL, D_FF), f32) * D_MODEL ** -0.5
    w_ffn_up = jax.random.normal(ks[3], (DEPTH, 2, D_MODEL, D_FF), f32) * D_MODEL ** -0.5
    w_ffn_down = jax.random.normal(ks[4], (DEPTH, 2, D_FF, D_MODEL), f32) * D_FF ** -0.5
    w_in = jax.random.normal(ks[5], (DEPTH, D_MODEL, D_IN), f32) * D_MODEL ** -0.5
    w_out = jax.random.normal(ks[6], (DEPTH, D_MIX, D_MODEL), f32) * D_MIX ** -0.5
    diff_lambda = 0.1 * jax.random.normal(ks[7], (DEPTH, 4, DIFF_QK_DIM), f32)
    diff_subln_gain = 1.0 + 0.02 * jax.random.normal(ks[8], (DEPTH, HEAD_DIM), f32)
    return {"x": x, "norm_gains": norm_gains, "w_ffn_gate": w_ffn_gate, "w_ffn_up": w_ffn_up,
            "w_ffn_down": w_ffn_down, "w_in": w_in, "w_out": w_out,
            "diff_lambda": diff_lambda, "diff_subln_gain": diff_subln_gain}

def second_block(x, norm_gains, w_ffn_gate, w_ffn_up, w_ffn_down, w_in, w_out, diff_lambda, diff_subln_gain):
    for layer in range(DEPTH):
        g = norm_gains[layer]
        h = rmsnorm(x, g[0])
        x = x + 0.5 * rmsnorm(swiglu(h, w_ffn_gate[layer, 0], w_ffn_up[layer, 0], w_ffn_down[layer, 0]), g[1])
        h = rmsnorm(x, g[2])
        x = x + rmsnorm(token_mixer(h, w_in[layer], w_out[layer], diff_lambda[layer], diff_subln_gain[layer], layer), g[3])
        h = rmsnorm(x, g[4])
        x = x + 0.5 * rmsnorm(swiglu(h, w_ffn_gate[layer, 1], w_ffn_up[layer, 1], w_ffn_down[layer, 1]), g[5])
    return x


def setup_inputs(seed=0):
    out = dict(first_inputs(seed))
    for name, value in second_inputs(seed + 1).items():
        if name != "x":
            out[name + "_2"] = value
    return out


def reference(
    x, c, ctx, c_ctx, w_ada, b_ada, norm_g, w_in, q_norm_g, w_uq, kv_norm_g, w_ukv, conv_w,
    conv_b, conv_ln_g, conv_ln_b, w_pw, b_pw, w_fourier, b_fourier, sgu_ln_g, sgu_ln_b, w_s,
    b_s, w_out, final_g, norm_gains_2, w_ffn_gate_2, w_ffn_up_2, w_ffn_down_2, w_in_2, w_out_2,
    diff_lambda_2, diff_subln_gain_2,
):
    x = first_block(
        x, c, ctx, c_ctx, w_ada, b_ada, norm_g, w_in, q_norm_g, w_uq, kv_norm_g, w_ukv, conv_w,
        conv_b, conv_ln_g, conv_ln_b, w_pw, b_pw, w_fourier, b_fourier, sgu_ln_g, sgu_ln_b, w_s,
        b_s, w_out, final_g,
    )
    return second_block(
        x, norm_gains_2, w_ffn_gate_2, w_ffn_up_2, w_ffn_down_2, w_in_2, w_out_2, diff_lambda_2,
        diff_subln_gain_2,
    )


_drawn_inputs = setup_inputs


def setup_inputs(seed=0):
    import zlib

    import numpy as np

    out = dict(_drawn_inputs(seed))
    spreads = {}
    factors = {'ctx': 4.5,
     'b_ada': 3.865,
     'norm_g': 5.325,
     'q_norm_g': 8.0,
     'kv_norm_g': 8.0,
     'conv_b': 8.0,
     'conv_ln_g': 8.0,
     'conv_ln_b': 35.131,
     'b_pw': 25.939,
     'b_fourier': 23.341,
     'sgu_ln_g': 8.0,
     'sgu_ln_b': 8.0,
     'diff_subln_gain_2': 14.577}
    for name, (base, spread) in spreads.items():
        noise = np.random.default_rng([zlib.crc32(name.encode()), seed]).standard_normal(out[name].shape)
        drawn = base * np.exp(spread * noise) if base else spread * noise
        out[name] = __import__('jax').numpy.asarray(drawn.astype(out[name].dtype))
    for name, factor in factors.items():
        out[name] = (out[name] * factor).astype(out[name].dtype)
    return out
```

```python
from contextlib import ExitStack

import numpy as np
import concourse.bass as bass
from concourse import mybir

F32 = mybir.dt.float32
ACT = mybir.ActivationFunctionType
ALU = mybir.AluOpType
AXX = mybir.AxisListType.X

P = 128
D = 1024
KD = D // P
T = 256
TT = 512
RMS_EPS = 1e-6
LN_EPS = 1e-5

HEADS = 4
NOPE = 64
ROPE = 32
QK = NOPE + ROPE
CONV_K = 31
PAD = CONV_K // 2
SEGP = T + 2 * PAD
FG_DIM = 64
ADA_SLOTS = 12
WIN_SLOTS = [(0, 256), (256, 160), (416, 256), (672, 256), (928, 256), (1184, 256), (1440, 256),
             (1696, 256), (1952, 256), (2208, 256), (2464, 256)]
R_BADA, R_NORM, R_QN, R_KVN, R_CW, R_CB, R_CLG, R_CLB, R_BPW, R_BF, R_C = 0, 24, 32, 34, 35, 97, 99, 101, 103, 105, 107
R_B1 = 107 + 16
R_SUB = 48

N_DIL, N_DIFF, N_SB = 6, 4, 6
FF = 2816
FFN_PAIRS = FF // (2 * P)
FFN_CHUNKS = FF // P
FFN_SLOTS = 3 * FFN_PAIRS
NEG = -1.0e30
RING = 6


class Marks:

    def __init__(self, nc, ctx, table):
        self.nc, self.ctx, self.table = nc, ctx, table
        self.sems, self.counts = {}, {}

    def sem(self, stage):
        if stage not in self.sems:
            self.sems[stage] = self.ctx.enter_context(self.nc.semaphore(stage))
        return self.sems[stage]

    def done(self, stage, *key):
        s = self.sem(stage)
        self.counts[stage] = self.counts.get(stage, 0) + 1
        self.table[(stage,) + key] = self.counts[stage]
        return s, 1

    def at(self, stage, *key):
        return self.sem(stage), self.table.get((stage,) + key, 1)


def constants():
    f = np.float32
    out = {}
    i = np.arange(P)
    ident = np.eye(P, dtype=f)
    ones = np.ones((P, P), f)
    heads2 = np.kron(np.eye(2), np.ones((64, 64))).astype(f) / 64
    ntri = -(i[:, None] >= i[None, :]).astype(f)
    a = 2 * np.pi * np.outer(np.arange(FG_DIM), np.arange(FG_DIM)) / FG_DIM
    scale = 1.0 / np.sqrt(T * FG_DIM)
    dft_d = np.concatenate([np.kron(np.eye(2), np.cos(a)), np.kron(np.eye(2), -np.sin(a))], 1) * scale
    b = 2 * np.pi * (np.outer(np.arange(T), np.arange(T)) % T) / T
    dft_n = np.stack([np.cos(b), np.sin(b)]).reshape(2, 2, P, T).transpose(2, 0, 1, 3).reshape(P, -1)
    strict = (i[:, None] < i[None, :]).astype(f)
    full = np.concatenate([strict, ones, strict], 1)
    gap = np.where(full > 0, 0.0, NEG)
    rows = T // 64
    inv = (f(10000.0) ** (-np.arange(0, 16, 2, dtype=f) / f(16))).astype(f)
    row = np.repeat(np.arange(rows), 64).astype(f)
    col = np.tile(np.arange(64), rows).astype(f)
    ang = np.stack([row[:, None] * inv, col[:, None] * inv], 1).astype(f)
    rope = np.zeros((P, 2 * T), f)
    for d in range(ROPE):
        ax, half, fr = d // 16, (d % 16) // 8, d % 8
        rope[NOPE + d, :T] = np.cos(ang[:, ax, fr])
        rope[NOPE + d, T:] = np.sin(ang[:, ax, fr]) * (1 if half else -1)
    out["k_base"] = np.concatenate([ident, ones, heads2, ntri, -ones, dft_d, dft_n, full, gap, rope], 1).astype(f)
    q = np.concatenate([np.tile(i[:, None], (1, P)), np.tile(P + i[:, None], (1, T))], 1)
    k = np.concatenate([i, np.arange(T)])[None, :]
    dist = q - k
    tabs = []
    count = (dist <= 128).astype(int) + (dist % 4 == 0) + (dist % 16 == 0)
    for h in range(N_DIL):
        slope = 2.0 ** (-8.0 * (h + 1) / N_DIL)
        ok = (dist >= 0) & (count > 0)
        tabs.append(np.where(ok, -slope * dist + np.log(np.maximum(count, 1)), NEG))
    for h in range(N_DIFF):
        slope = 2.0 ** (-8.0 * (h + 1) / N_DIFF)
        tabs.append(np.where(dist >= 0, -slope * dist, NEG))
    out["k_alibi"] = np.concatenate(tabs, 1).astype(f)
    return out


C_ID, C_ONES, C_H2, C_NTRI, C_NONE, C_DD, C_DN, C_FULL, C_GAP, C_ROPE, C_END = (
    0, 128, 256, 384, 512, 640, 896, 1920, 2304, 2688, 3200)

LAM_INIT = [0.8 - 0.6 * float(np.exp(-0.3 * m)) for m in range(2)]


def projection_banks():
    out = []
    for L in range(2):
        names = [("q", 0), ("q", 1), ("kv",), ("kr",), ("krs",)]
        names += [(n, j) for n in "agfu" for j in range(2)]
        names += [("v", t) for t in range(4 if L == 0 else 2)] + [("gate", j) for j in range(8)]
        out.append({(n if len(n) > 1 else n[0]): i % 4 for i, n in enumerate(names)})
    return out


PB = projection_banks()
YB = [{(t, h): 2 * t + h for t in range(4) for h in range(2)}, {(t, h): 4 + 2 * t + h for t in range(2) for h in range(2)}]
BLOCKS2 = ([("qk", b) for b in range(6)] + [("v", b) for b in range(3)] + [("qk", b) for b in range(6, 10)]
           + [("v", b) for b in (3, 4)] + [("qk", b) for b in range(10, 16)] + [("v", b) for b in (5, 6, 7)])
PB2 = {b: i % 4 for i, b in enumerate(BLOCKS2)}
VAFTER = {5: (0, 1, 2), 9: (3, 4), 15: (5, 6, 7)}
QKSC = [0.125] * 3 + [1.0] * 3 + [32 ** -0.5] * 2 + [1.0] * 2 + [0.125] * 3 + [1.0] * 3
UNIT_HEAD = list(range(N_DIL)) + [h for d in range(N_DIFF) for h in (None, N_DIL + d)]


def program(nc, I, out, table):
    ctx = ExitStack()
    with ctx:
        def sb(name, shape):
            return ctx.enter_context(nc.sbuf_tensor(name, shape, F32))

        M = Marks(nc, ctx, table)
        done, at = M.done, M.at

        ring = sb("weight_ring", [P, RING, 2048])
        X = sb("residual", [P, 4, D])
        SG = sb("gated", [P, KD, TT])
        XN = SG[:, :, :].rearrange("p a b -> p (a b)").rearrange("p (t d) -> p t d", t=4)
        hT = sb("hT", [P, KD, TT])
        GB = hT[:, :, :].rearrange("p a b -> p (a b)").rearrange("p (v d) -> p v d", v=4)
        KB = sb("const_base", [P, C_END])
        vec = sb("vectors", [P, 3, P])
        vT = sb("vectors_T", [P, 3, P])
        CS = sb("silu_c", [P, 16])
        ada = sb("ada", [P, 24, 2])
        adag = sb("ada_gain", [P, KD, 2])
        stat = sb("stat", [P, 64])
        eps = sb("eps", [P, 4])
        gate_diag = sb("gate_diag", [P, 2, 512])
        gain_row = sb("gain_row", [P, D])
        ytmp = sb("scaled_out", [P, 2, 512])
        bsrow = sb("b_s_row", [1, 1024])[:, :].rearrange("p (l n) -> p l n", l=2)
        lam_in = sb("lambda_in", [P, 2, 128])
        lamv = sb("lambda", [P, 2, 8])
        arena = sb("arena", [P, 19320])
        room = [0]

        def carve(n):
            a = room[0]
            room[0] += n
            assert room[0] <= 19320
            return arena[:, a:a + n]

        w_uq = carve(768).rearrange("p (j n) -> p j n", j=2)
        w_uqs = carve(256).rearrange("p (j n) -> p j n", j=2)
        w_ukv = carve(512)
        w_pw = carve(512).rearrange("p (j n) -> p j n", j=2)
        w_fo = carve(512).rearrange("p (j n) -> p j n", j=2)
        w_s = carve(512).rearrange("p (g n) -> p g n", g=4)
        wsT = carve(512).rearrange("p (g n) -> p g n", g=4)
        w_krs = carve(256).rearrange("p (k n) -> p k n", k=8)
        sgu_row = carve(512).rearrange("p (a n) -> p a n", a=2)
        qp = carve(1024).rearrange("p (j n) -> p j n", j=2)
        kvp = carve(512)
        sq = carve(1536).rearrange("p (j n) -> p j n", j=3)
        rq = carve(1024).rearrange("p (j n) -> p j n", j=2)
        krot = carve(512)
        CG = carve(4 * SEGP).rearrange("p (j s n) -> p j s n", j=2, s=2)
        cacc = carve(1024).rearrange("p (j n) -> p j n", j=2)
        csg = carve(1024).rearrange("p (j n) -> p j n", j=2)
        fT = carve(1024).rearrange("p (j n) -> p j n", j=2)
        FA = carve(2048).rearrange("p (t j n) -> p t j n", t=4, j=2)
        U = carve(1024).rearrange("p (j n) -> p j n", j=2)
        VN = carve(1024).rearrange("p (t n) -> p t n", t=4)
        Q = carve(2048).rearrange("p (h n) -> p h n", h=4)
        K = FA.rearrange("p t j n -> p (t j n)").rearrange("p (h n) -> p h n", h=4)
        V = fT.rearrange("p j n -> p (j n)").rearrange("p (t n) -> p t n", t=4)
        Pm = VN.rearrange("p t n -> p (t n)").rearrange("p (b n) -> p b n", b=2)
        PT = U.rearrange("p j n -> p (j n)").rearrange("p (k n) -> p k n", k=4)
        ropet = gate_diag[:, 0, :]
        room[0] = 0
        alibi = carve(3840).rearrange("p (h n) -> p h n", h=10)
        FQ = carve(16 * 256).rearrange("p (b n) -> p b n", b=16)
        FV = carve(2048).rearrange("p (t n) -> p t n", t=2)
        SS = carve(4 * 384).rearrange("p (b n) -> p b n", b=4)
        S2 = carve(2 * 384).rearrange("p (b n) -> p b n", b=2)
        PT2 = carve(2 * 384).rearrange("p (b n) -> p b n", b=2)
        ZE = carve(6 * 384).rearrange("p (b n) -> p b n", b=6)
        ZP = carve(6 * 384).rearrange("p (b n) -> p b n", b=6)
        OB2 = carve(512).rearrange("p (b n) -> p b n", b=2)
        sgate = carve(512).rearrange("p (b n) -> p b n", b=2)
        hbuf = carve(512).rearrange("p (b n) -> p b n", b=2)
        OT = SG[:, :, 0:T]

        ident, ones = KB[:, C_ID:C_ID + P], KB[:, C_ONES:C_ONES + P]
        heads2, ntri, negones = (KB[:, c:c + P] for c in (C_H2, C_NTRI, C_NONE))
        dft_d = KB[:, C_DD:C_DD + 256]
        dft_n = KB[:, C_DN:C_DN + 1024].rearrange("p (s t n) -> p s t n", s=2, t=2)
        full, gap = KB[:, C_FULL:C_FULL + 384], KB[:, C_GAP:C_GAP + 384]
        rcos, rsin = KB[NOPE:QK, C_ROPE:C_ROPE + T], KB[NOPE:QK, C_ROPE + T:C_ROPE + 2 * T]

        B = [ctx.enter_context(nc.psum_tensor(f"bank{i}", [P, 512], F32)) for i in range(8)]

        slot_loaded = [M.sem(f"slot{i}_loaded") for i in range(RING)]
        s_gu, s_silu, s_h, s_dn = (M.sem(n) for n in ("gate_up_ready", "silu_ready", "hidden_ready", "down_used"))

        def colslot(w, c0, n):
            return w.rearrange("(k p) n -> p k n", p=P)[:, :, c0:c0 + n], n

        SLOTS = []
        base = {}

        def add(name, items):
            base[name] = len(SLOTS)
            SLOTS.extend(items)

        def rows2(w, s):
            return w.rearrange("(s r p) n -> s p r n", r=2, p=P)[s], 0

        for L in range(2):
            add(("ada", L), [colslot(I["w_ada"][L], 256 * s, 256) for s in range(ADA_SLOTS)])
            add(("win", L), [colslot(I["w_in"][L], c, n) for c, n in WIN_SLOTS])
            add(("wout", L), [rows2(I["w_out"][L], s) for s in range(4)])
        SITES = [("ffn", 0), ("mix", 0), ("ffn", 1), ("ffn", 2), ("mix", 1), ("ffn", 3)]
        for kind, n in SITES:
            if kind == "ffn":
                add(("ffn", n), [None] * FFN_SLOTS)
            else:
                add(("win2", n), [colslot(I["w_in_2"][n], 256 * s, 256) for s in range(12)])
                add(("wout2", n), [rows2(I["w_out_2"][n], s) for s in range(4)])

        LAST = {}
        for L in range(2):
            for s in range(ADA_SLOTS):
                LAST[base[("ada", L)] + s] = ("ada_psum", L, s)
            ends = [("q", 1), ("krs",), ("a", 1), ("g", 1), ("f", 1), ("u", 1), ("v", 3 if L == 0 else 1)] + [("gate", 2 * s + 1) for s in range(4)]
            for s, e in enumerate(ends):
                LAST[base[("win", L)] + s] = ("proj", L) + e
            for s in range(4):
                LAST[base[("wout", L)] + s] = ("wout_used", L, s) if s < 3 else ("y_ready", "b1", L, 3 if L == 0 else 1, 1)
        for i, (kind, n) in enumerate(SITES):
            if kind == "ffn":
                for p in range(FFN_PAIRS):
                    m = base[("ffn", n)] + 3 * p
                    LAST[m] = LAST[m + 1] = ("gate_up_ready", n, p)
                    LAST[m + 2] = ("down_used", n, p) if p < FFN_PAIRS - 1 else ("y_ready", "site", i, 1, 1)
                    table[("gate_up_ready", n, p)] = n * FFN_CHUNKS + 2 * p + 2
                    table[("down_used", n, p)] = n * (FFN_CHUNKS - 1) + 2 * p + 2
            else:
                for s in range(12):
                    LAST[base[("win2", n)] + s] = ("proj2", n) + BLOCKS2[2 * s + 1]
                for s in range(4):
                    LAST[base[("wout2", n)] + s] = ("wout2_used", n, s) if s < 3 else ("y_ready", "site", i, 1, 1)

        def slot(n):
            return ring[:, n % RING, :]

        def filled(n):
            return slot_loaded[n % RING], 16 * (n // RING + 1)

        def cols(n, w=256):
            return slot(n)[:, 0:8 * w].rearrange("p (k n) -> p k n", k=8)

        def rows(n):
            return slot(n).rearrange("p (r n) -> p r n", r=2)

        block = ctx.enter_context(nc.Block())

        @block.sync
        def _(sp):
            def fill(n, src, w):
                if n >= RING:
                    sp.wait_ge(*at(*LAST[n - RING]))
                dst = cols(n, w) if w else rows(n)
                sp.dma_start(dst, src).then_inc(slot_loaded[n % RING], 16)

            sp.dma_start(vec[:, 0, :], I["k_vec1"][0]).then_inc(M.sem("vec_loaded"), 16)
            sp.dma_start(vec[:, 1, :], I["k_vec1"][1]).then_inc(M.sem("vec_loaded"), 16)
            sp.dma_start(vec[:, 2, :], I["k_vec2"]).then_inc(M.sem("vec_loaded"), 16)
            sp.dma_start(KB[:, 0:C_DD], I["k_base"][:, 0:C_DD]).then_inc(M.sem("vec_loaded"), 16)
            n_first = base[("ffn", 0)]
            for n in range(n_first):
                fill(n, *SLOTS[n])

            def ffn(idx):
                g = I["w_ffn_gate_2"][idx // 2, idx % 2].rearrange("(k p) (i n) -> i p k n", p=P, n=256)
                u = I["w_ffn_up_2"][idx // 2, idx % 2].rearrange("(k p) (i n) -> i p k n", p=P, n=256)
                d = I["w_ffn_down_2"][idx // 2, idx % 2].rearrange("(i r p) n -> i p r n", r=2, p=P)
                b0 = base[("ffn", idx)]
                f0, d0 = idx * FFN_CHUNKS, idx * (FFN_CHUNKS - 1)
                for p in range(3):
                    for q, src in enumerate((g, u, d)):
                        fill(b0 + 3 * p + q, src[p], 0 if q == 2 else 256)
                with sp.Fori(0, (FFN_PAIRS - 3) // 2) as j:
                    for c in range(2):
                        for q, src in enumerate((g, u, d)):
                            p = 3 + c
                            n = b0 + 3 * p + q
                            sp.wait_ge(s_gu if q < 2 else s_dn, j * 4 + ((f0 if q < 2 else d0) + 2 * p - 2))
                            s = src[bass.ds(j * 2 + p, 1)]
                            dst = cols(n) if q < 2 else rows(n)
                            sp.dma_start(dst, s.rearrange("i p a n -> p (i a) n")).then_inc(slot_loaded[n % RING], 16)

            for kind, n in SITES:
                if kind == "ffn":
                    ffn(n)
                else:
                    for s in range(base[("win2", n)], base[("wout2", n)] + 4):
                        fill(s, *SLOTS[s])
            for t in range(2):
                sp.wait_ge(*at("x_updated", "site", 5, t, 1))
                sp.dma_start(out[0].rearrange("(t p) d -> t p d", p=P)[t], X[:, t, :]).then_inc(M.sem("stored"), 16)
            sp.wait_ge(M.sem("stored"), 32)

        SW = 7 * 16

        @block.gpsimd
        def _(pool):
            def load(dst, src, stage):
                pool.dma_start(dst, src).then_inc(M.sem(stage), 16)

            pool.memset(eps[:, 0:1], RMS_EPS)
            pool.memset(eps[:, 1:2], LN_EPS)
            pool.memset(eps[:, 2:3], RMS_EPS * QK)
            pool.memset(eps[:, 3:4], 0.0)
            pool.memset(CG, 0.0).then_inc(*done("set_up"))
            load(KB[:, C_DD:], I["k_base"][:, C_DD:], "base_loaded")
            load(lam_in[:, :, :], I["diff_lambda_2"].rearrange("l a b -> (l a b)").rearrange("(l n) -> l n", l=2).partition_broadcast(P), "base_loaded")
            load(bsrow, I["b_s"].rearrange("l g n -> (l g n)").rearrange("(a l n) -> a l n", a=1, l=2), "base_loaded")

            def small_weights(L):
                load(w_uq, I["w_uq"][L].rearrange("(j p) n -> p j n", p=P), "small_loaded")
                load(w_ukv, I["w_ukv"][L], "small_loaded")
                load(w_pw, I["w_pw"][L].rearrange("(j p) n -> p j n", p=P), "small_loaded")
                load(w_fo, I["w_fourier"][L].rearrange("(j p) n -> p j n", p=P), "small_loaded")
                load(w_s, I["w_s"][L].rearrange("g i j -> i g j"), "small_loaded")
                load(sgu_row[:, 0, :], I["sgu_ln_g"][L].partition_broadcast(P), "small_loaded")
                load(sgu_row[:, 1, :], I["sgu_ln_b"][L].partition_broadcast(P), "small_loaded")

            def layer(L):
                nq = TT if L == 0 else T
                if L:
                    pool.wait_ge(*at("conv_out", 0, 1))
                small_weights(L)
                pool.wait_ge(M.sem("small_loaded"), SW * (L + 1))
                for j in range(2):
                    for half in range(2):
                        src = w_uq[:, j, :].rearrange("p (h n) -> p h n", h=4)[:, :, NOPE:QK].rearrange("p h (a x f) -> p h a x f", a=2, x=2)[:, :, :, 1 - half, :]
                        dst = w_uqs[:, j, :].rearrange("p (h a x f) -> p h a x f", h=4, a=2, x=2)[:, :, :, half, :]
                        last = pool.tensor_copy(dst, src)
                last.then_inc(*done("uq_swapped", L))
                n = base[("win", L)] + 1
                pool.wait_ge(*filled(n))
                for half in range(2):
                    src = cols(n, 160)[:, :, P:P + ROPE].rearrange("p k (a x f) -> p k a x f", a=2, x=2)[:, :, :, 1 - half, :]
                    dst = w_krs.rearrange("p k (a x f) -> p k a x f", a=2, x=2)[:, :, :, half, :]
                    last = pool.tensor_copy(dst, src)
                last.then_inc(*done("kr_swapped", L))
                for j in range(2):
                    pool.wait_ge(*at("a_ready", L, j))
                    pool.wait_ge(*at("conv_gate_ready", L, j))
                    for s in range(nq // T):
                        last = pool.tensor_tensor(CG[:, j, s, PAD:PAD + T], CG[:, j, s, PAD:PAD + T], csg[:, j, s * T:(s + 1) * T], ALU.mult)
                    last.then_inc(*done("glu_ready", L, j))
                for t in range(nq // P):
                    pool.wait_ge(*at("v_normalised", L, t))
                    pool.tensor_tensor(VN[:, t, :], VN[:, t, :], sgu_row[:, 0, :], ALU.mult).then_inc(*done("v_gained", L, t))
                    pool.wait_ge(*at("v_gained", L, t))
                    pool.tensor_tensor(VN[:, t, :], VN[:, t, :], sgu_row[:, 1, :], ALU.add).then_inc(*done("v_ready", L, t))
                for m in range(2):
                    pool.wait_ge(*at("u_ready", L, m))
                    pool.wait_ge(*at("sg_ready", L, 6 + m))
                    pool.tensor_tensor(U[:, m, 0:nq], U[:, m, 0:nq], SG[:, 6 + m, 0:nq], ALU.mult).then_inc(*done("u_gated", L, m))
                pool.wait_ge(*at("u_gated", L, 1))
                pool.wait_ge(*at("kr_ready", L))
                pool.wait_ge(*at("fourier_tok", L, 1))
                for h in range(HEADS):
                    last = pool.tensor_copy(K[NOPE:QK, h, :], krot[NOPE:QK, :])
                last.then_inc(*done("k_rope_ready", L))
                pool.wait_ge(*at("k_rope_ready", L))
                for t in range(nq // P):
                    for n in range(2):
                        pool.wait_ge(*at("out_scaled", "b1", L, t, n))
                        pool.tensor_tensor(X[:, t, n * 512:(n + 1) * 512], X[:, t, n * 512:(n + 1) * 512], ytmp[:, n, :], ALU.add).then_inc(*done("x_updated", "b1", L, t, n))

            layer(0)
            layer(1)
            pool.wait_ge(*at("final_scaled", 1))
            load(gain_row[:, :], I["norm_gains_2"][0, 1].partition_broadcast(P), "gain_loaded")
            pool.wait_ge(*at("conv_out", 1, 1))
            load(alibi.rearrange("p h n -> p (h n)"), I["k_alibi"], "alibi_loaded")
            for i, (kind, n) in enumerate(SITES):
                if kind == "mix":
                    pool.wait_ge(M.sem("base_loaded"), 48)
                    for h in range(N_SB):
                        pool.wait_ge(*at("softplus_ready", n, h))
                        pool.tensor_tensor(ZP[:, h, :], ZP[:, h, :], full, ALU.mult).then_inc(*done("softplus_masked", n, h))
                for t in range(2):
                    for hf in range(2):
                        pool.wait_ge(*at("out_scaled", "site", i, t, hf))
                        pool.tensor_tensor(X[:, t, hf * 512:(hf + 1) * 512], X[:, t, hf * 512:(hf + 1) * 512], ytmp[:, hf, :], ALU.add).then_inc(*done("x_updated", "site", i, t, hf))
                if i < 5:
                    nxt = i + 1
                    load(gain_row[:, :], I["norm_gains_2"][nxt // 3, 2 * (nxt % 3) + 1].partition_broadcast(P), "gain_loaded")

        @block.scalar
        def _(act):
            A = act.activation
            for t in range(2):
                act.dma_start(X[:, t, :], I["x"][0].rearrange("(t p) d -> t p d", p=P)[t]).then_inc(M.sem("x_loaded"), 16)
            for t in range(2):
                act.dma_start(X[:, 2 + t, :], I["ctx"][0].rearrange("(t p) d -> t p d", p=P)[t]).then_inc(M.sem("x_loaded"), 16)
            act.dma_start(gain_row[:, :], I["final_g"].partition_broadcast(P)).then_inc(M.sem("final_loaded"), 16)
            act.wait_ge(*at("vec_T", 0))
            A(CS[:, :], vT[:, 0, R_C:R_C + 16], ACT.Silu).then_inc(*done("silu_c"))
            act.wait_ge(M.sem("x_loaded"), 64)
            act.wait_ge(*at("set_up"))

            def norm(site, tiles):
                for t in tiles:
                    if site == ("b1", 1):
                        for hf in range(2):
                            act.wait_ge(*at("x_updated", "b1", 0, t, hf))
                    A(XN[:, t, :], X[:, t, :], ACT.Square, accum_out=stat[:, t:t + 1]).then_inc(*done("sum_squares", *site, t))
                act.wait_ge(*at("sum_squares", *site, tiles[-1]))
                act.wait_ge(*at("set_up"))
                A(stat[:, 8:8 + len(tiles)], stat[:, 0:len(tiles)], ACT.Sqrt, bias=eps[:, 0:1], scale=1.0 / D).then_inc(*done("rms_ready", *site))

            def layer(L):
                nq = TT if L == 0 else T
                norm(("b1", L), range(4))
                for c in range(0, KD, 2):
                    act.wait_ge(*at("x_T", "b1", L, c))
                    act.wait_ge(*at("ada_ready", L))
                    A(hT[:, c, 0:T], B[c % 4][:, 0:T], ACT.Identity, scale=adag[:, c, 0:1], bias=ada[:, c, 0:1])
                    A(hT[:, c, T:TT], B[c % 4][:, T:TT], ACT.Identity, scale=adag[:, c, 1:2], bias=ada[:, c, 1:2]).then_inc(*done("hT_ready_act", "b1", L, c))
                for j in range(2):
                    act.wait_ge(*at("proj", L, "q", j))
                    A(qp[:, j, 0:nq], B[PB[L]["q", j]][:, 0:nq], ACT.Copy)
                    A(sq[:, j, 0:nq], B[PB[L]["q", j]][:, 0:nq], ACT.Square).then_inc(*done("q_part_ready", L, j))
                act.wait_ge(*at("proj", L, "kv"))
                A(kvp, B[PB[L]["kv"]][:, :], ACT.Copy)
                A(sq[:, 2, :], B[PB[L]["kv"]][:, :], ACT.Square).then_inc(*done("kv_part_ready", L))
                for j in range(2):
                    act.wait_ge(*at("proj", L, "a", j))
                    if L:
                        act.wait_ge(*at("conv_tap", L - 1, j, CONV_K - 1))
                    else:
                        act.wait_ge(*at("set_up"))
                    src = B[PB[L]["a", j]][:, 0:nq].rearrange("p (s n) -> p s n", n=T)
                    A(CG[:, j, 0:nq // T, PAD:PAD + T], src, ACT.Copy).then_inc(*done("a_ready", L, j))
                act.wait_ge(*at("q_square_sum", L))
                A(rq[:, 0, 0:nq], B[6][:, 0:nq], ACT.Sqrt, bias=eps[:, 2:3], scale=float(QK) / 256).then_inc(*done("q_root", L))
                act.wait_ge(*at("kv_square_sum", L))
                A(rq[:, 1, :], B[7][:, :], ACT.Sqrt, bias=eps[:, 0:1], scale=1.0 / 128).then_inc(*done("kv_root", L))
                for j in range(2):
                    act.wait_ge(*at("proj", L, "g", j))
                    A(csg[:, j, 0:nq], B[PB[L]["g", j]][:, 0:nq], ACT.Sigmoid).then_inc(*done("conv_gate_ready", L, j))
                for j in range(2):
                    act.wait_ge(*at("proj", L, "f", j))
                    A(fT[:, j, 0:nq], B[PB[L]["f", j]][:, 0:nq], ACT.Copy).then_inc(*done("f_ready", L, j))
                for j in range(2):
                    act.wait_ge(*at("proj", L, "u", j))
                    A(U[:, j, 0:nq], B[PB[L]["u", j]][:, 0:nq], ACT.Copy).then_inc(*done("u_ready", L, j))
                act.wait_ge(*at("v_aggr", L, nq // P - 1))
                A(stat[:, 40:40 + nq // P], stat[:, 33:33 + 2 * (nq // P):2], ACT.Sqrt, bias=eps[:, 1:2]).then_inc(*done("v_root", L))
                for j in range(8):
                    act.wait_ge(*at("proj", L, "gate", j))
                    A(SG[:, j, 0:nq], B[PB[L]["gate", j]][:, 0:nq], ACT.Silu).then_inc(*done("sg_ready", L, j))
                for v in range(nq // T):
                    for hf in range(2):
                        act.wait_ge(*at("gate_rows", L, v, hf))
                        A(GB[:, v, hf * 512:(hf + 1) * 512], B[(2 * v + hf) % 4][:, :], ACT.Copy).then_inc(*done("gate_row_ready", L, v, hf))
                for h in range(HEADS):
                    act.wait_ge(*at("q_heads", L, h))
                    act.wait_ge(*at("glu_ready", L, 1))
                    A(Q[0:NOPE, h, 0:nq], B[h % 2][0:NOPE, 0:nq], ACT.Copy)
                    if L == 0:
                        A(Q[NOPE:QK, h, T:TT], B[h % 2][NOPE:QK, T:TT], ACT.Copy)
                    A(csg[NOPE:QK, h // 2, (h % 2) * T:(h % 2 + 1) * T], B[h % 2][NOPE:QK, 0:T], ACT.Copy).then_inc(*done("q_copied", L, h))
                for h in range(HEADS):
                    act.wait_ge(*at("k_heads", L, h))
                    act.wait_ge(*at("fourier_tok", L, 1))
                    A(K[0:NOPE, h, :], B[h % 2][0:NOPE, :], ACT.Copy).then_inc(*done("k_copied", L, h))
                for seg in range(nq // T):
                    keys = TT if seg == 0 else T
                    for h in range(HEADS):
                        for qt in range(2):
                            act.wait_ge(*at("neg_max", L, seg, h, qt))
                            A(Pm[:, qt, 0:keys], B[qt][:, 0:keys], ACT.Exp, bias=stat[:, 16 + qt:17 + qt], accum_out=stat[:, 18 + qt:19 + qt]).then_inc(*done("exp_ready", L, seg, h, qt))
                        for qt in range(2):
                            act.wait_ge(*at("p_T", L, seg, h, qt))
                            A(PT[:, 0:keys // P, qt * P:(qt + 1) * P], B[2 + qt][:, 0:keys].rearrange("p (k n) -> p k n", n=P), ACT.Copy).then_inc(*done("pT_ready", L, seg, h, qt))
                for j in range(2):
                    act.wait_ge(*at("conv_centred", L, j))
                    A(sq[:, j, 0:nq], cacc[:, j, 0:nq], ACT.Square).then_inc(*done("conv_square", L, j))
                act.wait_ge(*at("conv_var", L))
                A(rq[:, 0, 0:nq], B[1][:, 0:nq], ACT.Sqrt, bias=eps[:, 1:2], scale=1.0 / 256).then_inc(*done("conv_root", L))
                for j in range(2):
                    act.wait_ge(*at("conv_normalised", L, j))
                    A(csg[:, j, 0:nq], cacc[:, j, 0:nq], ACT.Silu, scale=vT[:, L, R_CLG + j:R_CLG + j + 1], bias=vT[:, L, R_CLB + j:R_CLB + j + 1]).then_inc(*done("conv_act", L, j))

            layer(0)
            layer(1)
            for t in range(2):
                for hf in range(2):
                    act.wait_ge(*at("x_updated", "b1", 1, t, hf))
                A(XN[:, t, :], X[:, t, :], ACT.Square, accum_out=stat[:, t:t + 1]).then_inc(*done("final_squares", t))
            act.wait_ge(*at("final_squares", 1))
            A(stat[:, 8:10], stat[:, 0:2], ACT.Sqrt, bias=eps[:, 0:1], scale=1.0 / D).then_inc(*done("final_root"))

            def site_norm(i):
                for t in range(2):
                    if i == 0:
                        act.wait_ge(*at("final_scaled", t))
                    else:
                        for hf in range(2):
                            act.wait_ge(*at("x_updated", "site", i - 1, t, hf))
                    A(XN[:, t, :], X[:, t, :], ACT.Square, accum_out=stat[:, t:t + 1]).then_inc(*done("sum_squares", "site", i, t))
                act.wait_ge(*at("sum_squares", "site", i, 1))
                A(stat[:, 8:10], stat[:, 0:2], ACT.Sqrt, bias=eps[:, 0:1], scale=1.0 / D).then_inc(*done("rms_ready", "site", i))
                for b in (0, 2):
                    act.wait_ge(*at("x_T", "site", i, b))
                    for q in range(2):
                        c = 2 * b + q
                        r = 8 * i + c
                        last = A(hT[:, c, 0:T], B[b][:, q * T:(q + 1) * T], ACT.Identity, scale=vT[:, 2, r:r + 1])
                    last.then_inc(*done("hT_ready_act", "site", i, b))

            def site_tail(i):
                for t in range(2):
                    for hf in range(2):
                        act.wait_ge(*at("y_ready", "site", i, t, hf))
                        A(XN[:, 2, 0:512] if hf else XN[:, 3, 0:512], B[4 + 2 * t + hf][:, :], ACT.Square, accum_out=stat[:, 10 + 2 * t + hf:11 + 2 * t + hf]).then_inc(*done("y_squares", i, t, hf))
                    act.wait_ge(*at("y_sum", i, t))
                    A(stat[:, 28 + t:29 + t], stat[:, 26 + t:27 + t], ACT.Sqrt, bias=eps[:, 0:1], scale=1.0 / D).then_inc(*done("y_root", i, t))

            def ffn(i, n):
                f0 = n * FFN_CHUNKS

                def silu(par, ready, free):
                    act.wait_ge(s_gu, ready)
                    if free is not None:
                        act.wait_ge(s_h, free)
                    A(sgate[:, par, :], B[par][:, 0:T], ACT.Silu).then_inc(s_silu, 1)

                silu(0, f0 + 1, f0 if n else None)
                silu(1, f0 + 2, f0 if n else None)
                with act.Fori(0, (FFN_PAIRS - 1) // 2) as j:
                    for c in range(4):
                        silu(c % 2, j * 4 + (f0 + 3 + c), j * 4 + (f0 + 1 + c))

            def mix(i, n):
                for b in range(16):
                    if b % 2 == 0:
                        act.wait_ge(*at("proj2", n, "qk", b))
                        sc = QKSC[b]
                        A(FQ[:, b, :], B[PB2["qk", b]][:, 0:T], ACT.Copy, scale=sc).then_inc(*done("qk_ready_act", n, b))
                for u in range(N_DIL + 2 * N_DIFF):
                    act.wait_ge(*at("neg_max2", n, u))
                    for qt, (a, w) in enumerate(((0, P), (P, T))):
                        last = A(SS[:, u % 4, a:a + w], S2[:, u % 2, a:a + w], ACT.Exp, scale=-1.0, bias=stat[:, 16 + 2 * (u % 2) + qt:17 + 2 * (u % 2) + qt], accum_out=stat[:, 20 + 2 * (u % 2) + qt:21 + 2 * (u % 2) + qt])
                    last.then_inc(*done("exp2_ready", n, u))
                    h = UNIT_HEAD[u]
                    if h is not None:
                        act.wait_ge(*at("p2_T", n, h))
                        A(PT2[:, h % 2, :], B[2 + h % 2][:, 0:384], ACT.Copy).then_inc(*done("pT2_ready", n, h))
                for b in range(2):
                    act.wait_ge(*at("ob_ready", n, b))
                    A(sgate[:, b, :], OB2[:, b, :], ACT.Square).then_inc(*done("ob_square", n, b))
                    act.wait_ge(*at("ob_sum", n, b))
                    A(sgate[:, b, :], B[4 + b][:, T:TT], ACT.Sqrt, bias=eps[:, 0:1]).then_inc(*done("ob_root", n, b))
                for h in range(N_SB):
                    act.wait_ge(*at("z_ready", n, h))
                    A(ZE[:, h, :], B[h][:, 0:384], ACT.Abs).then_inc(*done("z_abs", n, h))
                for h in range(N_SB):
                    act.wait_ge(*at("z_abs", n, h))
                    A(ZE[:, h, :], ZE[:, h, :], ACT.Exp, scale=-1.0).then_inc(*done("z_exp", n, h))
                for h in range(N_SB):
                    act.wait_ge(*at("z_exp", n, h))
                    A(ZE[:, h, :], ZE[:, h, :], ACT.Ln, bias=1.0).then_inc(*done("z_ln", n, h))
                for h in range(N_SB):
                    act.wait_ge(*at("log_weight", n, h))
                    A(ZP[:, h, :], ZE[:, h, :], ACT.Exp).then_inc(*done("weight_ready", n, h))

            for m in range(2):
                act.wait_ge(*at("lambda_sums", m))
                A(lamv[:, m, 2:4], lamv[:, m, 0:2], ACT.Exp).then_inc(*done("lambda_exp", m))
            for i, (kind, n) in enumerate(SITES):
                site_norm(i)
                (ffn if kind == "ffn" else mix)(i, n)
                site_tail(i)

        @block.vector
        def _(dve):
            TS, STT, TTn, CP = dve.tensor_scalar, dve.scalar_tensor_tensor, dve.tensor_tensor, dve.tensor_copy
            dve.wait_ge(*at("vec_transposed"))
            CP(vT[:, :, :], B[0][:, 0:384].rearrange("p (b n) -> p b n", b=3)).then_inc(*done("vec_T", 0))

            def scale_rows(site, tiles):
                dve.wait_ge(*at("rms_ready", *site))
                dve.reciprocal(stat[:, 12:12 + len(tiles)], stat[:, 8:8 + len(tiles)]).then_inc(*done("rms_inverse", *site))
                dve.wait_ge(*at("rms_inverse", *site))
                for t in tiles:
                    TS(XN[:, t, :], X[:, t, :], stat[:, 12 + t:13 + t], None, ALU.mult).then_inc(*done("x_scaled", *site, t))

            def layer(L):
                nq = TT if L == 0 else T
                nt = nq // P
                scale_rows(("b1", L), range(4))
                dve.wait_ge(*at("ada_psum", L, ADA_SLOTS - 1))
                TTn(ada[:, :, :], B[7][:, 0:48].rearrange("p (b v) -> p b v", v=2), vT[:, L, 0:24].unsqueeze(2).to_broadcast([P, 24, 2]), ALU.add).then_inc(*done("ada_biased", L))
                dve.wait_ge(*at("ada_biased", L))
                STT(adag[:, :, :], ada[:, 8:16, :], 1.0, vT[:, L, R_NORM:R_NORM + 8].unsqueeze(2).to_broadcast([P, 8, 2]), ALU.add, ALU.mult).then_inc(*done("ada_ready", L))
                dve.wait_ge(*at("ada_ready", L))
                for c in range(1, KD, 2):
                    dve.wait_ge(*at("x_T", "b1", L, c))
                    TS(hT[:, c, 0:T], B[c % 4][:, 0:T], adag[:, c, 0:1], ada[:, c, 0:1], ALU.mult, ALU.add)
                    TS(hT[:, c, T:TT], B[c % 4][:, T:TT], adag[:, c, 1:2], ada[:, c, 1:2], ALU.mult, ALU.add).then_inc(*done("hT_ready_dve", "b1", L, c))
                dve.wait_ge(*at("ws_transposed", L))
                CP(wsT, B[5][:, :].rearrange("p (g n) -> p g n", g=4)).then_inc(*done("wsT_ready", L))
                dve.wait_ge(*at("proj", L, "kr"))
                dve.wait_ge(M.sem("base_loaded"), 48)
                TTn(krot[NOPE:QK, 0:T], B[PB[L]["kr"]][NOPE:QK, 0:T], rcos, ALU.mult).then_inc(*done("kr_cos", L))
                CP(krot[NOPE:QK, T:TT], B[PB[L]["kr"]][NOPE:QK, T:TT]).then_inc(*done("kr_copied", L))
                dve.wait_ge(*at("proj", L, "krs"))
                TTn(ropet[NOPE:QK, 0:T], B[PB[L]["krs"]][NOPE:QK, 0:T], rsin, ALU.mult).then_inc(*done("kr_sin", L))
                dve.wait_ge(*at("kr_cos", L))
                dve.wait_ge(*at("kr_sin", L))
                TTn(krot[NOPE:QK, 0:T], krot[NOPE:QK, 0:T], ropet[NOPE:QK, 0:T], ALU.add).then_inc(*done("kr_ready", L))
                dve.wait_ge(*at("q_root", L))
                dve.reciprocal(rq[:, 0, 0:nq], rq[:, 0, 0:nq]).then_inc(*done("q_inverse", L))
                dve.wait_ge(*at("kv_root", L))
                dve.reciprocal(rq[:, 1, :], rq[:, 1, :]).then_inc(*done("kv_inverse", L))
                dve.wait_ge(*at("q_inverse", L))
                for j in range(2):
                    dve.wait_ge(*at("q_part_ready", L, j))
                    STT(qp[:, j, 0:nq], qp[:, j, 0:nq], vT[:, L, R_QN + j:R_QN + j + 1], rq[:, 0, 0:nq], ALU.mult, ALU.mult).then_inc(*done("q_latent", L, j))
                dve.wait_ge(*at("kv_inverse", L))
                STT(kvp, kvp, vT[:, L, R_KVN:R_KVN + 1], rq[:, 1, :], ALU.mult, ALU.mult).then_inc(*done("kv_latent", L))
                for t in range(nt):
                    dve.wait_ge(*at("fourier_feat", L, t))
                    CP(FA[:, t, :, :], B[6 + t % 2][:, :].rearrange("p (j n) -> p j n", j=2)).then_inc(*done("fa_ready", L, t))
                for t in range(nt):
                    dve.wait_ge(*at("proj", L, "v", t))
                    dve.bn_stats(stat[:, 44:50], B[PB[L]["v", t]][:, 0:256]).then_inc(*done("v_bn", L, t))
                    CP(VN[:, t, :], B[PB[L]["v", t]][:, 0:256]).then_inc(*done("v_copied", L, t))
                    dve.wait_ge(*at("v_bn", L, t))
                    dve.bn_aggr(stat[:, 32 + 2 * t:34 + 2 * t], stat[:, 44:50]).then_inc(*done("v_aggr", L, t))
                    dve.wait_ge(*at("v_aggr", L, t))
                for m in range(2):
                    dve.wait_ge(*at("fourier_tok", L, m))
                    CP(cacc[:, m, 0:nq], B[6 + m][:, 0:nq]).then_inc(*done("f_mixed", L, m))
                dve.wait_ge(*at("v_root", L))
                dve.reciprocal(stat[:, 40:40 + nt], stat[:, 40:40 + nt]).then_inc(*done("v_inverse", L))
                dve.wait_ge(*at("v_inverse", L))
                for t in range(nt):
                    dve.wait_ge(*at("v_copied", L, t))
                    TS(VN[:, t, :], VN[:, t, :], stat[:, 32 + 2 * t:33 + 2 * t], stat[:, 40 + t:41 + t], ALU.subtract, ALU.mult).then_inc(*done("v_normalised", L, t))
                for m in range(2):
                    dve.wait_ge(*at("fourier_out", L, m))
                    dve.wait_ge(*at("sg_ready", L, 4 + m))
                    STT(SG[:, 4 + m, 0:nq], B[4 + m][:, 0:nq], vT[:, L, R_BF + m:R_BF + m + 1], SG[:, 4 + m, 0:nq], ALU.add, ALU.mult).then_inc(*done("four_branch", L, m))
                for m in range(2):
                    dve.wait_ge(*at("sgu_mixed", L, m))
                    dve.wait_ge(*at("u_gated", L, m))
                    TTn(SG[:, 6 + m, 0:nq], B[6 + m][:, 0:nq], U[:, m, 0:nq], ALU.mult).then_inc(*done("sgu_branch", L, m))
                for v in range(nq // T):
                    for hf in range(2):
                        if v:
                            dve.wait_ge(*at("gate_rows", L, v - 1, hf))
                        elif L:
                            dve.wait_ge(*at("gate_rows", 0, 1, hf))
                        for c in range(4):
                            last = TS(gate_diag[:, hf, c * P:(c + 1) * P], ident, ada[:, 16 + 4 * hf + c, v:v + 1], None, ALU.mult)
                        last.then_inc(*done("gate_diag_ready", L, v, hf))
                for h in range(HEADS):
                    dve.wait_ge(*at("q_copied", L, h))
                    qc = csg[NOPE:QK, h // 2, (h % 2) * T:(h % 2 + 1) * T]
                    TTn(Q[NOPE:QK, h, 0:T], qc, rcos, ALU.mult).then_inc(*done("q_cos", L, h))
                    dve.wait_ge(*at("q_swapped", L, h))
                    TTn(ropet[NOPE:QK, (h % 2) * T:(h % 2 + 1) * T], B[2 + h % 2][NOPE:QK, 0:T], rsin, ALU.mult).then_inc(*done("q_sin", L, h))
                    dve.wait_ge(*at("q_sin", L, h))
                    dve.wait_ge(*at("q_cos", L, h))
                    TTn(Q[NOPE:QK, h, 0:T], Q[NOPE:QK, h, 0:T], ropet[NOPE:QK, (h % 2) * T:(h % 2 + 1) * T], ALU.add).then_inc(*done("q_ready", L, h))
                for t in range(4):
                    dve.wait_ge(*at("v_heads", L, t))
                    CP(V[:, t, :], B[4 + t][:, 0:256]).then_inc(*done("v_heads_ready", L, t))
                conv = conv_steps(L)
                for seg in range(nq // T):
                    keys = TT if seg == 0 else T
                    for h in range(HEADS):
                        for qt in range(2):
                            dve.wait_ge(*at("scores", L, seg, h, qt))
                            dve.reduce_max(stat[:, 16 + qt:17 + qt], B[qt][:, 0:keys], AXX, negate=True).then_inc(*done("neg_max", L, seg, h, qt))
                        for _ in range(8):
                            next(conv, None)
                        for qt in range(2):
                            dve.wait_ge(*at("exp_ready", L, seg, h, qt))
                            dve.reciprocal(stat[:, 20 + qt:21 + qt], stat[:, 18 + qt:19 + qt]).then_inc(*done("p_inverse", L, seg, h, qt))
                            dve.wait_ge(*at("p_inverse", L, seg, h, qt))
                            TS(Pm[:, qt, 0:keys], Pm[:, qt, 0:keys], stat[:, 20 + qt:21 + qt], None, ALU.mult).then_inc(*done("p_ready", L, seg, h, qt))
                        if h % 2:
                            dve.wait_ge(*at("attn", L, seg, h))
                            sl = SG[:, h // 2, seg * T:(seg + 1) * T]
                            TTn(sl, B[4 + h // 2][:, 0:T], sl, ALU.mult).then_inc(*done("attn_ready", L, h, seg))
                for _ in conv:
                    pass
                dve.wait_ge(*at("conv_mean", L))
                for j in range(2):
                    dve.wait_ge(*at("conv_tap", L, j, CONV_K - 1))
                    STT(cacc[:, j, 0:nq], B[0][:, 0:nq], -1.0 / 256, cacc[:, j, 0:nq], ALU.mult, ALU.add).then_inc(*done("conv_centred", L, j))
                dve.wait_ge(*at("conv_root", L))
                dve.reciprocal(rq[:, 0, 0:nq], rq[:, 0, 0:nq]).then_inc(*done("conv_inverse", L))
                dve.wait_ge(*at("conv_inverse", L))
                for j in range(2):
                    dve.wait_ge(*at("conv_square", L, j))
                    dve.wait_ge(*at("conv_centred", L, j))
                    TTn(cacc[:, j, 0:nq], cacc[:, j, 0:nq], rq[:, 0, 0:nq], ALU.mult).then_inc(*done("conv_normalised", L, j))
                for m in range(2):
                    dve.wait_ge(*at("conv_out", L, m))
                    STT(SG[:, 2 + m, 0:nq], B[2 + m][:, 0:nq], vT[:, L, R_BPW + m:R_BPW + m + 1], SG[:, 2 + m, 0:nq], ALU.add, ALU.mult).then_inc(*done("conv_branch", L, m))
                for t in range(nt):
                    for hf in range(2):
                        dve.wait_ge(*at("y_ready", "b1", L, t, hf))
                        dve.wait_ge(*at("gate_row_ready", L, t // 2, hf))
                        if t:
                            dve.wait_ge(*at("x_updated", "b1", L, t - 1, hf))
                        elif L:
                            dve.wait_ge(*at("x_updated", "b1", 0, 3, hf))
                        TTn(ytmp[:, hf, :], B[YB[L][t, hf]][:, :], GB[:, t // 2, hf * 512:(hf + 1) * 512], ALU.mult).then_inc(*done("out_scaled", "b1", L, t, hf))

            def conv_steps(L):
                nseg = 2 if L == 0 else 1
                for k in range(CONV_K):
                    for j in range(2):
                        accv = cacc[:, j, 0:nseg * T].rearrange("p (s n) -> p s n", n=T)
                        src = CG[:, j, 0:nseg, k:k + T]
                        w = vT[:, L, R_CW + 2 * k + j:R_CW + 2 * k + j + 1]
                        if k == 0:
                            dve.wait_ge(*at("glu_ready", L, j))
                            dve.wait_ge(*at("fourier_out", L, 1))
                            TS(accv, src, w, vT[:, L, R_CB + j:R_CB + j + 1], ALU.mult, ALU.add).then_inc(*done("conv_tap", L, j, k))
                        else:
                            dve.wait_ge(*at("conv_tap", L, j, k - 1))
                            STT(accv, src, w, accv, ALU.mult, ALU.add).then_inc(*done("conv_tap", L, j, k))
                    yield

            layer(0)
            layer(1)
            dve.wait_ge(*at("final_root"))
            dve.reciprocal(stat[:, 12:14], stat[:, 8:10]).then_inc(*done("final_inverse"))
            dve.wait_ge(*at("final_inverse"))
            dve.wait_ge(M.sem("final_loaded"), 16)
            for t in range(2):
                STT(X[:, t, :], X[:, t, :], stat[:, 12 + t:13 + t], gain_row[:, :], ALU.mult, ALU.mult).then_inc(*done("final_scaled", t))
            dve.wait_ge(M.sem("base_loaded"), 48)
            for m in range(2):
                for q in range(2):
                    last = dve.tensor_tensor_reduce(out=S2[:, m, q * 32:q * 32 + 32], in0=lam_in[:, m, q * 64:q * 64 + 32], in1=lam_in[:, m, q * 64 + 32:q * 64 + 64], scale=1.0, scalar=0.0, op0=ALU.mult, op1=ALU.add, accum_out=lamv[:, m, q:q + 1])
                last.then_inc(*done("lambda_sums", m))
            for m in range(2):
                init = LAM_INIT[m]
                dve.wait_ge(*at("lambda_exp", m))
                STT(lamv[:, m, 4:5], lamv[:, m, 3:4], init, lamv[:, m, 2:3], ALU.subtract, ALU.subtract).then_inc(*done("lambda_ready", m))
                TS(lamv[:, m, 5:6], vT[:, 2, R_SUB + m:R_SUB + m + 1], 1.0 - init, None, ALU.mult).then_inc(*done("sub_gain", m))

            def site_norm(i):
                if i == 0:
                    dve.wait_ge(*at("final_scaled", 1))
                scale_rows(("site", i), range(2))
                for b in (1, 3):
                    dve.wait_ge(*at("x_T", "site", i, b))
                    for q in range(2):
                        c = 2 * b + q
                        r = 8 * i + c
                        last = TS(hT[:, c, 0:T], B[b][:, q * T:(q + 1) * T], vT[:, 2, r:r + 1], None, ALU.mult)
                    last.then_inc(*done("hT_ready_dve", "site", i, b))

            def site_tail(i):
                kind, n = SITES[i]
                for t in range(2):
                    dve.wait_ge(*at("y_squares", i, t, 1))
                    TTn(stat[:, 26 + t:27 + t], stat[:, 10 + 2 * t:11 + 2 * t], stat[:, 11 + 2 * t:12 + 2 * t], ALU.add).then_inc(*done("y_sum", i, t))
                    dve.wait_ge(*at("y_root", i, t))
                    dve.reciprocal(stat[:, 28 + t:29 + t], stat[:, 28 + t:29 + t]).then_inc(*done("y_inverse", i, t))
                    dve.wait_ge(*at("y_inverse", i, t))
                    if kind == "ffn":
                        TS(stat[:, 30 + t:31 + t], stat[:, 28 + t:29 + t], 0.5, None, ALU.mult).then_inc(*done("y_half", i, t))
                        dve.wait_ge(*at("y_half", i, t))
                    sc = stat[:, 30 + t:31 + t] if kind == "ffn" else stat[:, 28 + t:29 + t]
                    dve.wait_ge(M.sem("gain_loaded"), 16 * (i + 1))
                    for hf in range(2):
                        if t:
                            dve.wait_ge(*at("x_updated", "site", i, 0, hf))
                        elif i:
                            dve.wait_ge(*at("x_updated", "site", i - 1, 1, hf))
                        else:
                            dve.wait_ge(*at("x_updated", "b1", 1, 1, hf))
                        STT(ytmp[:, hf, :], B[4 + 2 * t + hf][:, :], sc, gain_row[:, hf * 512:(hf + 1) * 512], ALU.mult, ALU.mult).then_inc(*done("out_scaled", "site", i, t, hf))

            def ffn(i, n):
                f0, d0 = n * FFN_CHUNKS, n * (FFN_CHUNKS - 1)

                def product(par, ready, free):
                    dve.wait_ge(s_silu, ready)
                    if free is not None:
                        dve.wait_ge(s_dn, free)
                    TTn(hbuf[:, par, :], B[par][:, T:TT], sgate[:, par, :], ALU.mult).then_inc(s_h, 1)

                product(0, f0 + 1, None)
                product(1, f0 + 2, None)
                with dve.Fori(0, (FFN_PAIRS - 1) // 2) as j:
                    for c in range(4):
                        product(c % 2, j * 4 + (f0 + 3 + c), j * 4 + (d0 + 1 + c))

            def mix(i, n):
                for b in range(16):
                    if b % 2:
                        dve.wait_ge(*at("proj2", n, "qk", b))
                        TS(FQ[:, b, :], B[PB2["qk", b]][:, 0:T], QKSC[b], None, ALU.mult).then_inc(*done("qk_ready_dve", n, b))
                    if b in VAFTER:
                        for vb in VAFTER[b]:
                            dve.wait_ge(*at("proj2", n, "v", vb))
                            CP(FV[:, :, vb * P:(vb + 1) * P], B[PB2["v", vb]][:, 0:T].rearrange("p (t n) -> p t n", t=2)).then_inc(*done("v2_ready", n, vb))
                if n == 0:
                    dve.wait_ge(M.sem("alibi_loaded"), 16)
                dve.wait_ge(*at("lambda_ready", n))

                def unit_bias(u):
                    hd = u if u < N_DIL else N_DIL + (u - N_DIL) // 2
                    dve.wait_ge(*at("scores2", n, u))
                    if u >= 2:
                        dve.wait_ge(*at("exp2_ready", n, u - 2))
                    for qt, (a, w) in enumerate(((0, P), (P, T))):
                        last = dve.tensor_tensor_reduce(out=S2[:, u % 2, a:a + w], in0=B[u % 2][:, a:a + w], in1=alibi[:, hd, a:a + w], scale=-1.0, scalar=-NEG, op0=ALU.add, op1=ALU.min, accum_out=stat[:, 16 + 2 * (u % 2) + qt:17 + 2 * (u % 2) + qt])
                    last.then_inc(*done("neg_max2", n, u))

                def unit_norm(u):
                    dve.wait_ge(*at("exp2_ready", n, u))
                    dve.reciprocal(stat[:, 54 + 2 * (u % 2):56 + 2 * (u % 2)], stat[:, 20 + 2 * (u % 2):22 + 2 * (u % 2)]).then_inc(*done("inverse2", n, u))
                    dve.wait_ge(*at("inverse2", n, u))
                    second = u >= N_DIL and (u - N_DIL) % 2
                    if second:
                        TS(stat[:, 58:60], stat[:, 54 + 2 * (u % 2):56 + 2 * (u % 2)], lamv[:, n, 4:5], None, ALU.mult).then_inc(*done("lambda_scaled", n, u))
                        dve.wait_ge(*at("lambda_scaled", n, u))
                        dve.wait_ge(*at("p2_ready", n, u - 1))
                        for qt, (a, w) in enumerate(((0, P), (P, T))):
                            last = STT(SS[:, u % 4, a:a + w], SS[:, u % 4, a:a + w], stat[:, 58 + qt:59 + qt], SS[:, (u - 1) % 4, a:a + w], ALU.mult, ALU.add)
                    else:
                        for qt, (a, w) in enumerate(((0, P), (P, T))):
                            last = TS(SS[:, u % 4, a:a + w], SS[:, u % 4, a:a + w], stat[:, 54 + 2 * (u % 2) + qt:55 + 2 * (u % 2) + qt], None, ALU.mult)
                    last.then_inc(*done("p2_ready", n, u))

                def head_out(h):
                    b = h // 2
                    dve.wait_ge(*at("attn2", n, h))
                    if b < 3:
                        CP(OT[:, b, :], B[4 + b % 2][:, 0:T]).then_inc(*done("o_ready", n, b))
                    else:
                        CP(OB2[:, b - 3, :], B[4 + b % 2][:, 0:T]).then_inc(*done("ob_ready", n, b - 3))

                NU = N_DIL + 2 * N_DIFF
                unit_bias(0)
                for u in range(NU):
                    if u + 1 < NU:
                        unit_bias(u + 1)
                    unit_norm(u)
                    h = UNIT_HEAD[u]
                    if h is not None and h % 2 == 0 and h:
                        head_out(h - 1)
                head_out(N_DIL + N_DIFF - 1)
                for b in range(2):
                    dve.wait_ge(*at("ob_root", n, b))
                    dve.reciprocal(sgate[:, b, :], sgate[:, b, :]).then_inc(*done("ob_inverse", n, b))
                    dve.wait_ge(*at("ob_inverse", n, b))
                    dve.wait_ge(*at("sub_gain", n))
                    STT(OT[:, 3 + b, :], OB2[:, b, :], lamv[:, n, 5:6], sgate[:, b, :], ALU.mult, ALU.mult).then_inc(*done("o_ready", n, 3 + b))
                for h in range(N_SB):
                    dve.wait_ge(*at("z_ln", n, h))
                    STT(ZP[:, h, :], B[h][:, 0:384], 0.0, ZE[:, h, :], ALU.max, ALU.add).then_inc(*done("softplus_ready", n, h))
                for h in range(N_SB):
                    dve.wait_ge(*at("z_less_sum", n, h))
                    STT(ZE[:, h, :], B[h][:, 0:384], 0.0, gap, ALU.min, ALU.add).then_inc(*done("log_weight", n, h))
                for b in range(3):
                    dve.wait_ge(*at("attn3", n, 2 * b + 1))
                    CP(OT[:, 5 + b, :], B[6 + b % 2][:, 0:T]).then_inc(*done("o_ready", n, 5 + b))

            for i, (kind, n) in enumerate(SITES):
                site_norm(i)
                (ffn if kind == "ffn" else mix)(i, n)
                site_tail(i)

        @block.tensor
        def _(pe):
            mm, tr = pe.matmul, pe.transpose
            readers = {b: [] for b in range(8)}

            def hand_over(b, *reads):
                old, readers[b] = readers[b], list(reads)
                return old

            pe.wait_ge(M.sem("vec_loaded"), 64)
            for r in hand_over(0, ("vec_T", 0)):
                pe.wait_ge(*at(*r))
            b = B[0]
            for q in range(3):
                last = tr(b[:, q * P:(q + 1) * P], vec[:, q, :], ident)
            last.then_inc(*done("vec_transposed"))

            def layer(L):
                nq = TT if L == 0 else T
                nt = nq // P
                pe.wait_ge(*at("silu_c"))
                for r in hand_over(7, ("ada_ready", L)):
                    pe.wait_ge(*at(*r))
                for s in range(ADA_SLOTS):
                    n = base[("ada", L)] + s
                    pe.wait_ge(*filled(n))
                    for q in range(2):
                        blk = 2 * s + q
                        for k in range(KD):
                            last = mm(B[7][:, 2 * blk:2 * blk + 2], cols(n)[:, k, q * P:(q + 1) * P], CS[:, k:16:8], start=(k == 0), stop=(k == KD - 1))
                    last.then_inc(*done("ada_psum", L, s))
                for c in range(KD):
                    for t in range(4):
                        pe.wait_ge(*at("x_scaled", "b1", L, t))
                    for r in hand_over(c % 4, ("hT_ready_act" if c % 2 == 0 else "hT_ready_dve", "b1", L, c)):
                        pe.wait_ge(*at(*r))
                    b = B[c % 4]
                    for t in range(4):
                        last = tr(b[:, t * P:(t + 1) * P], XN[:, t, c * P:(c + 1) * P], ident)
                    last.then_inc(*done("x_T", "b1", L, c))
                pe.wait_ge(M.sem("small_loaded"), SW * (L + 1))
                for r in hand_over(5, ("wsT_ready", L)):
                    pe.wait_ge(*at(*r))
                b = B[5]
                for g in range(4):
                    last = tr(b[:, g * P:(g + 1) * P], w_s[:, g, :], ident)
                last.then_inc(*done("ws_transposed", L))
                for c in range(KD):
                    pe.wait_ge(*at("hT_ready_act" if c % 2 == 0 else "hT_ready_dve", "b1", L, c))

                n0 = base[("win", L)]

                def project(name, j, n, lhs, out_rows, ncol, reader):
                    key = (name,) if j is None else (name, j)
                    for r in hand_over(PB[L][key if j is not None else name], reader):
                        pe.wait_ge(*at(*r))
                    b = B[PB[L][key if j is not None else name]]
                    for k in range(KD):
                        last = mm(b[out_rows, 0:ncol], lhs(k), hT[:, k, 0:ncol], start=(k == 0), stop=(k == KD - 1))
                    last.then_inc(*done("proj", L, *key))
                    return last

                def col(n, w, a, m):
                    return lambda k: cols(n, w)[:, k, a:a + m]

                allp = slice(0, P)

                def sq_sums():
                    for r in hand_over(6, ("q_root", L)):
                        pe.wait_ge(*at(*r))
                    for j in range(2):
                        pe.wait_ge(*at("q_part_ready", L, j))
                        last = mm(B[6][:, 0:nq], ones, sq[:, j, 0:nq], start=(j == 0), stop=(j == 1))
                    last.then_inc(*done("q_square_sum", L))
                    for r in hand_over(7, ("kv_root", L)):
                        pe.wait_ge(*at(*r))
                    pe.wait_ge(*at("kv_part_ready", L))
                    mm(B[7][:, :], ones, sq[:, 2, :], start=True, stop=True).then_inc(*done("kv_square_sum", L))

                pe.wait_ge(*filled(n0))
                for j in range(2):
                    project("q", j, n0, col(n0, 256, j * P, P), allp, nq, ("q_part_ready", L, j))
                n = n0 + 1
                pe.wait_ge(*filled(n))
                project("kv", None, n, col(n, 160, 0, P), allp, TT, ("kv_part_ready", L))
                project("kr", None, n, col(n, 160, P, ROPE), slice(NOPE, QK), TT, ("kr_copied", L))
                pe.wait_ge(*at("kr_swapped", L))
                project("krs", None, n, lambda k: w_krs[:, k, :], slice(NOPE, QK), T, ("kr_sin", L))
                for name, s, rd in (("a", 2, "a_ready"), ("g", 3, "conv_gate_ready"), ("f", 4, "f_ready"), ("u", 5, "u_ready")):
                    n = n0 + s
                    pe.wait_ge(*filled(n))
                    for j in range(2):
                        project(name, j, n, col(n, 256, j * P, P), allp, nq, (rd, L, j))
                    if name == "a":
                        sq_sums()
                n = n0 + 6
                pe.wait_ge(*filled(n))
                for t in range(nt):
                    for r in hand_over(PB[L]["v", t], ("v_copied", L, t)):
                        pe.wait_ge(*at(*r))
                    b = B[PB[L]["v", t]]
                    for k in range(KD):
                        last = mm(b[:, 0:256], hT[:, k, t * P:(t + 1) * P], cols(n)[:, k, :], start=(k == 0), stop=(k == KD - 1))
                    last.then_inc(*done("proj", L, "v", t))
                pe.wait_ge(M.sem("base_loaded"), 48)
                for t in range(nt):
                    for r in hand_over(6 + t % 2, ("fa_ready", L, t)):
                        pe.wait_ge(*at(*r))
                    b = B[6 + t % 2]
                    for j in range(2):
                        pe.wait_ge(*at("f_ready", L, j))
                        last = mm(b[:, j * 256:(j + 1) * 256], fT[:, j, t * P:(t + 1) * P], dft_d, start=True, stop=True)
                    last.then_inc(*done("fourier_feat", L, t))
                for s in range(4):
                    n = n0 + 7 + s
                    pe.wait_ge(*filled(n))
                    for q in range(2):
                        j = 2 * s + q
                        project("gate", j, n, col(n, 256, q * P, P), allp, nq, ("sg_ready", L, j))
                    if s == 0:
                        for m in range(2):
                            for r in hand_over(6 + m, ("f_mixed", L, m)):
                                pe.wait_ge(*at(*r))
                            b = B[6 + m]
                            for sg in range(nq // T):
                                q = 0
                                for tl in range(2):
                                    pe.wait_ge(*at("fa_ready", L, 2 * sg + tl))
                                    for cs in range(2):
                                        last = mm(b[:, sg * T:(sg + 1) * T], FA[:, 2 * sg + tl, m, cs * P:(cs + 1) * P], dft_n[:, cs, tl, :], start=(q == 0), stop=(q == 3))
                                        q += 1
                            last.then_inc(*done("fourier_tok", L, m))
                    if s == 1:
                        for m in range(2):
                            for r in hand_over(4 + m, ("four_branch", L, m)):
                                pe.wait_ge(*at(*r))
                            b = B[4 + m]
                            for j in range(2):
                                pe.wait_ge(*at("f_mixed", L, j))
                                last = mm(b[:, 0:nq], w_fo[:, j, m * P:(m + 1) * P], cacc[:, j, 0:nq], start=(j == 0), stop=(j == 1))
                            last.then_inc(*done("fourier_out", L, m))
                pe.wait_ge(*at("wsT_ready", L))
                for m in range(2):
                    for r in hand_over(6 + m, ("sgu_branch", L, m)):
                        pe.wait_ge(*at(*r))
                    b = B[6 + m]
                    for t in range(nt):
                        pe.wait_ge(*at("v_ready", L, t))
                        for gg in range(2):
                            g = 2 * m + gg
                            o = b[gg * 64:(gg + 1) * 64, t * P:(t + 1) * P]
                            mm(o, VN[:, t, g * 64:(g + 1) * 64], wsT[:, g, :], start=True, stop=False)
                            last = mm(o, ones[0:1, 0:64], bsrow[0:1, L, g * P:(g + 1) * P], start=False, stop=True)
                    last.then_inc(*done("sgu_mixed", L, m))
                for v in range(nq // T):
                    for hf in range(2):
                        for r in hand_over((2 * v + hf) % 4, ("gate_row_ready", L, v, hf)):
                            pe.wait_ge(*at(*r))
                        b = B[(2 * v + hf) % 4]
                        pe.wait_ge(*at("gate_diag_ready", L, v, hf))
                        mm(b[:, :], ones, gate_diag[:, hf, :], start=True, stop=True).then_inc(*done("gate_rows", L, v, hf))
                pe.wait_ge(*at("uq_swapped", L))
                for h in range(HEADS):
                    for r in hand_over(h % 2, ("q_copied", L, h)):
                        pe.wait_ge(*at(*r))
                    b = B[h % 2]
                    for j in range(2):
                        pe.wait_ge(*at("q_latent", L, j))
                        last = mm(b[0:QK, 0:nq], w_uq[:, j, h * QK:(h + 1) * QK], qp[:, j, 0:nq], start=(j == 0), stop=(j == 1))
                    last.then_inc(*done("q_heads", L, h))
                    for r in hand_over(2 + h % 2, ("q_sin", L, h)):
                        pe.wait_ge(*at(*r))
                    b = B[2 + h % 2]
                    for j in range(2):
                        last = mm(b[NOPE:QK, 0:T], w_uqs[:, j, h * ROPE:(h + 1) * ROPE], qp[:, j, 0:T], start=(j == 0), stop=(j == 1))
                    last.then_inc(*done("q_swapped", L, h))
                pe.wait_ge(*at("kv_latent", L))
                for h in range(HEADS):
                    for r in hand_over(h % 2, ("k_copied", L, h)):
                        pe.wait_ge(*at(*r))
                    b = B[h % 2]
                    mm(b[0:NOPE, :], w_ukv[:, h * P:h * P + NOPE], kvp, start=True, stop=True).then_inc(*done("k_heads", L, h))
                vcols = w_ukv.rearrange("p (h n) -> p h n", h=4)[:, :, NOPE:P]
                for t in range(4):
                    for r in hand_over(4 + t, ("v_heads_ready", L, t)):
                        pe.wait_ge(*at(*r))
                    b = B[4 + t]
                    mm(b[:, 0:256].rearrange("p (h n) -> p h n", h=4), kvp[:, t * P:(t + 1) * P], vcols, start=True, stop=True).then_inc(*done("v_heads", L, t))
                pe.wait_ge(*at("k_rope_ready", L))
                for seg in range(nq // T):
                    k0, keys = (0, TT) if seg == 0 else (T, T)
                    for h in range(HEADS):
                        pe.wait_ge(*at("k_copied", L, h))
                        pe.wait_ge(*at("q_ready", L, h))
                        for qt in range(2):
                            for r in hand_over(qt, ("exp_ready", L, seg, h, qt)):
                                pe.wait_ge(*at(*r))
                            b = B[qt]
                            mm(b[:, 0:keys], Q[0:QK, h, seg * T + qt * P:seg * T + (qt + 1) * P], K[0:QK, h, k0:k0 + keys], start=True, stop=True).then_inc(*done("scores", L, seg, h, qt))
                        for qt in range(2):
                            for r in hand_over(2 + qt, ("pT_ready", L, seg, h, qt)):
                                pe.wait_ge(*at(*r))
                            b = B[2 + qt]
                            pe.wait_ge(*at("p_ready", L, seg, h, qt))
                            for kt in range(keys // P):
                                last = tr(b[:, kt * P:(kt + 1) * P], Pm[:, qt, kt * P:(kt + 1) * P], ident)
                            last.then_inc(*done("p_T", L, seg, h, qt))
                        b = B[4 + h // 2]
                        if h % 2 == 0:
                            for r in hand_over(4 + h // 2, ("attn_ready", L, h + 1, seg)):
                                pe.wait_ge(*at(*r))
                        for qt in range(2):
                            pe.wait_ge(*at("pT_ready", L, seg, h, qt))
                        for kt in range(keys // P):
                            pe.wait_ge(*at("v_heads_ready", L, k0 // P + kt))
                            last = mm(b[(h % 2) * 64:(h % 2 + 1) * 64, 0:T], V[:, k0 // P + kt, h * 64:(h + 1) * 64], PT[:, kt, :], start=(kt == 0), stop=(kt == keys // P - 1))
                        last.then_inc(*done("attn", L, seg, h))
                for j in range(2):
                    pe.wait_ge(*at("conv_tap", L, j, CONV_K - 1))
                for r in hand_over(0, ("conv_centred", L, 1)):
                    pe.wait_ge(*at(*r))
                b = B[0]
                for j in range(2):
                    last = mm(b[:, 0:nq], ones, cacc[:, j, 0:nq], start=(j == 0), stop=(j == 1))
                last.then_inc(*done("conv_mean", L))
                for r in hand_over(1, ("conv_root", L)):
                    pe.wait_ge(*at(*r))
                b = B[1]
                for j in range(2):
                    pe.wait_ge(*at("conv_square", L, j))
                    last = mm(b[:, 0:nq], ones, sq[:, j, 0:nq], start=(j == 0), stop=(j == 1))
                last.then_inc(*done("conv_var", L))
                for m in range(2):
                    for r in hand_over(2 + m, ("conv_branch", L, m)):
                        pe.wait_ge(*at(*r))
                    b = B[2 + m]
                    for j in range(2):
                        pe.wait_ge(*at("conv_act", L, j))
                        last = mm(b[:, 0:nq], w_pw[:, j, m * P:(m + 1) * P], csg[:, j, 0:nq], start=(j == 0), stop=(j == 1))
                    last.then_inc(*done("conv_out", L, m))
                for stage in ("four_branch", "sgu_branch", "conv_branch"):
                    pe.wait_ge(*at(stage, L, 1))
                pe.wait_ge(*at("attn_ready", L, HEADS - 1, nq // T - 1))
                for t in range(nt):
                    for hf in range(2):
                        for r in hand_over(YB[L][t, hf], ("out_scaled", "b1", L, t, hf)):
                            pe.wait_ge(*at(*r))
                for s in range(4):
                    n = base[("wout", L)] + s
                    pe.wait_ge(*filled(n))
                    for r in range(2):
                        k = 2 * s + r
                        for t in range(nt):
                            for hf in range(2):
                                last = mm(B[YB[L][t, hf]][:, :], SG[:, k, t * P:(t + 1) * P], rows(n)[:, r, hf * 512:(hf + 1) * 512], start=(k == 0), stop=(k == KD - 1))
                                if k == KD - 1:
                                    last.then_inc(*done("y_ready", "b1", L, t, hf))
                    if s < 3:
                        last.then_inc(*done("wout_used", L, s))

            def site_norm(i):
                for b in range(4):
                    for r in hand_over(b, ("hT_ready_act" if b % 2 == 0 else "hT_ready_dve", "site", i, b)):
                        pe.wait_ge(*at(*r))
                    bk = B[b]
                    for q in range(2):
                        for t in range(2):
                            pe.wait_ge(*at("x_scaled", "site", i, t))
                            c = 2 * b + q
                            last = tr(bk[:, q * T + t * P:q * T + (t + 1) * P], XN[:, t, c * P:(c + 1) * P], ident)
                    last.then_inc(*done("x_T", "site", i, b))
                for b in range(4):
                    pe.wait_ge(*at("hT_ready_act" if b % 2 == 0 else "hT_ready_dve", "site", i, b))

            def ffn(i, n):
                f0 = n * FFN_CHUNKS
                b0 = base[("ffn", n)]
                for q in range(4):
                    for r in hand_over(q):
                        pe.wait_ge(*at(*r))
                for t in range(2):
                    for hf in range(2):
                        for r in hand_over(4 + 2 * t + hf, ("out_scaled", "site", i, t, hf)):
                            pe.wait_ge(*at(*r))

                def gate_up(par, slot_n, free, j=None):
                    if free is not None:
                        pe.wait_ge(s_h, free)
                    for q in range(2):
                        pe.wait_ge(*at_slot(slot_n + q, j))
                        w = cols(slot_n + q)
                        for k in range(KD):
                            last = mm(B[par][:, q * T:(q + 1) * T], w[:, k, par * P:(par + 1) * P], hT[:, k, 0:T], start=(k == 0), stop=(k == KD - 1))
                    last.then_inc(s_gu, 1)

                def down(par, slot_n, ready, first, final, j=None):
                    pe.wait_ge(s_h, ready)
                    pe.wait_ge(*at_slot(slot_n, j))
                    w = rows(slot_n)
                    for t in range(2):
                        for hf in range(2):
                            last = mm(B[4 + 2 * t + hf][:, :], hbuf[:, par, t * P:(t + 1) * P], w[:, par, hf * 512:(hf + 1) * 512], start=first, stop=final, skip_group_check=True)
                            if final:
                                last.then_inc(*done("y_ready", "site", i, t, hf))
                    if not final:
                        last.then_inc(s_dn, 1)

                def at_slot(m, j=None):
                    v = 16 * (m // RING + 1)
                    return slot_loaded[m % RING], v if j is None else j * 16 + v

                gate_up(0, b0, f0 if n else None)
                gate_up(1, b0, f0 if n else None)
                down(0, b0 + 2, f0 + 1, True, False)
                with pe.Fori(0, (FFN_PAIRS - 1) // 2) as j:
                    for c in range(2):
                        m = b0 + 3 * (1 + c)
                        fc = f0 + 2 + 2 * c
                        gate_up(0, m, j * 4 + (fc - 1), j)
                        down(1, m - 1, j * 4 + fc, False, False, j)
                        gate_up(1, m, j * 4 + fc, j)
                        down(0, m + 2, j * 4 + (fc + 1), False, False, j)
                down(1, b0 + FFN_SLOTS - 1, f0 + FFN_CHUNKS, False, True)

            def mix(i, n):
                n0 = base[("win2", n)]
                for blk in range(24):
                    s = n0 + blk // 2
                    pe.wait_ge(*filled(s))
                    kind, idx = BLOCKS2[blk]
                    w = cols(s)
                    a = (blk % 2) * P
                    if kind == "qk":
                        for r in hand_over(PB2[kind, idx], ("qk_ready_act" if idx % 2 == 0 else "qk_ready_dve", n, idx)):
                            pe.wait_ge(*at(*r))
                        b = B[PB2[kind, idx]]
                        for k in range(KD):
                            last = mm(b[:, 0:T], w[:, k, a:a + P], hT[:, k, 0:T], start=(k == 0), stop=(k == KD - 1))
                    else:
                        for r in hand_over(PB2[kind, idx], ("v2_ready", n, idx)):
                            pe.wait_ge(*at(*r))
                        b = B[PB2[kind, idx]]
                        for t in range(2):
                            for k in range(KD):
                                last = mm(b[:, t * P:(t + 1) * P], hT[:, k, t * P:(t + 1) * P], w[:, k, a:a + P], start=(k == 0), stop=(k == KD - 1))
                    last.then_inc(*done("proj2", n, kind, idx))
                for b in range(16):
                    pe.wait_ge(*at("qk_ready_act" if b % 2 == 0 else "qk_ready_dve", n, b))

                def score(u):
                    if u < N_DIL:
                        qb, kb, p0, kk = u // 2, 3 + u // 2, (u % 2) * 64, 64
                    else:
                        d = u - N_DIL
                        qb, kb, p0, kk = 6 + d // 4, 8 + d // 4, (d % 4) * 32, 32
                    for r in hand_over(u % 2, ("neg_max2", n, u)):
                        pe.wait_ge(*at(*r))
                    b = B[u % 2]
                    mm(b[:, 0:P], FQ[p0:p0 + kk, qb, 0:P], FQ[p0:p0 + kk, kb, 0:P], start=True, stop=True)
                    mm(b[:, P:384], FQ[p0:p0 + kk, qb, P:T], FQ[p0:p0 + kk, kb, :], start=True, stop=True).then_inc(*done("scores2", n, u))

                def value(h, u):
                    for r in hand_over(2 + h % 2, ("pT2_ready", n, h)):
                        pe.wait_ge(*at(*r))
                    b = B[2 + h % 2]
                    pe.wait_ge(*at("p2_ready", n, u))
                    src = SS[:, u % 4, :]
                    tr(b[:, 0:P], src[:, 0:P], ident)
                    tr(b[:, P:T], src[:, P:T], ident)
                    tr(b[:, T:384], src[:, T:384], ident).then_inc(*done("p2_T", n, h))

                def weighted(h):
                    blk = h // 2
                    if h % 2 == 0:
                        for r in hand_over(4 + blk % 2, ("o_ready", n, blk) if blk < 3 else ("ob_ready", n, blk - 3)):
                            pe.wait_ge(*at(*r))
                    o = B[4 + blk % 2][(h % 2) * 64:(h % 2 + 1) * 64, :]
                    pe.wait_ge(*at("pT2_ready", n, h))
                    pe.wait_ge(*at("v2_ready", n, 4))
                    mm(o[:, 0:T], FV[:, 0, h * 64:(h + 1) * 64], PT2[:, h % 2, 0:T], start=True, stop=False, skip_group_check=True)
                    mm(o[:, P:T], FV[:, 1, h * 64:(h + 1) * 64], PT2[:, h % 2, T:384], start=False, stop=True, skip_group_check=True).then_inc(*done("attn2", n, h))

                NU = N_DIL + 2 * N_DIFF
                score(0)
                for u in range(NU):
                    if u + 1 < NU:
                        score(u + 1)
                    h = UNIT_HEAD[u]
                    if h is not None:
                        value(h, u)
                        weighted(h)
                def z(h):
                    for r in hand_over(h, ("log_weight", n, h)):
                        pe.wait_ge(*at(*r))
                    b = B[h]
                    p0, qb, kb = (h % 2) * 64, 10 + h // 2, 13 + h // 2
                    mm(b[:, 0:T], FQ[p0:p0 + 64, kb, 0:P], FQ[p0:p0 + 64, qb, :], start=True, stop=False, skip_group_check=True)
                    mm(b[:, T:384], FQ[p0:p0 + 64, kb, P:T], FQ[p0:p0 + 64, qb, P:T], start=False, stop=False, skip_group_check=True).then_inc(*done("z_ready", n, h))

                for b in range(2):
                    pe.wait_ge(*at("ob_square", n, b))
                    for r in hand_over(4 + b, ("ob_root", n, b)):
                        pe.wait_ge(*at(*r))
                    mm(B[4 + b][:, T:TT], heads2, sgate[:, b, :], start=True, stop=True).then_inc(*done("ob_sum", n, b))
                for h in range(N_SB):
                    z(h)
                for h in range(N_SB):
                    pe.wait_ge(*at("softplus_masked", n, h))
                    mm(B[h][:, 0:384], ntri, ZP[:, h, :], start=False, stop=False, skip_group_check=True)
                    mm(B[h][:, P:T], negones, ZP[:, h, T:384], start=False, stop=True, skip_group_check=True).then_inc(*done("z_less_sum", n, h))
                for h in range(N_SB):
                    if h % 2 == 0:
                        for r in hand_over(6 + (h // 2) % 2, ("o_ready", n, 5 + h // 2)):
                            pe.wait_ge(*at(*r))
                    o = B[6 + (h // 2) % 2][(h % 2) * 64:(h % 2 + 1) * 64, :]
                    pe.wait_ge(*at("weight_ready", n, h))
                    pe.wait_ge(*at("v2_ready", n, 7))
                    hv = N_DIL + N_DIFF + h
                    mm(o[:, 0:T], FV[:, 0, hv * 64:(hv + 1) * 64], ZP[:, h, 0:T], start=True, stop=False, skip_group_check=True)
                    mm(o[:, P:T], FV[:, 1, hv * 64:(hv + 1) * 64], ZP[:, h, T:384], start=False, stop=True, skip_group_check=True).then_inc(*done("attn3", n, h))
                for t in range(2):
                    for hf in range(2):
                        for r in hand_over(4 + 2 * t + hf, ("out_scaled", "site", i, t, hf)):
                            pe.wait_ge(*at(*r))
                for s in range(4):
                    m = base[("wout2", n)] + s
                    pe.wait_ge(*filled(m))
                    for r in range(2):
                        k = 2 * s + r
                        pe.wait_ge(*at("o_ready", n, k))
                        for t in range(2):
                            for hf in range(2):
                                last = mm(B[4 + 2 * t + hf][:, :], OT[:, k, t * P:(t + 1) * P], rows(m)[:, r, hf * 512:(hf + 1) * 512], start=(k == 0), stop=(k == KD - 1))
                                if k == KD - 1:
                                    last.then_inc(*done("y_ready", "site", i, t, hf))
                    if s < 3:
                        last.then_inc(*done("wout2_used", n, s))

            layer(0)
            layer(1)
            for i, (kind, n) in enumerate(SITES):
                site_norm(i)
                (ffn if kind == "ffn" else mix)(i, n)


INPUTS = ["x", "c", "ctx", "c_ctx", "w_ada", "w_in", "w_uq", "w_ukv", "w_pw", "w_fourier", "sgu_ln_g", "sgu_ln_b", "w_s", "b_s",
          "w_out", "final_g", "norm_gains_2", "w_ffn_gate_2", "w_ffn_up_2", "w_ffn_down_2", "w_in_2", "w_out_2", "diff_lambda_2"]
VECTORS = ["b_ada", "norm_g", "q_norm_g", "kv_norm_g", "conv_w", "conv_b", "conv_ln_g", "conv_ln_b", "b_pw", "b_fourier"]


def kernel(**inputs):
    import numpy as _np
    import concourse.bacc as _bacc
    from contextlib import ExitStack as _ExitStack
    from concourse import mybir as _mybir
    from concourse.bass_utils import run_bass_kernel_spmd as _run

    a = {k: _np.asarray(v) for k, v in inputs.items()}
    arrays = {n: _np.ascontiguousarray(a[n]) for n in INPUTS if n not in ("c", "c_ctx")}
    banks = []
    for L in range(2):
        rows = [a[n][L].reshape(-1, 128) for n in VECTORS] + [a["c"].reshape(-1, 128), a["c_ctx"].reshape(-1, 128)]
        rows.append(_np.zeros((128 - sum(r.shape[0] for r in rows), 128), _np.float32))
        banks.append(_np.concatenate(rows))
    arrays["k_vec1"] = _np.stack(banks)
    rows = [a["norm_gains_2"][i // 3, 2 * (i % 3)].reshape(-1, 128) for i in range(6)]
    rows += [_np.concatenate([a["diff_subln_gain_2"][m]] * 2)[None] for m in range(2)]
    rows.append(_np.zeros((128 - 50, 128), _np.float32))
    arrays["k_vec2"] = _np.concatenate(rows)
    arrays.update(constants())

    def build(table):
        nc = _bacc.Bacc("TRN2", target_bir_lowering=False, num_devices=1)
        I = {n: nc.dram_tensor("in_" + n, v.shape, _mybir.dt.from_np(v.dtype), kind="ExternalInput").ap() for n, v in arrays.items()}
        out = nc.dram_tensor("out_0", (1, 256, 1024), _mybir.dt.float32, kind="ExternalOutput").ap()
        program(nc, I, out, table)
        return nc

    table = {}
    build(table)
    nc = build(table)
    r = _run(nc, [{"in_" + n: v for n, v in arrays.items()}], core_ids=[0])
    return r.results[0]["out_0"]
```

```python
from contextlib import ExitStack

import numpy as np
import concourse.bass as bass
from concourse import mybir

F32 = mybir.dt.float32
F32R = mybir.dt.float32r
ACT = mybir.ActivationFunctionType
ALU = mybir.AluOpType
AXX = mybir.AxisListType.X

P = 128
D = 1024
KD = D // P
T = 256
TT = 512
RMS_EPS = 1e-6
LN_EPS = 1e-5

HEADS = 4
NOPE = 64
ROPE = 32
QK = NOPE + ROPE
CONV_K = 31
PAD = CONV_K // 2
SEGP = T + 2 * PAD
FG_DIM = 64
ADA_SLOTS = 12
WIN_SLOTS = [(0, 256), (256, 160), (416, 256), (672, 256), (928, 256), (1184, 256), (1440, 256),
             (1696, 256), (1952, 256), (2208, 256), (2464, 256)]
R_BADA, R_NORM, R_QN, R_KVN, R_CW, R_CB, R_CLG, R_CLB, R_BPW, R_BF, R_C = 0, 24, 32, 34, 35, 97, 99, 101, 103, 105, 107
R_B1 = 107 + 16
R_SUB = 48

N_DIL, N_DIFF, N_SB = 6, 4, 6
FF = 2816
FFN_PAIRS = FF // (2 * P)
FFN_CHUNKS = FF // P
FFN_SLOTS = 3 * FFN_PAIRS
NEG = -1.0e30
RING = 3
SPLIT = 6


class Marks:

    def __init__(self, nc, ctx, table):
        self.nc, self.ctx, self.table = nc, ctx, table
        self.sems, self.counts = {}, {}

    def sem(self, stage):
        if stage not in self.sems:
            self.sems[stage] = self.ctx.enter_context(self.nc.semaphore(stage))
        return self.sems[stage]

    def done(self, stage, *key):
        s = self.sem(stage)
        self.counts[stage] = self.counts.get(stage, 0) + 1
        self.table[(stage,) + key] = self.counts[stage]
        return s, 1

    def at(self, stage, *key):
        return self.sem(stage), self.table.get((stage,) + key, 1)


def constants():
    f = np.float32
    out = {}
    i = np.arange(P)
    ident = np.eye(P, dtype=f)
    ones = np.ones((P, P), f)
    heads2 = np.kron(np.eye(2), np.ones((64, 64))).astype(f) / 64
    ntri = -(i[:, None] >= i[None, :]).astype(f)
    a = 2 * np.pi * np.outer(np.arange(FG_DIM), np.arange(FG_DIM)) / FG_DIM
    scale = 1.0 / np.sqrt(T * FG_DIM)
    dft_d = np.concatenate([np.kron(np.eye(2), np.cos(a)), np.kron(np.eye(2), -np.sin(a))], 1) * scale
    b = 2 * np.pi * (np.outer(np.arange(T), np.arange(T)) % T) / T
    dft_n = np.stack([np.cos(b), np.sin(b)]).reshape(2, 2, P, T).transpose(2, 0, 1, 3).reshape(P, -1)
    strict = (i[:, None] < i[None, :]).astype(f)
    full = np.concatenate([strict, ones, strict], 1)
    gap = np.where(full > 0, 0.0, NEG)
    rows = T // 64
    inv = (f(10000.0) ** (-np.arange(0, 16, 2, dtype=f) / f(16))).astype(f)
    row = np.repeat(np.arange(rows), 64).astype(f)
    col = np.tile(np.arange(64), rows).astype(f)
    ang = np.stack([row[:, None] * inv, col[:, None] * inv], 1).astype(f)
    rope = np.zeros((P, 2 * T), f)
    for d in range(ROPE):
        ax, half, fr = d // 16, (d % 16) // 8, d % 8
        rope[NOPE + d, :T] = np.cos(ang[:, ax, fr])
        rope[NOPE + d, T:] = np.sin(ang[:, ax, fr]) * (1 if half else -1)
    out["k_base"] = np.concatenate([ident, ones, heads2, ntri, -ones, dft_d, dft_n, full, gap, rope], 1).astype(f)
    q = np.concatenate([np.tile(i[:, None], (1, P)), np.tile(P + i[:, None], (1, T))], 1)
    k = np.concatenate([i, np.arange(T)])[None, :]
    dist = q - k
    tabs = []
    count = (dist <= 128).astype(int) + (dist % 4 == 0) + (dist % 16 == 0)
    for h in range(N_DIL):
        slope = 2.0 ** (-8.0 * (h + 1) / N_DIL)
        ok = (dist >= 0) & (count > 0)
        tabs.append(np.where(ok, -slope * dist + np.log(np.maximum(count, 1)), NEG))
    for h in range(N_DIFF):
        slope = 2.0 ** (-8.0 * (h + 1) / N_DIFF)
        tabs.append(np.where(dist >= 0, -slope * dist, NEG))
    out["k_alibi"] = np.concatenate(tabs, 1).astype(f)
    return out


C_ID, C_ONES, C_H2, C_NTRI, C_NONE, C_DD, C_DN, C_FULL, C_GAP, C_ROPE, C_END = (
    0, 128, 256, 384, 512, 640, 896, 1920, 2304, 2688, 3200)

LAM_INIT = [0.8 - 0.6 * float(np.exp(-0.3 * m)) for m in range(2)]


def projection_banks():
    out = []
    for L in range(2):
        names = [("q", 0), ("q", 1), ("kv",), ("kr",), ("krs",)]
        names += [(n, j) for n in "agfu" for j in range(2)]
        names += [("v", t) for t in range(4 if L == 0 else 2)] + [("gate", j) for j in range(8)]
        out.append({(n if len(n) > 1 else n[0]): i % 4 for i, n in enumerate(names)})
    return out


PB = projection_banks()
ADA_AT = (slice(0, 2), slice(32, 34))
ADA_STEP = [range(3 * i // 2, 3 * (i + 1) // 2) for i in range(8)]
YB = [{(t, h): 2 * t + h for t in range(4) for h in range(2)}, {(t, h): 4 + 2 * t + h for t in range(2) for h in range(2)}]
MIX_SLOTS = [((0, 1), "qk", (0, 1)), ((2, 3), "qk", (2, 3)), ((4, 5), "qk", (4, 5)), ((6, 7), "v", (0, 1)), ((8, 23), "v", (2, 7)),
             ((9, 10), "qk", (6, 7)), ((11, 12), "qk", (8, 9)), ((13, 14), "v", (3, 4)),
             ((15, 16), "qk", (10, 11)), ((17, 18), "qk", (12, 13)), ((19, 20), "qk", (14, 15)), ((21, 22), "v", (5, 6))]
PROJ2 = [(kind, b) for _, kind, bs in MIX_SLOTS for b in (bs if kind == "qk" else bs[:1])]
PB2 = {b: i % 4 for i, b in enumerate(PROJ2)}
QKSC = [0.125] * 3 + [1.0] * 3 + [32 ** -0.5] * 2 + [1.0] * 2 + [0.125] * 3 + [1.0] * 3
UNIT_HEAD = list(range(N_DIL)) + [h for d in range(N_DIFF) for h in (None, N_DIL + d)]


def program(nc, I, out, table):
    ctx = ExitStack()
    with ctx:
        def sb(name, shape, scope=ctx, dt=F32):
            return scope.enter_context(nc.sbuf_tensor(name, shape, dt))

        M = Marks(nc, ctx, table)
        done, at = M.done, M.at

        ring = sb("weight_ring", [P, RING, 2048])
        X = sb("residual", [P, 2, D])
        KB = sb("const_base", [P, C_END])
        vec = sb("vectors", [P, 3, P])
        vT = sb("vectors_T", [P, 3, P])
        CS = sb("silu_c", [P, 16])
        ada = sb("ada", [P, 24, 2])
        adag = sb("ada_gain", [P, KD, 2])
        stat = sb("stat", [P, 64])
        eps = sb("eps", [P, 4])
        ada_row = sb("ada_rows", [34, 256])
        gain_row = sb("gain_row", [P, D])
        ytmp = sb("scaled_out", [P, 2, 512])
        lam_in = sb("lambda_in", [P, 2, 128])
        lamv = sb("lambda", [P, 2, 8])
        first = ctx.enter_context(ExitStack())
        XC = sb("residual_ctx", [P, 2, D], first)
        SG = sb("gated", [P, KD, TT], first)
        XN = SG[:, :, :].rearrange("p a b -> p (a b)").rearrange("p (t d) -> p t d", t=4)
        hT = sb("hT", [P, KD, TT], first)
        GB = hT[:, :, :].rearrange("p a b -> p (a b)").rearrange("p (v d) -> p v d", v=4)
        gate_diag = sb("gate_diag", [P, 2, 512], first)
        bsrow = sb("b_s_row", [1, 1024], first)[:, :].rearrange("p (l n) -> p l n", l=2)
        arena = sb("arena", [P, 19320], first)
        room = [0]

        def carve(n):
            a = room[0]
            room[0] += n
            assert room[0] <= 19320
            return arena[:, a:a + n]

        w_uq = carve(768).rearrange("p (j n) -> p j n", j=2)
        w_uqs = carve(256).rearrange("p (j n) -> p j n", j=2)
        w_ukv = carve(512)
        w_pw = carve(512).rearrange("p (j n) -> p j n", j=2)
        w_fo = carve(512).rearrange("p (j n) -> p j n", j=2)
        w_s = carve(512).rearrange("p (g n) -> p g n", g=4)
        wsT = carve(512).rearrange("p (g n) -> p g n", g=4)
        w_krs = carve(256).rearrange("p (k n) -> p k n", k=8)
        sgu_row = carve(512).rearrange("p (a n) -> p a n", a=2)
        qp = carve(1024).rearrange("p (j n) -> p j n", j=2)
        kvp = carve(512)
        sq = carve(1536).rearrange("p (j n) -> p j n", j=3)
        rq = carve(1024).rearrange("p (j n) -> p j n", j=2)
        krot = carve(512)
        CG = carve(4 * SEGP).rearrange("p (j s n) -> p j s n", j=2, s=2)
        cacc = carve(1024).rearrange("p (j n) -> p j n", j=2)
        csg = carve(1024).rearrange("p (j n) -> p j n", j=2)
        fT = carve(1024).rearrange("p (j n) -> p j n", j=2)
        FA = carve(2048).rearrange("p (t j n) -> p t j n", t=4, j=2)
        U = carve(1024).rearrange("p (j n) -> p j n", j=2)
        VN = carve(1024).rearrange("p (t n) -> p t n", t=4)
        Q = carve(2048).rearrange("p (h n) -> p h n", h=4)
        K = FA.rearrange("p t j n -> p (t j n)").rearrange("p (h n) -> p h n", h=4)
        V = fT.rearrange("p j n -> p (j n)").rearrange("p (t n) -> p t n", t=4)
        Pm = [w.rearrange("p t n -> p (t n)").rearrange("p (b n) -> p b n", b=2) for w in (VN, sq[:, 0:2, :])]
        PT = [w.rearrange("p j n -> p (j n)").rearrange("p (k n) -> p k n", k=4) for w in (U, csg)]
        ropet = gate_diag[:, 0, :]
        first.close()
        XN2 = sb("x_scaled_2", [P, 2, D])
        WH = sb("weights_high", [P, SPLIT, 1024], dt=F32R)
        WL = sb("weights_low", [P, SPLIT, 1024], dt=F32R)
        HH = sb("input_high", [P, KD, T], dt=F32R)
        HL = sb("input_low", [P, KD, T], dt=F32R)
        HBH = sb("hidden_high", [P, 2, T], dt=F32R)
        HBL = sb("hidden_low", [P, 2, T], dt=F32R)
        hbuf = sb("hidden", [P, 2, T])
        sgate = sb("silu_gate", [P, 2, T])
        alibi = sb("alibi", [P, 10, 384])
        FQ = sb("qk_feature_major", [P, 16, T])
        FV = sb("v_token_major", [P, 2, D])
        ZE = sb("mixer_maps", [P, 6, 384])
        SS, S2 = ZE[:, 0:4, :], ZE[:, 4:6, :]
        PT2 = sb("weights_T", [P, 2, 384])
        ZP = sb("softplus", [P, 6, 384])
        OB2 = sb("differential_out", [P, 2, T])

        ident, ones = KB[:, C_ID:C_ID + P], KB[:, C_ONES:C_ONES + P]
        heads2, ntri, negones = (KB[:, c:c + P] for c in (C_H2, C_NTRI, C_NONE))
        dft_d = KB[:, C_DD:C_DD + 256]
        dft_n = KB[:, C_DN:C_DN + 1024].rearrange("p (s t n) -> p s t n", s=2, t=2)
        full, gap = KB[:, C_FULL:C_FULL + 384], KB[:, C_GAP:C_GAP + 384]
        rcos, rsin = KB[NOPE:QK, C_ROPE:C_ROPE + T], KB[NOPE:QK, C_ROPE + T:C_ROPE + 2 * T]

        B = [ctx.enter_context(nc.psum_tensor(f"bank{i}", [P, 512], F32)) for i in range(8)]

        slot_loaded = [M.sem(f"slot{i}_loaded") for i in range(RING)]
        s_silu, s_h, s_hh, s_hl = (M.sem(n) for n in ("silu_ready", "hidden_ready", "hidden_high_ready", "hidden_low_ready"))
        s_high, s_low, s_used = (M.sem(n) for n in ("unit_high_ready", "unit_low_ready", "unit_used"))

        def xt(t):
            return X[:, t, :] if t < 2 else XC[:, t - 2, :]

        def colslot(w, c0, n):
            return w.rearrange("(k p) n -> p k n", p=P)[:, :, c0:c0 + n], n

        SLOTS = []
        base = {}
        two_part = set()

        def add(name, items):
            base[name] = len(SLOTS)
            SLOTS.extend(items)

        def rows2(w, s):
            return w.rearrange("(s r p) n -> s p r n", r=2, p=P)[s], 0

        def ada_slots(L):
            return [colslot(I["w_ada"][L], 256 * s, 256) for s in range(ADA_SLOTS)]

        for L in range(2):
            if L == 0:
                add(("ada", 0), ada_slots(0))
            add(("win", L), [colslot(I["w_in"][L], c, n) for c, n in WIN_SLOTS])
            if L == 0:
                add(("ada", 1), ada_slots(1))
            add(("wout", L), [rows2(I["w_out"][L], s) for s in range(4)])
        SITES = [("ffn", 0), ("mix", 0), ("ffn", 1), ("ffn", 2), ("mix", 1), ("ffn", 3)]
        for kind, n in SITES:
            if kind == "ffn":
                add(("ffn", n), [None] * FFN_SLOTS)
            else:
                w = I["w_in_2"][n]
                two_part.update(len(SLOTS) + s for s, ((b0, b1), _, _) in enumerate(MIX_SLOTS) if b1 != b0 + 1)
                add(("win2", n), [colslot(w, P * b0, 256) if b1 == b0 + 1 else ((colslot(w, P * b0, P)[0], colslot(w, P * b1, P)[0]), P) for (b0, b1), _, _ in MIX_SLOTS])
                add(("wout2", n), [rows2(I["w_out_2"][n], s) for s in range(4)])

        UNITS2, unit_base = [], []
        for kind, n in SITES:
            unit_base.append(len(UNITS2))
            if kind == "ffn":
                b0 = base[("ffn", n)]
                for q in range(FFN_PAIRS):
                    m = b0 + 3 * q
                    UNITS2 += [(m, 0, "c"), (m + 1, 0, "c")] + ([(m - 1, 1, "r")] if q else []) + [(m, 1, "c"), (m + 1, 1, "c"), (m + 2, 0, "r")]
                UNITS2.append((b0 + FFN_SLOTS - 1, 1, "r"))
            else:
                UNITS2 += [(base[("win2", n)] + q // 2, q % 2, "c") for q in range(24)] + [(base[("wout2", n)] + q // 2, q % 2, "r") for q in range(8)]
        unit_base.append(len(UNITS2))
        last_unit = {m: U for U, (m, _, _) in enumerate(UNITS2)}

        LAST = {}
        for L in range(2):
            for s in range(ADA_SLOTS):
                LAST[base[("ada", L)] + s] = ("ada_rows", L, s)
            ends = [("q", 1), ("krs",), ("a", 1), ("g", 1), ("f", 1), ("u", 1), ("v", 3 if L == 0 else 1)] + [("gate", 2 * s + 1) for s in range(4)]
            for s, e in enumerate(ends):
                LAST[base[("win", L)] + s] = ("proj", L) + e
            for s in range(4):
                LAST[base[("wout", L)] + s] = ("wout_used", L, s) if s < 3 else ("y_ready", "b1", L, 3 if L == 0 else 1, 1)
        def slot(n):
            return ring[:, n % RING, :]

        def filled(n):
            return slot_loaded[n % RING], 16 * (n // RING + 1 + sum(m <= n and m % RING == n % RING for m in two_part))

        def cols(n, w=256):
            return slot(n)[:, 0:8 * w].rearrange("p (k n) -> p k n", k=8)

        def rows(n):
            return slot(n).rearrange("p (r n) -> p r n", r=2)

        def step(v, j, per):
            return v if j is None else j * per + v

        def y_out(i, t, hf):
            return (s_used, unit_base[i + 1]) if (t, hf) == (1, 1) else at("y_ready", "site", i, t, hf)

        def unit_source(U):
            n, half, kind = UNITS2[U]
            return cols(n)[:, :, half * P:(half + 1) * P] if kind == "c" else rows(n)[:, half, :]

        def unit_in(W, U):
            w = W[:, U % SPLIT, :]
            return w.rearrange("p (k n) -> p k n", k=8) if UNITS2[U][2] == "c" else w

        def at_slot(m, j=None):
            sem, count = filled(m)
            return sem, step(count, j, 16)

        block = ctx.enter_context(nc.Block())

        @block.sync
        def _(sp):
            def fill(n, src, w):
                if n - RING in last_unit:
                    sp.wait_ge(s_low, last_unit[n - RING] + 1)
                elif n >= RING:
                    sp.wait_ge(*at(*LAST[n - RING]))
                if n in two_part:
                    for q in range(2):
                        sp.dma_start(cols(n)[:, :, q * P:(q + 1) * P], src[q]).then_inc(slot_loaded[n % RING], 16)
                    return
                dst = cols(n, w) if w else rows(n)
                sp.dma_start(dst, src).then_inc(slot_loaded[n % RING], 16)

            sp.dma_start(vec[:, 0, :], I["k_vec1"][0]).then_inc(M.sem("vec_loaded"), 16)
            sp.dma_start(vec[:, 1, :], I["k_vec1"][1]).then_inc(M.sem("vec_loaded"), 16)
            sp.dma_start(vec[:, 2, :], I["k_vec2"]).then_inc(M.sem("vec_loaded"), 16)
            sp.dma_start(KB[:, 0:C_DD], I["k_base"][:, 0:C_DD]).then_inc(M.sem("vec_loaded"), 16)
            n_first = base[("ffn", 0)]
            for n in range(n_first):
                fill(n, *SLOTS[n])

            def ffn(idx):
                g = I["w_ffn_gate_2"][idx // 2, idx % 2].rearrange("(k p) (i n) -> i p k n", p=P, n=256)
                u = I["w_ffn_up_2"][idx // 2, idx % 2].rearrange("(k p) (i n) -> i p k n", p=P, n=256)
                d = I["w_ffn_down_2"][idx // 2, idx % 2].rearrange("(i r p) n -> i p r n", r=2, p=P)
                b0 = base[("ffn", idx)]
                for q, src in enumerate((g, u, d)):
                    fill(b0 + q, src[0], 0 if q == 2 else 256)
                with sp.Fori(0, FFN_PAIRS - 1) as j:
                    for q, src in enumerate((g, u, d)):
                        n = b0 + 3 + q
                        sp.wait_ge(s_low, j * 6 + (last_unit[n - RING] + 1))
                        s = src[bass.ds(j + 1, 1)]
                        dst = cols(n) if q < 2 else rows(n)
                        sp.dma_start(dst, s.rearrange("i p a n -> p (i a) n")).then_inc(slot_loaded[n % RING], 16)

            for kind, n in SITES:
                if kind == "ffn":
                    ffn(n)
                else:
                    for s in range(base[("win2", n)], base[("wout2", n)] + 4):
                        fill(s, *SLOTS[s])
            for t in range(2):
                sp.wait_ge(*at("x_updated", "site", 5, t, 1))
                sp.dma_start(out[0].rearrange("(t p) d -> t p d", p=P)[t], X[:, t, :]).then_inc(M.sem("stored"), 16)
            sp.wait_ge(M.sem("stored"), 32)

        SW = 7 * 16

        @block.gpsimd
        def _(pool):
            def load(dst, src, stage):
                pool.dma_start(dst, src).then_inc(M.sem(stage), 16)

            pool.memset(eps[:, 0:1], RMS_EPS)
            pool.memset(eps[:, 1:2], LN_EPS)
            pool.memset(eps[:, 2:3], RMS_EPS * QK)
            pool.memset(eps[:, 3:4], 0.0)
            pool.memset(CG, 0.0).then_inc(*done("set_up"))
            load(KB[:, C_DD:], I["k_base"][:, C_DD:], "base_loaded")
            load(lam_in[:, :, :], I["diff_lambda_2"].rearrange("l a b -> (l a b)").rearrange("(l n) -> l n", l=2).partition_broadcast(P), "base_loaded")
            load(bsrow, I["b_s"].rearrange("l g n -> (l g n)").rearrange("(a l n) -> a l n", a=1, l=2), "base_loaded")

            def small_weights(L):
                load(w_uq, I["w_uq"][L].rearrange("(j p) n -> p j n", p=P), "small_loaded")
                load(w_ukv, I["w_ukv"][L], "small_loaded")
                load(w_pw, I["w_pw"][L].rearrange("(j p) n -> p j n", p=P), "small_loaded")
                load(w_fo, I["w_fourier"][L].rearrange("(j p) n -> p j n", p=P), "small_loaded")
                load(w_s, I["w_s"][L].rearrange("g i j -> i g j"), "small_loaded")
                load(sgu_row[:, 0, :], I["sgu_ln_g"][L].partition_broadcast(P), "small_loaded")
                load(sgu_row[:, 1, :], I["sgu_ln_b"][L].partition_broadcast(P), "small_loaded")

            def layer(L):
                nq = TT if L == 0 else T
                if L:
                    pool.wait_ge(*at("conv_out", 0, 1))
                small_weights(L)
                pool.wait_ge(M.sem("small_loaded"), SW * (L + 1))
                for j in range(2):
                    for half in range(2):
                        src = w_uq[:, j, :].rearrange("p (h n) -> p h n", h=4)[:, :, NOPE:QK].rearrange("p h (a x f) -> p h a x f", a=2, x=2)[:, :, :, 1 - half, :]
                        dst = w_uqs[:, j, :].rearrange("p (h a x f) -> p h a x f", h=4, a=2, x=2)[:, :, :, half, :]
                        last = pool.tensor_copy(dst, src)
                last.then_inc(*done("uq_swapped", L))
                n = base[("win", L)] + 1
                pool.wait_ge(*filled(n))
                for half in range(2):
                    src = cols(n, 160)[:, :, P:P + ROPE].rearrange("p k (a x f) -> p k a x f", a=2, x=2)[:, :, :, 1 - half, :]
                    dst = w_krs.rearrange("p k (a x f) -> p k a x f", a=2, x=2)[:, :, :, half, :]
                    last = pool.tensor_copy(dst, src)
                last.then_inc(*done("kr_swapped", L))
                for j in range(2):
                    pool.wait_ge(*at("a_ready", L, j))
                    pool.wait_ge(*at("conv_gate_ready", L, j))
                    for s in range(nq // T):
                        last = pool.tensor_tensor(CG[:, j, s, PAD:PAD + T], CG[:, j, s, PAD:PAD + T], csg[:, j, s * T:(s + 1) * T], ALU.mult)
                    last.then_inc(*done("glu_ready", L, j))
                for t in range(nq // P):
                    pool.wait_ge(*at("v_normalised", L, t))
                    pool.tensor_tensor(VN[:, t, :], VN[:, t, :], sgu_row[:, 0, :], ALU.mult).then_inc(*done("v_gained", L, t))
                    pool.wait_ge(*at("v_gained", L, t))
                    pool.tensor_tensor(VN[:, t, :], VN[:, t, :], sgu_row[:, 1, :], ALU.add).then_inc(*done("v_ready", L, t))
                for m in range(2):
                    pool.wait_ge(*at("u_ready", L, m))
                    pool.wait_ge(*at("sg_ready", L, 6 + m))
                    pool.tensor_tensor(U[:, m, 0:nq], U[:, m, 0:nq], SG[:, 6 + m, 0:nq], ALU.mult).then_inc(*done("u_gated", L, m))
                pool.wait_ge(*at("u_gated", L, 1))
                pool.wait_ge(*at("kr_ready", L))
                pool.wait_ge(*at("fourier_tok", L, 1))
                for h in range(HEADS):
                    last = pool.tensor_copy(K[NOPE:QK, h, :], krot[NOPE:QK, :])
                last.then_inc(*done("k_rope_ready", L))
                pool.wait_ge(*at("k_rope_ready", L))
                for t in range(nq // P):
                    for n in range(2):
                        pool.wait_ge(*at("out_scaled", "b1", L, t, n))
                        x = xt(t)[:, n * 512:(n + 1) * 512]
                        pool.tensor_tensor(x, x, ytmp[:, n, :], ALU.add).then_inc(*done("x_updated", "b1", L, t, n))

            layer(0)
            layer(1)
            pool.wait_ge(*at("final_scaled", 1))
            load(gain_row[:, :], I["norm_gains_2"][0, 1].partition_broadcast(P), "gain_loaded")
            pool.wait_ge(*at("conv_out", 1, 1))
            load(alibi[:, :, :].rearrange("p h n -> p (h n)"), I["k_alibi"], "alibi_loaded")
            for i, (kind, n) in enumerate(SITES):
                if kind == "mix":
                    pool.wait_ge(M.sem("base_loaded"), 48)
                    for h in range(N_SB):
                        pool.wait_ge(*at("softplus_ready", n, h))
                        pool.tensor_tensor(ZP[:, h, :], ZP[:, h, :], full, ALU.mult).then_inc(*done("softplus_masked", n, h))
                for t in range(2):
                    for hf in range(2):
                        pool.wait_ge(*at("out_scaled", "site", i, t, hf))
                        pool.tensor_tensor(X[:, t, hf * 512:(hf + 1) * 512], X[:, t, hf * 512:(hf + 1) * 512], ytmp[:, hf, :], ALU.add).then_inc(*done("x_updated", "site", i, t, hf))
                if i < 5:
                    nxt = i + 1
                    load(gain_row[:, :], I["norm_gains_2"][nxt // 3, 2 * (nxt % 3) + 1].partition_broadcast(P), "gain_loaded")

        @block.scalar
        def _(act):
            A = act.activation
            for t in range(2):
                act.dma_start(X[:, t, :], I["x"][0].rearrange("(t p) d -> t p d", p=P)[t]).then_inc(M.sem("x_loaded"), 16)
            for t in range(2):
                act.dma_start(XC[:, t, :], I["ctx"][0].rearrange("(t p) d -> t p d", p=P)[t]).then_inc(M.sem("x_loaded"), 16)
            act.dma_start(gain_row[:, :], I["final_g"].partition_broadcast(P)).then_inc(M.sem("final_loaded"), 16)
            act.wait_ge(*at("vec_T", 0))
            A(CS[:, :], vT[:, 0, R_C:R_C + 16], ACT.Silu).then_inc(*done("silu_c"))
            act.wait_ge(M.sem("x_loaded"), 64)
            act.wait_ge(*at("set_up"))

            def ada_copy(L, s):
                act.wait_ge(*at("ada_rows", L, s))
                A(ada_row[ADA_AT[s % 2], :], B[6][ADA_AT[s % 2], 0:T], ACT.Copy).then_inc(*done("ada_copied", L, s))

            def norm(site, tiles):
                for t in tiles:
                    if site == ("b1", 1):
                        for hf in range(2):
                            act.wait_ge(*at("x_updated", "b1", 0, t, hf))
                    A(XN[:, t, :], xt(t), ACT.Square, accum_out=stat[:, t:t + 1]).then_inc(*done("sum_squares", *site, t))
                act.wait_ge(*at("sum_squares", *site, tiles[-1]))
                act.wait_ge(*at("set_up"))
                A(stat[:, 8:8 + len(tiles)], stat[:, 0:len(tiles)], ACT.Sqrt, bias=eps[:, 0:1], scale=1.0 / D).then_inc(*done("rms_ready", *site))

            def layer(L):
                nq = TT if L == 0 else T
                norm(("b1", L), range(4))
                if L == 0:
                    for s in range(ADA_SLOTS):
                        ada_copy(0, s)
                for c in range(0, KD, 2):
                    act.wait_ge(*at("x_T", "b1", L, c))
                    act.wait_ge(*at("ada_ready", L))
                    A(hT[:, c, 0:T], B[c % 4][:, 0:T], ACT.Identity, scale=adag[:, c, 0:1], bias=ada[:, c, 0:1])
                    A(hT[:, c, T:TT], B[c % 4][:, T:TT], ACT.Identity, scale=adag[:, c, 1:2], bias=ada[:, c, 1:2]).then_inc(*done("hT_ready_act", "b1", L, c))
                for j in range(2):
                    act.wait_ge(*at("proj", L, "q", j))
                    A(qp[:, j, 0:nq], B[PB[L]["q", j]][:, 0:nq], ACT.Copy)
                    A(sq[:, j, 0:nq], B[PB[L]["q", j]][:, 0:nq], ACT.Square).then_inc(*done("q_part_ready", L, j))
                act.wait_ge(*at("proj", L, "kv"))
                A(kvp, B[PB[L]["kv"]][:, :], ACT.Copy)
                A(sq[:, 2, :], B[PB[L]["kv"]][:, :], ACT.Square).then_inc(*done("kv_part_ready", L))
                for j in range(2):
                    act.wait_ge(*at("proj", L, "a", j))
                    if L:
                        act.wait_ge(*at("conv_tap", L - 1, j, CONV_K - 1))
                    else:
                        act.wait_ge(*at("set_up"))
                    src = B[PB[L]["a", j]][:, 0:nq].rearrange("p (s n) -> p s n", n=T)
                    A(CG[:, j, 0:nq // T, PAD:PAD + T], src, ACT.Copy).then_inc(*done("a_ready", L, j))
                act.wait_ge(*at("q_square_sum", L))
                A(rq[:, 0, 0:nq], B[6][:, 0:nq], ACT.Sqrt, bias=eps[:, 2:3], scale=float(QK) / 256).then_inc(*done("q_root", L))
                act.wait_ge(*at("kv_square_sum", L))
                A(rq[:, 1, :], B[7][:, :], ACT.Sqrt, bias=eps[:, 0:1], scale=1.0 / 128).then_inc(*done("kv_root", L))
                for j in range(2):
                    act.wait_ge(*at("proj", L, "g", j))
                    A(csg[:, j, 0:nq], B[PB[L]["g", j]][:, 0:nq], ACT.Sigmoid).then_inc(*done("conv_gate_ready", L, j))
                for j in range(2):
                    act.wait_ge(*at("proj", L, "f", j))
                    A(fT[:, j, 0:nq], B[PB[L]["f", j]][:, 0:nq], ACT.Copy).then_inc(*done("f_ready", L, j))
                for j in range(2):
                    act.wait_ge(*at("proj", L, "u", j))
                    A(U[:, j, 0:nq], B[PB[L]["u", j]][:, 0:nq], ACT.Copy).then_inc(*done("u_ready", L, j))
                act.wait_ge(*at("v_aggr", L, nq // P - 1))
                A(stat[:, 40:40 + nq // P], stat[:, 33:33 + 2 * (nq // P):2], ACT.Sqrt, bias=eps[:, 1:2]).then_inc(*done("v_root", L))
                for j in range(8):
                    act.wait_ge(*at("proj", L, "gate", j))
                    A(SG[:, j, 0:nq], B[PB[L]["gate", j]][:, 0:nq], ACT.Silu).then_inc(*done("sg_ready", L, j))
                for v in range(nq // T):
                    for hf in range(2):
                        act.wait_ge(*at("gate_rows", L, v, hf))
                        A(GB[:, v, hf * 512:(hf + 1) * 512], B[(2 * v + hf) % 4][:, :], ACT.Copy).then_inc(*done("gate_row_ready", L, v, hf))
                for h in range(HEADS):
                    act.wait_ge(*at("q_heads", L, h))
                    act.wait_ge(*at("glu_ready", L, 1))
                    A(Q[0:NOPE, h, 0:nq], B[h % 2][0:NOPE, 0:nq], ACT.Copy)
                    if L == 0:
                        A(Q[NOPE:QK, h, T:TT], B[h % 2][NOPE:QK, T:TT], ACT.Copy)
                    A(csg[NOPE:QK, h // 2, (h % 2) * T:(h % 2 + 1) * T], B[h % 2][NOPE:QK, 0:T], ACT.Copy).then_inc(*done("q_copied", L, h))
                for h in range(HEADS):
                    act.wait_ge(*at("k_heads", L, h))
                    act.wait_ge(*at("fourier_tok", L, 1))
                    A(K[0:NOPE, h, :], B[h % 2][0:NOPE, :], ACT.Copy).then_inc(*done("k_copied", L, h))
                def weights(i):
                    seg, h, par = UNITS[i] + (i % 2,)
                    keys = TT if seg == 0 else T
                    for qt in range(2):
                        act.wait_ge(*at("neg_max", L, seg, h, qt))
                        A(Pm[par][:, qt, 0:keys], B[qt][:, 0:keys], ACT.Exp, bias=stat[:, 16 + 2 * par + qt:17 + 2 * par + qt], accum_out=stat[:, 20 + 2 * par + qt:21 + 2 * par + qt]).then_inc(*done("exp_ready", L, seg, h, qt))

                def transposed(i):
                    seg, h, par = UNITS[i] + (i % 2,)
                    keys = TT if seg == 0 else T
                    for qt in range(2):
                        act.wait_ge(*at("p_T", L, seg, h, qt))
                        A(PT[par][:, 0:keys // P, qt * P:(qt + 1) * P], B[2 + qt][:, 0:keys].rearrange("p (k n) -> p k n", n=P), ACT.Copy).then_inc(*done("pT_ready", L, seg, h, qt))

                UNITS = [(seg, h) for seg in range(nq // T) for h in range(HEADS)]
                weights(0)
                for i in range(len(UNITS)):
                    if i + 1 < len(UNITS):
                        weights(i + 1)
                    if L == 0:
                        for sl in ADA_STEP[i]:
                            ada_copy(1, sl)
                    transposed(i)
                for j in range(2):
                    act.wait_ge(*at("conv_centred", L, j))
                    A(sq[:, j, 0:nq], cacc[:, j, 0:nq], ACT.Square).then_inc(*done("conv_square", L, j))
                act.wait_ge(*at("conv_var", L))
                A(rq[:, 0, 0:nq], B[1][:, 0:nq], ACT.Sqrt, bias=eps[:, 1:2], scale=1.0 / 256).then_inc(*done("conv_root", L))
                for j in range(2):
                    act.wait_ge(*at("conv_normalised", L, j))
                    A(csg[:, j, 0:nq], cacc[:, j, 0:nq], ACT.Silu, scale=vT[:, L, R_CLG + j:R_CLG + j + 1], bias=vT[:, L, R_CLB + j:R_CLB + j + 1]).then_inc(*done("conv_act", L, j))

            layer(0)
            layer(1)
            for t in range(2):
                for hf in range(2):
                    act.wait_ge(*at("x_updated", "b1", 1, t, hf))
                A(XN2[:, t, :], X[:, t, :], ACT.Square, accum_out=stat[:, t:t + 1]).then_inc(*done("final_squares", t))
            act.wait_ge(*at("final_squares", 1))
            A(stat[:, 8:10], stat[:, 0:2], ACT.Sqrt, bias=eps[:, 0:1], scale=1.0 / D).then_inc(*done("final_root"))

            def high(U, j=None):
                act.wait_ge(*at_slot(UNITS2[U][0], j))
                if U >= SPLIT:
                    act.wait_ge(s_used, step(U - SPLIT + 1, j, 6))
                A(unit_in(WH, U), unit_source(U), ACT.Copy).then_inc(s_high, 1)

            def site_norm(i):
                for t in range(2):
                    if i == 0:
                        act.wait_ge(*at("final_scaled", t))
                    else:
                        for hf in range(2):
                            act.wait_ge(*at("x_updated", "site", i - 1, t, hf))
                    A(XN2[:, t, :], X[:, t, :], ACT.Square, accum_out=stat[:, t:t + 1]).then_inc(*done("sum_squares", "site", i, t))
                act.wait_ge(*at("sum_squares", "site", i, 1))
                A(stat[:, 8:10], stat[:, 0:2], ACT.Sqrt, bias=eps[:, 0:1], scale=1.0 / D).then_inc(*done("rms_ready", "site", i))
                for b in range(4):
                    act.wait_ge(*at("x_T", "site", i, b))
                    for q in range(2):
                        c = 2 * b + q
                        r = 8 * i + c
                        last = A(HH[:, c, :], B[b][:, q * T:(q + 1) * T], ACT.Identity, scale=vT[:, 2, r:r + 1])
                    last.then_inc(*done("input_high", i, b))

            def site_tail(i):
                for t in range(2):
                    for hf in range(2):
                        act.wait_ge(*y_out(i, t, hf))
                        A(XN2[:, hf, 0:512], B[4 + 2 * t + hf][:, :], ACT.Square, accum_out=stat[:, 10 + 2 * t + hf:11 + 2 * t + hf]).then_inc(*done("y_squares", i, t, hf))
                    act.wait_ge(*at("y_scale", "sum", i, t))
                    A(stat[:, 28 + t:29 + t], stat[:, 26 + t:27 + t], ACT.Sqrt, bias=eps[:, 0:1], scale=1.0 / D).then_inc(*done("y_root", i, t))

            def ffn(i, n):
                f0 = n * FFN_CHUNKS

                def silu(par, ready, free):
                    act.wait_ge(s_used, ready)
                    if free is not None:
                        act.wait_ge(s_h, free)
                    A(sgate[:, par, :], B[par][:, 0:T], ACT.Silu).then_inc(s_silu, 1)

                def hidden_high(par, ready, used, j=None):
                    act.wait_ge(s_h, ready)
                    if used is not None:
                        act.wait_ge(s_used, step(used + 1, j, 6))
                    A(HBH[:, par, :], hbuf[:, par, :], ACT.Copy).then_inc(s_hh, 1)

                a = unit_base[i]
                silu(0, a + 2, f0 if n else None)
                high(a + 6)
                hidden_high(0, f0 + 1, None)
                high(a + 7)
                silu(1, a + 4, f0 if n else None)
                high(a + 8)
                hidden_high(1, f0 + 2, None)
                high(a + 9)
                high(a + 10)

                def pair(a, f, j=None):
                    split = [U for U in range(a + 6, a + 12) if U < len(UNITS2)]
                    silu(0, step(a + 2, j, 6), step(f - 1, j, 2))
                    if split:
                        high(split[0], j)
                    hidden_high(0, step(f + 1, j, 2), a - 1, j)
                    for U in split[1:3]:
                        high(U, j)
                    silu(1, step(a + 5, j, 6), step(f, j, 2))
                    for U in split[3:4]:
                        high(U, j)
                    hidden_high(1, step(f + 2, j, 2), a + 2, j)
                    for U in split[4:]:
                        high(U, j)

                with act.Fori(0, FFN_PAIRS - 2) as j:
                    pair(a + 5, f0 + 2, j)
                pair(a + 5 + 6 * (FFN_PAIRS - 2), f0 + FFN_CHUNKS - 2)

            def mix(i, n):
                u0 = unit_base[i]
                for s, (_, kind, blocks) in enumerate(MIX_SLOTS):
                    for q, b in enumerate(blocks):
                        if kind == "qk" and b % 2 == 0:
                            act.wait_ge(s_used, u0 + 2 * s + q + 1)
                            A(FQ[:, b, :], B[PB2["qk", b]][:, 0:T], ACT.Copy, scale=QKSC[b]).then_inc(*done("qk_ready_act", n, b))
                        high(u0 + 2 * s + q + SPLIT)
                for u in range(N_DIL + 2 * N_DIFF):
                    act.wait_ge(*at("neg_max2", n, u))
                    for qt, (a, w) in enumerate(((0, P), (P, T))):
                        last = A(SS[:, u % 4, a:a + w], S2[:, u % 2, a:a + w], ACT.Exp, scale=-1.0, bias=stat[:, 16 + 2 * (u % 2) + qt:17 + 2 * (u % 2) + qt], accum_out=stat[:, 20 + 2 * (u % 2) + qt:21 + 2 * (u % 2) + qt])
                    last.then_inc(*done("exp2_ready", n, u))
                    h = UNIT_HEAD[u]
                    if h is not None:
                        act.wait_ge(*at("p2_T", n, h))
                        A(PT2[:, h % 2, :], B[2 + h % 2][:, 0:384], ACT.Copy).then_inc(*done("pT2_ready", n, h))
                for b in range(2):
                    act.wait_ge(*at("ob_ready", n, b))
                    A(sgate[:, b, :], OB2[:, b, :], ACT.Square).then_inc(*done("ob_square", n, b))
                    act.wait_ge(*at("ob_sum", n, b))
                    A(sgate[:, b, :], B[4 + b][:, T:TT], ACT.Sqrt, bias=eps[:, 0:1]).then_inc(*done("ob_root", n, b))
                for h in range(N_SB):
                    act.wait_ge(*at("z_ready", n, h))
                    A(ZE[:, h, :], B[h][:, 0:384], ACT.Abs).then_inc(*done("z_abs", n, h))
                for h in range(N_SB):
                    act.wait_ge(*at("z_abs", n, h))
                    A(ZE[:, h, :], ZE[:, h, :], ACT.Exp, scale=-1.0).then_inc(*done("z_exp", n, h))
                for h in range(N_SB):
                    act.wait_ge(*at("z_exp", n, h))
                    A(ZE[:, h, :], ZE[:, h, :], ACT.Ln, bias=1.0).then_inc(*done("z_ln", n, h))
                for h in range(N_SB):
                    act.wait_ge(*at("log_weight", n, h))
                    A(ZP[:, h, :], ZE[:, h, :], ACT.Exp).then_inc(*done("weight_ready", n, h))
                for U in range(u0 + 24, u0 + 31):
                    high(U + SPLIT)

            for unit in range(SPLIT):
                high(unit)
            for m in range(2):
                act.wait_ge(*at("lambda_sums", m))
                A(lamv[:, m, 2:4], lamv[:, m, 0:2], ACT.Exp).then_inc(*done("lambda_exp", m))
            for i, (kind, n) in enumerate(SITES):
                site_norm(i)
                (ffn if kind == "ffn" else mix)(i, n)
                site_tail(i)
                if i < 5:
                    high(unit_base[i + 1] + SPLIT - 1)

        @block.vector
        def _(dve):
            TS, STT, TTn, CP = dve.tensor_scalar, dve.scalar_tensor_tensor, dve.tensor_tensor, dve.tensor_copy
            dve.wait_ge(*at("vec_transposed"))
            CP(vT[:, :, :], B[0][:, 0:384].rearrange("p (b n) -> p b n", b=3)).then_inc(*done("vec_T", 0))

            def scale_rows(site, tiles):
                dve.wait_ge(*at("rms_ready", *site))
                dve.reciprocal(stat[:, 12:12 + len(tiles)], stat[:, 8:8 + len(tiles)]).then_inc(*done("inverse", "rms", *site))
                dve.wait_ge(*at("inverse", "rms", *site))
                for t in tiles:
                    TS(XN[:, t, :] if site[0] == "b1" else XN2[:, t, :], xt(t), stat[:, 12 + t:13 + t], None, ALU.mult).then_inc(*done("x_scaled", *site, t))

            def modulation(L):
                dve.wait_ge(*at("ada_T", L, ADA_SLOTS - 1))
                TTn(ada[:, :, :], B[7][:, 0:48].rearrange("p (b v) -> p b v", v=2), vT[:, L, 0:24].unsqueeze(2).to_broadcast([P, 24, 2]), ALU.add).then_inc(*done("ada_biased", L))
                dve.wait_ge(*at("ada_biased", L))
                STT(adag[:, :, :], ada[:, 8:16, :], 1.0, vT[:, L, R_NORM:R_NORM + 8].unsqueeze(2).to_broadcast([P, 8, 2]), ALU.add, ALU.mult).then_inc(*done("ada_ready", L))

            def layer(L):
                nq = TT if L == 0 else T
                nt = nq // P
                scale_rows(("b1", L), range(4))
                if L == 0:
                    modulation(0)
                dve.wait_ge(*at("ada_ready", L))
                for c in range(1, KD, 2):
                    dve.wait_ge(*at("x_T", "b1", L, c))
                    TS(hT[:, c, 0:T], B[c % 4][:, 0:T], adag[:, c, 0:1], ada[:, c, 0:1], ALU.mult, ALU.add)
                    TS(hT[:, c, T:TT], B[c % 4][:, T:TT], adag[:, c, 1:2], ada[:, c, 1:2], ALU.mult, ALU.add).then_inc(*done("hT_ready_dve", "b1", L, c))
                dve.wait_ge(*at("ws_transposed", L))
                CP(wsT, B[5][:, :].rearrange("p (g n) -> p g n", g=4)).then_inc(*done("wsT_ready", L))
                dve.wait_ge(*at("proj", L, "kr"))
                dve.wait_ge(M.sem("base_loaded"), 48)
                TTn(krot[NOPE:QK, 0:T], B[PB[L]["kr"]][NOPE:QK, 0:T], rcos, ALU.mult).then_inc(*done("kr_cos", L))
                CP(krot[NOPE:QK, T:TT], B[PB[L]["kr"]][NOPE:QK, T:TT]).then_inc(*done("kr_copied", L))
                dve.wait_ge(*at("proj", L, "krs"))
                TTn(ropet[NOPE:QK, 0:T], B[PB[L]["krs"]][NOPE:QK, 0:T], rsin, ALU.mult).then_inc(*done("kr_sin", L))
                dve.wait_ge(*at("kr_cos", L))
                dve.wait_ge(*at("kr_sin", L))
                TTn(krot[NOPE:QK, 0:T], krot[NOPE:QK, 0:T], ropet[NOPE:QK, 0:T], ALU.add).then_inc(*done("kr_ready", L))
                dve.wait_ge(*at("q_root", L))
                dve.reciprocal(rq[:, 0, 0:nq], rq[:, 0, 0:nq]).then_inc(*done("inverse", "q", L))
                dve.wait_ge(*at("kv_root", L))
                dve.reciprocal(rq[:, 1, :], rq[:, 1, :]).then_inc(*done("inverse", "kv", L))
                dve.wait_ge(*at("inverse", "q", L))
                for j in range(2):
                    dve.wait_ge(*at("q_part_ready", L, j))
                    STT(qp[:, j, 0:nq], qp[:, j, 0:nq], vT[:, L, R_QN + j:R_QN + j + 1], rq[:, 0, 0:nq], ALU.mult, ALU.mult).then_inc(*done("q_latent", L, j))
                dve.wait_ge(*at("inverse", "kv", L))
                STT(kvp, kvp, vT[:, L, R_KVN:R_KVN + 1], rq[:, 1, :], ALU.mult, ALU.mult).then_inc(*done("kv_latent", L))
                for t in range(nt):
                    dve.wait_ge(*at("fourier_feat", L, t))
                    CP(FA[:, t, :, :], B[6 + t % 2][:, :].rearrange("p (j n) -> p j n", j=2)).then_inc(*done("fa_ready", L, t))
                for t in range(nt):
                    dve.wait_ge(*at("proj", L, "v", t))
                    dve.bn_stats(stat[:, 44:50], B[PB[L]["v", t]][:, 0:256]).then_inc(*done("v_bn", L, t))
                    CP(VN[:, t, :], B[PB[L]["v", t]][:, 0:256]).then_inc(*done("v_copied", L, t))
                    dve.wait_ge(*at("v_bn", L, t))
                    dve.bn_aggr(stat[:, 32 + 2 * t:34 + 2 * t], stat[:, 44:50]).then_inc(*done("v_aggr", L, t))
                    dve.wait_ge(*at("v_aggr", L, t))
                for m in range(2):
                    dve.wait_ge(*at("fourier_tok", L, m))
                    CP(cacc[:, m, 0:nq], B[6 + m][:, 0:nq]).then_inc(*done("f_mixed", L, m))
                dve.wait_ge(*at("v_root", L))
                dve.reciprocal(stat[:, 40:40 + nt], stat[:, 40:40 + nt]).then_inc(*done("inverse", "v", L))
                dve.wait_ge(*at("inverse", "v", L))
                for t in range(nt):
                    dve.wait_ge(*at("v_copied", L, t))
                    TS(VN[:, t, :], VN[:, t, :], stat[:, 32 + 2 * t:33 + 2 * t], stat[:, 40 + t:41 + t], ALU.subtract, ALU.mult).then_inc(*done("v_normalised", L, t))
                for m in range(2):
                    dve.wait_ge(*at("fourier_out", L, m))
                    dve.wait_ge(*at("sg_ready", L, 4 + m))
                    STT(SG[:, 4 + m, 0:nq], B[4 + m][:, 0:nq], vT[:, L, R_BF + m:R_BF + m + 1], SG[:, 4 + m, 0:nq], ALU.add, ALU.mult).then_inc(*done("four_branch", L, m))
                for m in range(2):
                    dve.wait_ge(*at("sgu_mixed", L, m))
                    dve.wait_ge(*at("u_gated", L, m))
                    TTn(SG[:, 6 + m, 0:nq], B[6 + m][:, 0:nq], U[:, m, 0:nq], ALU.mult).then_inc(*done("sgu_branch", L, m))
                for v in range(nq // T):
                    for hf in range(2):
                        if v:
                            dve.wait_ge(*at("gate_rows", L, v - 1, hf))
                        elif L:
                            dve.wait_ge(*at("gate_rows", 0, 1, hf))
                        for c in range(4):
                            last = TS(gate_diag[:, hf, c * P:(c + 1) * P], ident, ada[:, 16 + 4 * hf + c, v:v + 1], None, ALU.mult)
                        last.then_inc(*done("gate_diag_ready", L, v, hf))
                for h in range(HEADS):
                    dve.wait_ge(*at("q_copied", L, h))
                    qc = csg[NOPE:QK, h // 2, (h % 2) * T:(h % 2 + 1) * T]
                    TTn(Q[NOPE:QK, h, 0:T], qc, rcos, ALU.mult).then_inc(*done("q_cos", L, h))
                    dve.wait_ge(*at("q_swapped", L, h))
                    TTn(ropet[NOPE:QK, (h % 2) * T:(h % 2 + 1) * T], B[2 + h % 2][NOPE:QK, 0:T], rsin, ALU.mult).then_inc(*done("q_sin", L, h))
                    dve.wait_ge(*at("q_sin", L, h))
                    dve.wait_ge(*at("q_cos", L, h))
                    TTn(Q[NOPE:QK, h, 0:T], Q[NOPE:QK, h, 0:T], ropet[NOPE:QK, (h % 2) * T:(h % 2 + 1) * T], ALU.add).then_inc(*done("q_ready", L, h))
                for t in range(4):
                    dve.wait_ge(*at("v_heads", L, t))
                    CP(V[:, t, :], B[4 + t][:, 0:256]).then_inc(*done("v_heads_ready", L, t))
                conv = conv_steps(L)
                UNITS = [(seg, h) for seg in range(nq // T) for h in range(HEADS)]

                def row_max(i):
                    seg, h, par = UNITS[i] + (i % 2,)
                    for qt in range(2):
                        dve.wait_ge(*at("scores", L, seg, h, qt))
                        dve.reduce_max(stat[:, 16 + 2 * par + qt:17 + 2 * par + qt], B[qt][:, 0:TT if seg == 0 else T], AXX, negate=True).then_inc(*done("neg_max", L, seg, h, qt))

                def row_scale(i):
                    seg, h, par = UNITS[i] + (i % 2,)
                    keys = TT if seg == 0 else T
                    for qt in range(2):
                        dve.wait_ge(*at("exp_ready", L, seg, h, qt))
                    dve.reciprocal(stat[:, 24 + 2 * par:26 + 2 * par], stat[:, 20 + 2 * par:22 + 2 * par]).then_inc(*done("inverse", "p", L, seg, h))
                    dve.wait_ge(*at("inverse", "p", L, seg, h))
                    for qt in range(2):
                        TS(Pm[par][:, qt, 0:keys], Pm[par][:, qt, 0:keys], stat[:, 24 + 2 * par + qt:25 + 2 * par + qt], None, ALU.mult).then_inc(*done("p_ready", L, seg, h, qt))

                def gated_heads(i):
                    seg, h = UNITS[i]
                    if h % 2:
                        dve.wait_ge(*at("attn", L, seg, h))
                        sl = SG[:, h // 2, seg * T:(seg + 1) * T]
                        TTn(sl, B[4 + h // 2][:, 0:T], sl, ALU.mult).then_inc(*done("attn_ready", L, h, seg))

                row_max(0)
                for i in range(len(UNITS)):
                    row_scale(i)
                    if i + 1 < len(UNITS):
                        row_max(i + 1)
                    if i:
                        gated_heads(i - 1)
                    for _ in range(4 if L == 0 else 8):
                        next(conv, None)
                gated_heads(len(UNITS) - 1)
                for _ in conv:
                    pass
                if L == 0:
                    modulation(1)
                dve.wait_ge(*at("conv_mean", L))
                for j in range(2):
                    dve.wait_ge(*at("conv_tap", L, j, CONV_K - 1))
                    STT(cacc[:, j, 0:nq], B[0][:, 0:nq], -1.0 / 256, cacc[:, j, 0:nq], ALU.mult, ALU.add).then_inc(*done("conv_centred", L, j))
                dve.wait_ge(*at("conv_root", L))
                dve.reciprocal(rq[:, 0, 0:nq], rq[:, 0, 0:nq]).then_inc(*done("inverse", "conv", L))
                dve.wait_ge(*at("inverse", "conv", L))
                for j in range(2):
                    dve.wait_ge(*at("conv_square", L, j))
                    dve.wait_ge(*at("conv_centred", L, j))
                    TTn(cacc[:, j, 0:nq], cacc[:, j, 0:nq], rq[:, 0, 0:nq], ALU.mult).then_inc(*done("conv_normalised", L, j))
                for m in range(2):
                    dve.wait_ge(*at("conv_out", L, m))
                    STT(SG[:, 2 + m, 0:nq], B[2 + m][:, 0:nq], vT[:, L, R_BPW + m:R_BPW + m + 1], SG[:, 2 + m, 0:nq], ALU.add, ALU.mult).then_inc(*done("conv_branch", L, m))
                for t in range(nt):
                    for hf in range(2):
                        dve.wait_ge(*at("y_ready", "b1", L, t, hf))
                        dve.wait_ge(*at("gate_row_ready", L, t // 2, hf))
                        if t:
                            dve.wait_ge(*at("x_updated", "b1", L, t - 1, hf))
                        elif L:
                            dve.wait_ge(*at("x_updated", "b1", 0, 3, hf))
                        TTn(ytmp[:, hf, :], B[YB[L][t, hf]][:, :], GB[:, t // 2, hf * 512:(hf + 1) * 512], ALU.mult).then_inc(*done("out_scaled", "b1", L, t, hf))

            def conv_steps(L):
                nseg = 2 if L == 0 else 1
                for k in range(CONV_K):
                    for j in range(2):
                        accv = cacc[:, j, 0:nseg * T].rearrange("p (s n) -> p s n", n=T)
                        src = CG[:, j, 0:nseg, k:k + T]
                        w = vT[:, L, R_CW + 2 * k + j:R_CW + 2 * k + j + 1]
                        if k == 0:
                            dve.wait_ge(*at("glu_ready", L, j))
                            dve.wait_ge(*at("fourier_out", L, 1))
                            TS(accv, src, w, vT[:, L, R_CB + j:R_CB + j + 1], ALU.mult, ALU.add).then_inc(*done("conv_tap", L, j, k))
                        else:
                            dve.wait_ge(*at("conv_tap", L, j, k - 1))
                            STT(accv, src, w, accv, ALU.mult, ALU.add).then_inc(*done("conv_tap", L, j, k))
                    yield

            def low(U, j=None):
                dve.wait_ge(s_high, step(U + 1, j, 6))
                TTn(unit_in(WL, U), unit_source(U), unit_in(WH, U).bitcast(F32), ALU.subtract).then_inc(s_low, 1)

            layer(0)
            layer(1)
            dve.wait_ge(*at("final_root"))
            dve.reciprocal(stat[:, 12:14], stat[:, 8:10]).then_inc(*done("inverse", "final"))
            dve.wait_ge(*at("inverse", "final"))
            dve.wait_ge(M.sem("final_loaded"), 16)
            for t in range(2):
                STT(X[:, t, :], X[:, t, :], stat[:, 12 + t:13 + t], gain_row[:, :], ALU.mult, ALU.mult).then_inc(*done("final_scaled", t))
            for unit in range(SPLIT):
                low(unit)
            dve.wait_ge(M.sem("base_loaded"), 48)
            for m in range(2):
                for q in range(2):
                    last = dve.tensor_tensor_reduce(out=S2[:, m, q * 32:q * 32 + 32], in0=lam_in[:, m, q * 64:q * 64 + 32], in1=lam_in[:, m, q * 64 + 32:q * 64 + 64], scale=1.0, scalar=0.0, op0=ALU.mult, op1=ALU.add, accum_out=lamv[:, m, q:q + 1])
                last.then_inc(*done("lambda_sums", m))
            for m in range(2):
                init = LAM_INIT[m]
                dve.wait_ge(*at("lambda_exp", m))
                STT(lamv[:, m, 4:5], lamv[:, m, 3:4], init, lamv[:, m, 2:3], ALU.subtract, ALU.subtract).then_inc(*done("lambda_ready", m))
                TS(lamv[:, m, 5:6], vT[:, 2, R_SUB + m:R_SUB + m + 1], 1.0 - init, None, ALU.mult).then_inc(*done("sub_gain", m))

            def site_norm(i):
                if i == 0:
                    dve.wait_ge(*at("final_scaled", 1))
                scale_rows(("site", i), range(2))
                for b in range(4):
                    dve.wait_ge(*at("input_high", i, b))
                    for q in range(2):
                        c = 2 * b + q
                        r = 8 * i + c
                        last = STT(HL[:, c, :], B[b][:, q * T:(q + 1) * T], vT[:, 2, r:r + 1], HH[:, c, :].bitcast(F32), ALU.mult, ALU.subtract)
                    last.then_inc(*done("input_ready", i, b))

            def site_tail(i):
                kind, n = SITES[i]
                for t in range(2):
                    dve.wait_ge(*at("y_squares", i, t, 1))
                    TTn(stat[:, 26 + t:27 + t], stat[:, 10 + 2 * t:11 + 2 * t], stat[:, 11 + 2 * t:12 + 2 * t], ALU.add).then_inc(*done("y_scale", "sum", i, t))
                    dve.wait_ge(*at("y_root", i, t))
                    dve.reciprocal(stat[:, 28 + t:29 + t], stat[:, 28 + t:29 + t]).then_inc(*done("y_scale", "inverse", i, t))
                    dve.wait_ge(*at("y_scale", "inverse", i, t))
                    if kind == "ffn":
                        TS(stat[:, 30 + t:31 + t], stat[:, 28 + t:29 + t], 0.5, None, ALU.mult).then_inc(*done("y_scale", "half", i, t))
                        dve.wait_ge(*at("y_scale", "half", i, t))
                    sc = stat[:, 30 + t:31 + t] if kind == "ffn" else stat[:, 28 + t:29 + t]
                    dve.wait_ge(M.sem("gain_loaded"), 16 * (i + 1))
                    for hf in range(2):
                        if t:
                            dve.wait_ge(*at("x_updated", "site", i, 0, hf))
                        elif i:
                            dve.wait_ge(*at("x_updated", "site", i - 1, 1, hf))
                        else:
                            dve.wait_ge(*at("x_updated", "b1", 1, 1, hf))
                        STT(ytmp[:, hf, :], B[4 + 2 * t + hf][:, :], sc, gain_row[:, hf * 512:(hf + 1) * 512], ALU.mult, ALU.mult).then_inc(*done("out_scaled", "site", i, t, hf))

            def ffn(i, n):
                f0 = n * FFN_CHUNKS

                def product(par, ready):
                    dve.wait_ge(s_silu, ready)
                    TTn(hbuf[:, par, :], B[par][:, T:TT], sgate[:, par, :], ALU.mult).then_inc(s_h, 1)

                def hidden_low(par, ready):
                    dve.wait_ge(s_hh, ready)
                    TTn(HBL[:, par, :], hbuf[:, par, :], HBH[:, par, :].bitcast(F32), ALU.subtract).then_inc(s_hl, 1)

                a = unit_base[i]
                product(0, f0 + 1)
                low(a + 6)
                hidden_low(0, f0 + 1)
                low(a + 7)
                product(1, f0 + 2)
                low(a + 8)
                hidden_low(1, f0 + 2)
                low(a + 9)
                low(a + 10)

                def pair(a, f, j=None):
                    split = [U for U in range(a + 6, a + 12) if U < len(UNITS2)]
                    product(0, step(f + 1, j, 2))
                    for U in split[0:1]:
                        low(U, j)
                    hidden_low(0, step(f + 1, j, 2))
                    for U in split[1:3]:
                        low(U, j)
                    product(1, step(f + 2, j, 2))
                    for U in split[3:4]:
                        low(U, j)
                    hidden_low(1, step(f + 2, j, 2))
                    for U in split[4:]:
                        low(U, j)

                with dve.Fori(0, FFN_PAIRS - 2) as j:
                    pair(a + 5, f0 + 2, j)
                pair(a + 5 + 6 * (FFN_PAIRS - 2), f0 + FFN_CHUNKS - 2)

            def mix(i, n):
                u0 = unit_base[i]
                for s, (_, kind, blocks) in enumerate(MIX_SLOTS):
                    if kind == "v":
                        dve.wait_ge(s_used, u0 + 2 * s + 2)
                        src = B[PB2["v", blocks[0]]][:, :].rearrange("p (t b n) -> p t b n", t=2, b=2)
                        dst = FV[:, :, :].rearrange("p t (b n) -> p t b n", n=P)[:, :, blocks[0]:blocks[1] + 1:blocks[1] - blocks[0], :]
                        for t in range(2):
                            last = CP(dst[:, t], src[:, t])
                        last.then_inc(*done("v2_ready", n, blocks[0]))
                    for q, b in enumerate(blocks):
                        if kind == "qk" and b % 2:
                            dve.wait_ge(s_used, u0 + 2 * s + q + 1)
                            TS(FQ[:, b, :], B[PB2["qk", b]][:, 0:T], QKSC[b], None, ALU.mult).then_inc(*done("qk_ready_dve", n, b))
                        low(u0 + 2 * s + q + SPLIT)
                if n == 0:
                    dve.wait_ge(M.sem("alibi_loaded"), 16)
                dve.wait_ge(*at("lambda_ready", n))

                def unit_bias(u):
                    hd = u if u < N_DIL else N_DIL + (u - N_DIL) // 2
                    dve.wait_ge(*at("scores2", n, u))
                    if u >= 2:
                        dve.wait_ge(*at("exp2_ready", n, u - 2))
                    for qt, (a, w) in enumerate(((0, P), (P, T))):
                        last = dve.tensor_tensor_reduce(out=S2[:, u % 2, a:a + w], in0=B[u % 2][:, a:a + w], in1=alibi[:, hd, a:a + w], scale=-1.0, scalar=-NEG, op0=ALU.add, op1=ALU.min, accum_out=stat[:, 16 + 2 * (u % 2) + qt:17 + 2 * (u % 2) + qt])
                    last.then_inc(*done("neg_max2", n, u))

                def unit_norm(u):
                    dve.wait_ge(*at("exp2_ready", n, u))
                    dve.reciprocal(stat[:, 54 + 2 * (u % 2):56 + 2 * (u % 2)], stat[:, 20 + 2 * (u % 2):22 + 2 * (u % 2)]).then_inc(*done("inverse2", n, u))
                    dve.wait_ge(*at("inverse2", n, u))
                    second = u >= N_DIL and (u - N_DIL) % 2
                    if second:
                        TS(stat[:, 58:60], stat[:, 54 + 2 * (u % 2):56 + 2 * (u % 2)], lamv[:, n, 4:5], None, ALU.mult).then_inc(*done("lambda_scaled", n, u))
                        dve.wait_ge(*at("lambda_scaled", n, u))
                        dve.wait_ge(*at("p2_ready", n, u - 1))
                        for qt, (a, w) in enumerate(((0, P), (P, T))):
                            last = STT(SS[:, u % 4, a:a + w], SS[:, u % 4, a:a + w], stat[:, 58 + qt:59 + qt], SS[:, (u - 1) % 4, a:a + w], ALU.mult, ALU.add)
                    else:
                        for qt, (a, w) in enumerate(((0, P), (P, T))):
                            last = TS(SS[:, u % 4, a:a + w], SS[:, u % 4, a:a + w], stat[:, 54 + 2 * (u % 2) + qt:55 + 2 * (u % 2) + qt], None, ALU.mult)
                    last.then_inc(*done("p2_ready", n, u))

                def split_out(b, src, stage):
                    CP(HH[:, b, :], src).then_inc(*done("o_part", n, "high", b))
                    dve.wait_ge(*at("o_part", n, "high", b))
                    TTn(HL[:, b, :], src, HH[:, b, :].bitcast(F32), ALU.subtract).then_inc(*done(stage, n, b))

                def head_out(h):
                    b = h // 2
                    dve.wait_ge(*at("attn2", n, h))
                    if b < 3:
                        split_out(b, B[4 + b % 2][:, 0:T], "o_ready")
                    else:
                        CP(OB2[:, b - 3, :], B[4 + b % 2][:, 0:T]).then_inc(*done("ob_ready", n, b - 3))

                NU = N_DIL + 2 * N_DIFF
                unit_bias(0)
                for u in range(NU):
                    if u + 1 < NU:
                        unit_bias(u + 1)
                    unit_norm(u)
                    h = UNIT_HEAD[u]
                    if h is not None and h % 2 == 0 and h:
                        head_out(h - 1)
                head_out(N_DIL + N_DIFF - 1)
                for b in range(2):
                    dve.wait_ge(*at("ob_root", n, b))
                    dve.reciprocal(sgate[:, b, :], sgate[:, b, :]).then_inc(*done("ob_inverse", n, b))
                    dve.wait_ge(*at("ob_inverse", n, b))
                    dve.wait_ge(*at("sub_gain", n))
                    STT(OB2[:, b, :], OB2[:, b, :], lamv[:, n, 5:6], sgate[:, b, :], ALU.mult, ALU.mult).then_inc(*done("o_part", n, "normed", b))
                    dve.wait_ge(*at("o_part", n, "normed", b))
                    split_out(3 + b, OB2[:, b, :], "o_ready")
                for h in range(N_SB):
                    dve.wait_ge(*at("z_ln", n, h))
                    STT(ZP[:, h, :], B[h][:, 0:384], 0.0, ZE[:, h, :], ALU.max, ALU.add).then_inc(*done("softplus_ready", n, h))
                for h in range(N_SB):
                    dve.wait_ge(*at("z_less_sum", n, h))
                    STT(ZE[:, h, :], B[h][:, 0:384], 0.0, gap, ALU.min, ALU.add).then_inc(*done("log_weight", n, h))
                for b in range(3):
                    dve.wait_ge(*at("attn3", n, 2 * b + 1))
                    split_out(5 + b, B[6 + b % 2][:, 0:T], "o_ready")
                for U in range(u0 + 24, u0 + 31):
                    low(U + SPLIT)

            for i, (kind, n) in enumerate(SITES):
                site_norm(i)
                (ffn if kind == "ffn" else mix)(i, n)
                site_tail(i)
                if i < 5:
                    low(unit_base[i + 1] + SPLIT - 1)

        @block.tensor
        def _(pe):
            mm, tr = pe.matmul, pe.transpose
            readers = {b: [] for b in range(8)}

            def hand_over(b, *reads):
                old, readers[b] = readers[b], list(reads)
                return old

            pe.wait_ge(M.sem("vec_loaded"), 64)
            for r in hand_over(0, ("vec_T", 0)):
                pe.wait_ge(*at(*r))
            b = B[0]
            for q in range(3):
                last = tr(b[:, q * P:(q + 1) * P], vec[:, q, :], ident)
            last.then_inc(*done("vec_transposed"))

            def ada_product(L, s):
                pe.wait_ge(*at("silu_c"))
                if s == 0:
                    for r in hand_over(6, ("ada_copied", L, ADA_SLOTS - 1)):
                        pe.wait_ge(*at(*r))
                if s >= 2:
                    pe.wait_ge(*at("ada_copied", L, s - 2))
                n = base[("ada", L)] + s
                pe.wait_ge(*filled(n))
                for k in range(KD):
                    last = mm(B[6][ADA_AT[s % 2], 0:T], CS[:, k:16:8], cols(n)[:, k, :], start=(k == 0), stop=(k == KD - 1), skip_group_check=True)
                last.then_inc(*done("ada_rows", L, s))

            def ada_transpose(L, s):
                if s == 0:
                    for r in hand_over(7, ("ada_biased", L)):
                        pe.wait_ge(*at(*r))
                else:
                    pe.wait_ge(*at("ada_T", L, s - 1))
                pe.wait_ge(*at("ada_copied", L, s))
                for q in range(2):
                    blk = 2 * s + q
                    last = tr(B[7][:, 2 * blk:2 * blk + 2], ada_row[ADA_AT[s % 2], q * P:(q + 1) * P], ident[ADA_AT[s % 2], ADA_AT[s % 2]])
                last.then_inc(*done("ada_T", L, s))

            def layer(L):
                nq = TT if L == 0 else T
                nt = nq // P
                if L == 0:
                    for sl in range(ADA_SLOTS):
                        ada_product(0, sl)
                        if sl:
                            ada_transpose(0, sl - 1)
                    ada_transpose(0, ADA_SLOTS - 1)
                for c in range(KD):
                    for t in range(4):
                        pe.wait_ge(*at("x_scaled", "b1", L, t))
                    for r in hand_over(c % 4, ("hT_ready_act" if c % 2 == 0 else "hT_ready_dve", "b1", L, c)):
                        pe.wait_ge(*at(*r))
                    b = B[c % 4]
                    for t in range(4):
                        last = tr(b[:, t * P:(t + 1) * P], XN[:, t, c * P:(c + 1) * P], ident)
                    last.then_inc(*done("x_T", "b1", L, c))
                pe.wait_ge(M.sem("small_loaded"), SW * (L + 1))
                for r in hand_over(5, ("wsT_ready", L)):
                    pe.wait_ge(*at(*r))
                b = B[5]
                for g in range(4):
                    last = tr(b[:, g * P:(g + 1) * P], w_s[:, g, :], ident)
                last.then_inc(*done("ws_transposed", L))
                for c in range(KD):
                    pe.wait_ge(*at("hT_ready_act" if c % 2 == 0 else "hT_ready_dve", "b1", L, c))

                n0 = base[("win", L)]

                def project(name, j, n, lhs, out_rows, ncol, reader):
                    key = (name,) if j is None else (name, j)
                    for r in hand_over(PB[L][key if j is not None else name], reader):
                        pe.wait_ge(*at(*r))
                    b = B[PB[L][key if j is not None else name]]
                    for k in range(KD):
                        last = mm(b[out_rows, 0:ncol], lhs(k), hT[:, k, 0:ncol], start=(k == 0), stop=(k == KD - 1))
                    last.then_inc(*done("proj", L, *key))
                    return last

                def col(n, w, a, m):
                    return lambda k: cols(n, w)[:, k, a:a + m]

                allp = slice(0, P)

                def sq_sums():
                    for r in hand_over(6, ("q_root", L)):
                        pe.wait_ge(*at(*r))
                    for j in range(2):
                        pe.wait_ge(*at("q_part_ready", L, j))
                        last = mm(B[6][:, 0:nq], ones, sq[:, j, 0:nq], start=(j == 0), stop=(j == 1))
                    last.then_inc(*done("q_square_sum", L))
                    for r in hand_over(7, ("kv_root", L)):
                        pe.wait_ge(*at(*r))
                    pe.wait_ge(*at("kv_part_ready", L))
                    mm(B[7][:, :], ones, sq[:, 2, :], start=True, stop=True).then_inc(*done("kv_square_sum", L))

                pe.wait_ge(*filled(n0))
                for j in range(2):
                    project("q", j, n0, col(n0, 256, j * P, P), allp, nq, ("q_part_ready", L, j))
                n = n0 + 1
                pe.wait_ge(*filled(n))
                project("kv", None, n, col(n, 160, 0, P), allp, TT, ("kv_part_ready", L))
                project("kr", None, n, col(n, 160, P, ROPE), slice(NOPE, QK), TT, ("kr_copied", L))
                pe.wait_ge(*at("kr_swapped", L))
                project("krs", None, n, lambda k: w_krs[:, k, :], slice(NOPE, QK), T, ("kr_sin", L))
                for name, s, rd in (("a", 2, "a_ready"), ("g", 3, "conv_gate_ready"), ("f", 4, "f_ready"), ("u", 5, "u_ready")):
                    n = n0 + s
                    pe.wait_ge(*filled(n))
                    for j in range(2):
                        project(name, j, n, col(n, 256, j * P, P), allp, nq, (rd, L, j))
                    if name == "a":
                        sq_sums()
                n = n0 + 6
                pe.wait_ge(*filled(n))
                for t in range(nt):
                    for r in hand_over(PB[L]["v", t], ("v_copied", L, t)):
                        pe.wait_ge(*at(*r))
                    b = B[PB[L]["v", t]]
                    for k in range(KD):
                        last = mm(b[:, 0:256], hT[:, k, t * P:(t + 1) * P], cols(n)[:, k, :], start=(k == 0), stop=(k == KD - 1))
                    last.then_inc(*done("proj", L, "v", t))
                pe.wait_ge(M.sem("base_loaded"), 48)
                for t in range(nt):
                    for r in hand_over(6 + t % 2, ("fa_ready", L, t)):
                        pe.wait_ge(*at(*r))
                    b = B[6 + t % 2]
                    for j in range(2):
                        pe.wait_ge(*at("f_ready", L, j))
                        last = mm(b[:, j * 256:(j + 1) * 256], fT[:, j, t * P:(t + 1) * P], dft_d, start=True, stop=True)
                    last.then_inc(*done("fourier_feat", L, t))
                for s in range(4):
                    n = n0 + 7 + s
                    pe.wait_ge(*filled(n))
                    for q in range(2):
                        j = 2 * s + q
                        project("gate", j, n, col(n, 256, q * P, P), allp, nq, ("sg_ready", L, j))
                    if s == 0:
                        for m in range(2):
                            for r in hand_over(6 + m, ("f_mixed", L, m)):
                                pe.wait_ge(*at(*r))
                            b = B[6 + m]
                            for sg in range(nq // T):
                                q = 0
                                for tl in range(2):
                                    pe.wait_ge(*at("fa_ready", L, 2 * sg + tl))
                                    for cs in range(2):
                                        last = mm(b[:, sg * T:(sg + 1) * T], FA[:, 2 * sg + tl, m, cs * P:(cs + 1) * P], dft_n[:, cs, tl, :], start=(q == 0), stop=(q == 3))
                                        q += 1
                            last.then_inc(*done("fourier_tok", L, m))
                    if s == 1:
                        for m in range(2):
                            for r in hand_over(4 + m, ("four_branch", L, m)):
                                pe.wait_ge(*at(*r))
                            b = B[4 + m]
                            for j in range(2):
                                pe.wait_ge(*at("f_mixed", L, j))
                                last = mm(b[:, 0:nq], w_fo[:, j, m * P:(m + 1) * P], cacc[:, j, 0:nq], start=(j == 0), stop=(j == 1))
                            last.then_inc(*done("fourier_out", L, m))
                pe.wait_ge(*at("wsT_ready", L))
                for m in range(2):
                    for r in hand_over(6 + m, ("sgu_branch", L, m)):
                        pe.wait_ge(*at(*r))
                    b = B[6 + m]
                    for t in range(nt):
                        pe.wait_ge(*at("v_ready", L, t))
                        for gg in range(2):
                            g = 2 * m + gg
                            o = b[gg * 64:(gg + 1) * 64, t * P:(t + 1) * P]
                            mm(o, VN[:, t, g * 64:(g + 1) * 64], wsT[:, g, :], start=True, stop=False)
                            last = mm(o, ones[0:1, 0:64], bsrow[0:1, L, g * P:(g + 1) * P], start=False, stop=True)
                    last.then_inc(*done("sgu_mixed", L, m))
                for v in range(nq // T):
                    for hf in range(2):
                        for r in hand_over((2 * v + hf) % 4, ("gate_row_ready", L, v, hf)):
                            pe.wait_ge(*at(*r))
                        b = B[(2 * v + hf) % 4]
                        pe.wait_ge(*at("gate_diag_ready", L, v, hf))
                        mm(b[:, :], ones, gate_diag[:, hf, :], start=True, stop=True).then_inc(*done("gate_rows", L, v, hf))
                pe.wait_ge(*at("uq_swapped", L))
                for h in range(HEADS):
                    for r in hand_over(h % 2, ("q_copied", L, h)):
                        pe.wait_ge(*at(*r))
                    b = B[h % 2]
                    for j in range(2):
                        pe.wait_ge(*at("q_latent", L, j))
                        last = mm(b[0:QK, 0:nq], w_uq[:, j, h * QK:(h + 1) * QK], qp[:, j, 0:nq], start=(j == 0), stop=(j == 1))
                    last.then_inc(*done("q_heads", L, h))
                    for r in hand_over(2 + h % 2, ("q_sin", L, h)):
                        pe.wait_ge(*at(*r))
                    b = B[2 + h % 2]
                    for j in range(2):
                        last = mm(b[NOPE:QK, 0:T], w_uqs[:, j, h * ROPE:(h + 1) * ROPE], qp[:, j, 0:T], start=(j == 0), stop=(j == 1))
                    last.then_inc(*done("q_swapped", L, h))
                pe.wait_ge(*at("kv_latent", L))
                for h in range(HEADS):
                    for r in hand_over(h % 2, ("k_copied", L, h)):
                        pe.wait_ge(*at(*r))
                    b = B[h % 2]
                    mm(b[0:NOPE, :], w_ukv[:, h * P:h * P + NOPE], kvp, start=True, stop=True).then_inc(*done("k_heads", L, h))
                vcols = w_ukv.rearrange("p (h n) -> p h n", h=4)[:, :, NOPE:P]
                for t in range(4):
                    for r in hand_over(4 + t, ("v_heads_ready", L, t)):
                        pe.wait_ge(*at(*r))
                    b = B[4 + t]
                    mm(b[:, 0:256].rearrange("p (h n) -> p h n", h=4), kvp[:, t * P:(t + 1) * P], vcols, start=True, stop=True).then_inc(*done("v_heads", L, t))
                pe.wait_ge(*at("k_rope_ready", L))
                UNITS = [(seg, h) for seg in range(nq // T) for h in range(HEADS)]

                def scores(i):
                    seg, h = UNITS[i]
                    k0, keys = (0, TT) if seg == 0 else (T, T)
                    pe.wait_ge(*at("k_copied", L, h))
                    pe.wait_ge(*at("q_ready", L, h))
                    for qt in range(2):
                        for r in hand_over(qt, ("exp_ready", L, seg, h, qt)):
                            pe.wait_ge(*at(*r))
                        b = B[qt]
                        mm(b[:, 0:keys], Q[0:QK, h, seg * T + qt * P:seg * T + (qt + 1) * P], K[0:QK, h, k0:k0 + keys], start=True, stop=True).then_inc(*done("scores", L, seg, h, qt))

                def transposes(i):
                    seg, h = UNITS[i]
                    for qt in range(2):
                        for r in hand_over(2 + qt, ("pT_ready", L, seg, h, qt)):
                            pe.wait_ge(*at(*r))
                        b = B[2 + qt]
                        pe.wait_ge(*at("p_ready", L, seg, h, qt))
                        for kt in range(4 if seg == 0 else 2):
                            last = tr(b[:, kt * P:(kt + 1) * P], Pm[i % 2][:, qt, kt * P:(kt + 1) * P], ident)
                        last.then_inc(*done("p_T", L, seg, h, qt))

                def weighted(i):
                    seg, h = UNITS[i]
                    k0, nk = (0, 4) if seg == 0 else (2, 2)
                    b = B[4 + h // 2]
                    if h % 2 == 0:
                        for r in hand_over(4 + h // 2, ("attn_ready", L, h + 1, seg)):
                            pe.wait_ge(*at(*r))
                    for qt in range(2):
                        pe.wait_ge(*at("pT_ready", L, seg, h, qt))
                    for kt in range(nk):
                        pe.wait_ge(*at("v_heads_ready", L, k0 + kt))
                        last = mm(b[(h % 2) * 64:(h % 2 + 1) * 64, 0:T], V[:, k0 + kt, h * 64:(h + 1) * 64], PT[i % 2][:, kt, :], start=(kt == 0), stop=(kt == nk - 1))
                    last.then_inc(*done("attn", L, seg, h))

                scores(0)
                for i in range(len(UNITS)):
                    if i + 1 < len(UNITS):
                        scores(i + 1)
                    if L == 0:
                        for sl in ADA_STEP[i]:
                            ada_product(1, sl)
                    transposes(i)
                    if L == 0:
                        for sl in ADA_STEP[i]:
                            ada_transpose(1, sl)
                    if i:
                        weighted(i - 1)
                weighted(len(UNITS) - 1)
                for j in range(2):
                    pe.wait_ge(*at("conv_tap", L, j, CONV_K - 1))
                for r in hand_over(0, ("conv_centred", L, 1)):
                    pe.wait_ge(*at(*r))
                b = B[0]
                for j in range(2):
                    last = mm(b[:, 0:nq], ones, cacc[:, j, 0:nq], start=(j == 0), stop=(j == 1))
                last.then_inc(*done("conv_mean", L))
                for r in hand_over(1, ("conv_root", L)):
                    pe.wait_ge(*at(*r))
                b = B[1]
                for j in range(2):
                    pe.wait_ge(*at("conv_square", L, j))
                    last = mm(b[:, 0:nq], ones, sq[:, j, 0:nq], start=(j == 0), stop=(j == 1))
                last.then_inc(*done("conv_var", L))
                for m in range(2):
                    for r in hand_over(2 + m, ("conv_branch", L, m)):
                        pe.wait_ge(*at(*r))
                    b = B[2 + m]
                    for j in range(2):
                        pe.wait_ge(*at("conv_act", L, j))
                        last = mm(b[:, 0:nq], w_pw[:, j, m * P:(m + 1) * P], csg[:, j, 0:nq], start=(j == 0), stop=(j == 1))
                    last.then_inc(*done("conv_out", L, m))
                for stage in ("four_branch", "sgu_branch", "conv_branch"):
                    pe.wait_ge(*at(stage, L, 1))
                pe.wait_ge(*at("attn_ready", L, HEADS - 1, nq // T - 1))
                for t in range(nt):
                    for hf in range(2):
                        for r in hand_over(YB[L][t, hf], ("out_scaled", "b1", L, t, hf)):
                            pe.wait_ge(*at(*r))
                for s in range(4):
                    n = base[("wout", L)] + s
                    pe.wait_ge(*filled(n))
                    for r in range(2):
                        k = 2 * s + r
                        for t in range(nt):
                            for hf in range(2):
                                last = mm(B[YB[L][t, hf]][:, :], SG[:, k, t * P:(t + 1) * P], rows(n)[:, r, hf * 512:(hf + 1) * 512], start=(k == 0), stop=(k == KD - 1))
                                if k == KD - 1:
                                    last.then_inc(*done("y_ready", "b1", L, t, hf))
                    if s < 3:
                        last.then_inc(*done("wout_used", L, s))

            def site_norm(i):
                for b in range(4):
                    for r in hand_over(b, ("input_ready", i, b)):
                        pe.wait_ge(*at(*r))
                    bk = B[b]
                    for q in range(2):
                        for t in range(2):
                            pe.wait_ge(*at("x_scaled", "site", i, t))
                            c = 2 * b + q
                            last = tr(bk[:, q * T + t * P:q * T + (t + 1) * P], XN2[:, t, c * P:(c + 1) * P], ident)
                    last.then_inc(*done("x_T", "site", i, b))
                for b in range(4):
                    pe.wait_ge(*at("input_ready", i, b))

            def three(o, lhs, rhs, start, stop):
                for m, (x, y) in enumerate(((0, 0), (0, 1), (1, 0))):
                    last = mm(o, lhs(x), rhs(y), start=start and m == 0, stop=stop and m == 2, skip_group_check=True)
                return last

            W, H, HB = (WH, WL), (HH, HL), (HBH, HBL)

            def feature_major(o, U):
                for k in range(KD):
                    last = three(o, lambda x: unit_in(W[x], U)[:, k, :], lambda y: H[y][:, k, :], k == 0, k == KD - 1)
                return last

            def ffn(i, n):
                f0 = n * FFN_CHUNKS
                for q in range(4):
                    for r in hand_over(q):
                        pe.wait_ge(*at(*r))
                for t in range(2):
                    for hf in range(2):
                        for r in hand_over(4 + 2 * t + hf, ("out_scaled", "site", i, t, hf)):
                            pe.wait_ge(*at(*r))

                def gate_up(par, U, free, j=None):
                    if free is not None:
                        pe.wait_ge(s_h, free)
                    for q in range(2):
                        pe.wait_ge(s_low, step(U + q + 1, j, 6))
                        feature_major(B[par][:, q * T:(q + 1) * T], U + q).then_inc(s_used, 1)

                def down(par, U, ready, first, final, j=None):
                    pe.wait_ge(s_hl, ready)
                    pe.wait_ge(s_low, step(U + 1, j, 6))
                    for t in range(2):
                        for hf in range(2):
                            last = three(B[4 + 2 * t + hf][:, :], lambda x: HB[x][:, par, t * P:(t + 1) * P], lambda y: W[y][:, U % SPLIT, hf * 512:(hf + 1) * 512], first, final)
                            if final and (t, hf) != (1, 1):
                                last.then_inc(*done("y_ready", "site", i, t, hf))
                    last.then_inc(s_used, 1)

                a = unit_base[i]
                gate_up(0, a, f0 if n else None)
                gate_up(1, a + 2, f0 if n else None)
                down(0, a + 4, f0 + 1, True, False)

                def pair(a, f, j=None):
                    gate_up(0, a, step(f - 1, j, 2), j)
                    down(1, a + 2, step(f, j, 2), False, False, j)
                    gate_up(1, a + 3, step(f, j, 2), j)
                    down(0, a + 5, step(f + 1, j, 2), False, False, j)

                with pe.Fori(0, FFN_PAIRS - 2) as j:
                    pair(a + 5, f0 + 2, j)
                pair(a + 5 + 6 * (FFN_PAIRS - 2), f0 + FFN_CHUNKS - 2)
                down(1, a + 6 * FFN_PAIRS - 1, f0 + FFN_CHUNKS, False, True)

            def mix(i, n):
                u0 = unit_base[i]
                for s, (_, kind, blocks) in enumerate(MIX_SLOTS):
                    if kind == "qk":
                        for q, idx in enumerate(blocks):
                            U = u0 + 2 * s + q
                            for r in hand_over(PB2[kind, idx], ("qk_ready_act" if idx % 2 == 0 else "qk_ready_dve", n, idx)):
                                pe.wait_ge(*at(*r))
                            pe.wait_ge(s_low, U + 1)
                            feature_major(B[PB2[kind, idx]][:, 0:T], U).then_inc(s_used, 1)
                    else:
                        U = u0 + 2 * s
                        for r in hand_over(PB2[kind, blocks[0]], ("v2_ready", n, blocks[0])):
                            pe.wait_ge(*at(*r))
                        pe.wait_ge(s_low, U + 2)
                        wide = [w[:, U % SPLIT:U % SPLIT + 2, :].rearrange("p u (k n) -> p k u n", k=8) for w in W]
                        for t in range(2):
                            o = B[PB2[kind, blocks[0]]][:, t * T:(t + 1) * T].rearrange("p (u n) -> p u n", u=2)
                            for k in range(KD):
                                last = three(o, lambda x: H[x][:, k, t * P:(t + 1) * P], lambda y: wide[y][:, k], k == 0, k == KD - 1)
                        last.then_inc(s_used, 2)
                for b in range(16):
                    pe.wait_ge(*at("qk_ready_act" if b % 2 == 0 else "qk_ready_dve", n, b))

                def score(u):
                    if u < N_DIL:
                        qb, kb, p0, kk = u // 2, 3 + u // 2, (u % 2) * 64, 64
                    else:
                        d = u - N_DIL
                        qb, kb, p0, kk = 6 + d // 4, 8 + d // 4, (d % 4) * 32, 32
                    for r in hand_over(u % 2, ("neg_max2", n, u)):
                        pe.wait_ge(*at(*r))
                    b = B[u % 2]
                    mm(b[:, 0:P], FQ[p0:p0 + kk, qb, 0:P], FQ[p0:p0 + kk, kb, 0:P], start=True, stop=True)
                    mm(b[:, P:384], FQ[p0:p0 + kk, qb, P:T], FQ[p0:p0 + kk, kb, :], start=True, stop=True).then_inc(*done("scores2", n, u))

                def value(h, u):
                    for r in hand_over(2 + h % 2, ("pT2_ready", n, h)):
                        pe.wait_ge(*at(*r))
                    b = B[2 + h % 2]
                    pe.wait_ge(*at("p2_ready", n, u))
                    src = SS[:, u % 4, :]
                    tr(b[:, 0:P], src[:, 0:P], ident)
                    tr(b[:, P:T], src[:, P:T], ident)
                    tr(b[:, T:384], src[:, T:384], ident).then_inc(*done("p2_T", n, h))

                def weighted(h):
                    blk = h // 2
                    if h % 2 == 0:
                        for r in hand_over(4 + blk % 2, ("o_ready", n, blk) if blk < 3 else ("ob_ready", n, blk - 3)):
                            pe.wait_ge(*at(*r))
                    o = B[4 + blk % 2][(h % 2) * 64:(h % 2 + 1) * 64, :]
                    pe.wait_ge(*at("pT2_ready", n, h))
                    pe.wait_ge(*at("v2_ready", n, 3))
                    mm(o[:, 0:T], FV[:, 0, h * 64:(h + 1) * 64], PT2[:, h % 2, 0:T], start=True, stop=False, skip_group_check=True)
                    mm(o[:, P:T], FV[:, 1, h * 64:(h + 1) * 64], PT2[:, h % 2, T:384], start=False, stop=True, skip_group_check=True).then_inc(*done("attn2", n, h))

                NU = N_DIL + 2 * N_DIFF
                score(0)
                for u in range(NU):
                    if u + 1 < NU:
                        score(u + 1)
                    h = UNIT_HEAD[u]
                    if h is not None:
                        value(h, u)
                        weighted(h)
                def z(h):
                    for r in hand_over(h, ("log_weight", n, h)):
                        pe.wait_ge(*at(*r))
                    b = B[h]
                    p0, qb, kb = (h % 2) * 64, 10 + h // 2, 13 + h // 2
                    mm(b[:, 0:T], FQ[p0:p0 + 64, kb, 0:P], FQ[p0:p0 + 64, qb, :], start=True, stop=False, skip_group_check=True)
                    mm(b[:, T:384], FQ[p0:p0 + 64, kb, P:T], FQ[p0:p0 + 64, qb, P:T], start=False, stop=False, skip_group_check=True).then_inc(*done("z_ready", n, h))

                for b in range(2):
                    pe.wait_ge(*at("ob_square", n, b))
                    for r in hand_over(4 + b, ("ob_root", n, b)):
                        pe.wait_ge(*at(*r))
                    mm(B[4 + b][:, T:TT], heads2, sgate[:, b, :], start=True, stop=True).then_inc(*done("ob_sum", n, b))
                for h in range(N_SB):
                    z(h)
                for h in range(N_SB):
                    pe.wait_ge(*at("softplus_masked", n, h))
                    mm(B[h][:, 0:384], ntri, ZP[:, h, :], start=False, stop=False, skip_group_check=True)
                    mm(B[h][:, P:T], negones, ZP[:, h, T:384], start=False, stop=True, skip_group_check=True).then_inc(*done("z_less_sum", n, h))
                for h in range(N_SB):
                    if h % 2 == 0:
                        for r in hand_over(6 + (h // 2) % 2, ("o_ready", n, 5 + h // 2)):
                            pe.wait_ge(*at(*r))
                    o = B[6 + (h // 2) % 2][(h % 2) * 64:(h % 2 + 1) * 64, :]
                    pe.wait_ge(*at("weight_ready", n, h))
                    pe.wait_ge(*at("v2_ready", n, 5))
                    hv = N_DIL + N_DIFF + h
                    mm(o[:, 0:T], FV[:, 0, hv * 64:(hv + 1) * 64], ZP[:, h, 0:T], start=True, stop=False, skip_group_check=True)
                    mm(o[:, P:T], FV[:, 1, hv * 64:(hv + 1) * 64], ZP[:, h, T:384], start=False, stop=True, skip_group_check=True).then_inc(*done("attn3", n, h))
                for t in range(2):
                    for hf in range(2):
                        for r in hand_over(4 + 2 * t + hf, ("out_scaled", "site", i, t, hf)):
                            pe.wait_ge(*at(*r))
                for k in range(KD):
                    U = u0 + 24 + k
                    pe.wait_ge(s_low, U + 1)
                    pe.wait_ge(*at("o_ready", n, k))
                    for t in range(2):
                        for hf in range(2):
                            last = three(B[4 + 2 * t + hf][:, :], lambda x: H[x][:, k, t * P:(t + 1) * P], lambda y: W[y][:, U % SPLIT, hf * 512:(hf + 1) * 512], k == 0, k == KD - 1)
                            if k == KD - 1 and (t, hf) != (1, 1):
                                last.then_inc(*done("y_ready", "site", i, t, hf))
                    last.then_inc(s_used, 1)

            layer(0)
            layer(1)
            for i, (kind, n) in enumerate(SITES):
                site_norm(i)
                (ffn if kind == "ffn" else mix)(i, n)


INPUTS = ["x", "c", "ctx", "c_ctx", "w_ada", "w_in", "w_uq", "w_ukv", "w_pw", "w_fourier", "sgu_ln_g", "sgu_ln_b", "w_s", "b_s",
          "w_out", "final_g", "norm_gains_2", "w_ffn_gate_2", "w_ffn_up_2", "w_ffn_down_2", "w_in_2", "w_out_2", "diff_lambda_2"]
VECTORS = ["b_ada", "norm_g", "q_norm_g", "kv_norm_g", "conv_w", "conv_b", "conv_ln_g", "conv_ln_b", "b_pw", "b_fourier"]


def kernel(**inputs):
    import numpy as _np
    import concourse.bacc as _bacc
    from contextlib import ExitStack as _ExitStack
    from concourse import mybir as _mybir
    from concourse.bass_utils import run_bass_kernel_spmd as _run

    a = {k: _np.asarray(v) for k, v in inputs.items()}
    arrays = {n: _np.ascontiguousarray(a[n]) for n in INPUTS if n not in ("c", "c_ctx")}
    banks = []
    for L in range(2):
        rows = [a[n][L].reshape(-1, 128) for n in VECTORS] + [a["c"].reshape(-1, 128), a["c_ctx"].reshape(-1, 128)]
        rows.append(_np.zeros((128 - sum(r.shape[0] for r in rows), 128), _np.float32))
        banks.append(_np.concatenate(rows))
    arrays["k_vec1"] = _np.stack(banks)
    rows = [a["norm_gains_2"][i // 3, 2 * (i % 3)].reshape(-1, 128) for i in range(6)]
    rows += [_np.concatenate([a["diff_subln_gain_2"][m]] * 2)[None] for m in range(2)]
    rows.append(_np.zeros((128 - 50, 128), _np.float32))
    arrays["k_vec2"] = _np.concatenate(rows)
    arrays.update(constants())

    def build(table):
        nc = _bacc.Bacc("TRN2", target_bir_lowering=False, num_devices=1)
        I = {n: nc.dram_tensor("in_" + n, v.shape, _mybir.dt.from_np(v.dtype), kind="ExternalInput").ap() for n, v in arrays.items()}
        out = nc.dram_tensor("out_0", (1, 256, 1024), _mybir.dt.float32, kind="ExternalOutput").ap()
        program(nc, I, out, table)
        return nc

    table = {}
    build(table)
    nc = build(table)
    r = _run(nc, [{"in_" + n: v for n, v in arrays.items()}], core_ids=[0])
    return r.results[0]["out_0"]
```

```python
from contextlib import ExitStack

import numpy as np
import concourse.bass as bass
from concourse import mybir

F32 = mybir.dt.float32
F32R = mybir.dt.float32r
ACT = mybir.ActivationFunctionType
ALU = mybir.AluOpType
AXX = mybir.AxisListType.X

P = 128
D = 1024
KD = D // P
T = 256
TT = 512
RMS_EPS = 1e-6
LN_EPS = 1e-5

HEADS = 4
NOPE = 64
ROPE = 32
QK = NOPE + ROPE
CONV_K = 31
PAD = CONV_K // 2
CONV_AHEAD = 12
SEGP = T + 2 * PAD
FG_DIM = 64
ADA_SLOTS = 12
WIN_SLOTS = [(0, 256), (256, 160), (416, 256), (672, 256), (928, 256), (1184, 256), (1440, 256),
             (1696, 256), (1952, 256), (2208, 256), (2464, 256)]
WOUT_ORDER = ((0, 1, 2, 3), (0, 2, 3, 1))
R_BADA, R_NORM, R_QN, R_KVN, R_CW, R_CB, R_CLG, R_CLB, R_BPW, R_BF, R_C = 0, 24, 32, 34, 35, 97, 99, 101, 103, 105, 107
R_SUB = 48

N_DIL, N_DIFF, N_SB = 6, 4, 6
FF = 2816
FFN_PAIRS = FF // (2 * P)
FFN_CHUNKS = FF // P
FFN_SLOTS = 3 * FFN_PAIRS
NEG = -1.0e30
RING = 3
SPLIT = 6


class Marks:

    def __init__(self, nc, ctx, table):
        self.nc, self.ctx, self.table = nc, ctx, table
        self.sems, self.counts = {}, {}

    def sem(self, stage):
        if stage not in self.sems:
            self.sems[stage] = self.ctx.enter_context(self.nc.semaphore(stage))
        return self.sems[stage]

    def done(self, stage, *key):
        s = self.sem(stage)
        self.counts[stage] = self.counts.get(stage, 0) + 1
        self.table[(stage,) + key] = self.counts[stage]
        return s, 1

    def at(self, stage, *key):
        return self.sem(stage), self.table.get((stage,) + key, 1)


def constants():
    f = np.float32
    out = {}
    i = np.arange(P)
    ident = np.eye(P, dtype=f)
    ones = np.ones((P, P), f)
    heads2 = np.kron(np.eye(2), np.ones((64, 64))).astype(f) / 64
    ntri = -(i[:, None] >= i[None, :]).astype(f)
    a = 2 * np.pi * np.outer(np.arange(FG_DIM), np.arange(FG_DIM)) / FG_DIM
    scale = 1.0 / np.sqrt(T * FG_DIM)
    dft_d = np.concatenate([np.kron(np.eye(2), np.cos(a)), np.kron(np.eye(2), -np.sin(a))], 1) * scale
    b = 2 * np.pi * (np.outer(np.arange(T), np.arange(T)) % T) / T
    dft_n = np.stack([np.cos(b), np.sin(b)]).reshape(2, 2, P, T).transpose(2, 0, 1, 3).reshape(P, -1)
    strict = (i[:, None] < i[None, :]).astype(f)
    full = np.concatenate([strict, ones, strict], 1)
    gap = np.where(full > 0, 0.0, NEG)
    rows = T // 64
    inv = (f(10000.0) ** (-np.arange(0, 16, 2, dtype=f) / f(16))).astype(f)
    row = np.repeat(np.arange(rows), 64).astype(f)
    col = np.tile(np.arange(64), rows).astype(f)
    ang = np.stack([row[:, None] * inv, col[:, None] * inv], 1).astype(f)
    rope = np.zeros((P, 2 * T), f)
    for d in range(ROPE):
        ax, half, fr = d // 16, (d % 16) // 8, d % 8
        rope[NOPE + d, :T] = np.cos(ang[:, ax, fr])
        rope[NOPE + d, T:] = np.sin(ang[:, ax, fr]) * (1 if half else -1)
    out["k_base"] = np.concatenate([ident, ones, heads2, ntri, -ones, dft_d, dft_n, full, gap, rope], 1).astype(f)
    q = np.concatenate([np.tile(i[:, None], (1, P)), np.tile(P + i[:, None], (1, T))], 1)
    k = np.concatenate([i, np.arange(T)])[None, :]
    dist = q - k
    tabs = []
    count = (dist <= 128).astype(int) + (dist % 4 == 0) + (dist % 16 == 0)
    for h in range(N_DIL):
        slope = 2.0 ** (-8.0 * (h + 1) / N_DIL)
        ok = (dist >= 0) & (count > 0)
        tabs.append(np.where(ok, -slope * dist + np.log(np.maximum(count, 1)), NEG))
    for h in range(N_DIFF):
        slope = 2.0 ** (-8.0 * (h + 1) / N_DIFF)
        tabs.append(np.where(dist >= 0, -slope * dist, NEG))
    out["k_alibi"] = np.concatenate(tabs, 1).astype(f)
    return out


C_ID, C_ONES, C_H2, C_NTRI, C_NONE, C_DD, C_DN, C_FULL, C_GAP, C_ROPE, C_END = (
    0, 128, 256, 384, 512, 640, 896, 1920, 2304, 2688, 3200)

LAM_INIT = [0.8 - 0.6 * float(np.exp(-0.3 * m)) for m in range(2)]


def projection_banks():
    out = []
    for L in range(2):
        names = [("q", 0), ("q", 1), ("kv",), ("kr",), ("krs",)]
        names += [(n, j) for n in "agfu" for j in range(2)]
        names += [("v", t) for t in range(4 if L == 0 else 2)] + [("gate", j) for j in range(8)]
        out.append({(n if len(n) > 1 else n[0]): i % 4 for i, n in enumerate(names)})
    return out


PB = projection_banks()
ADA_AT = (slice(0, 2), slice(32, 34))
ADA_STEP = [range(3 * i // 2, 3 * (i + 1) // 2) for i in range(8)]
YB = [{(t, h): 2 * t + h for t in range(4) for h in range(2)}, {(t, h): 4 + 2 * t + h for t in range(2) for h in range(2)}]
MIX_SLOTS = [((0, 1), "qk", (0, 1)), ((2, 3), "qk", (2, 3)), ((4, 5), "qk", (4, 5)), ((6, 7), "v", (0, 1)), ((8, 23), "v", (2, 7)),
             ((9, 10), "qk", (6, 7)), ((11, 12), "qk", (8, 9)), ((13, 14), "v", (3, 4)),
             ((15, 16), "qk", (10, 11)), ((17, 18), "qk", (12, 13)), ((19, 20), "qk", (14, 15)), ((21, 22), "v", (5, 6))]
PROJ2_AHEAD, PROJ2_STEPS, PB2 = [], [], {}
for s, (_, kind, blocks) in enumerate(MIX_SLOTS):
    if kind == "qk":
        (PROJ2_AHEAD if s < 5 else PROJ2_STEPS).extend((2 * s + q, kind, (b,), (0, 1)) for q, b in enumerate(blocks))
    elif s < 5:
        PROJ2_AHEAD.append((2 * s, kind, blocks, (0, 1)))
    else:
        PROJ2_STEPS += [(2 * s, kind, blocks, (0,)), (2 * s, kind, blocks, (1,))]
for _, kind, blocks, _ in PROJ2_AHEAD + PROJ2_STEPS:
    PB2.setdefault((kind, blocks[0]), 6 + len(PB2) % 2)
QKSC = [0.125] * 3 + [1.0] * 3 + [32 ** -0.5] * 2 + [1.0] * 2 + [0.125] * 3 + [1.0] * 3
SB_GROUPS = (range(0, 4), range(4, N_SB))
SB_OUT = (2, 3, 0)
UNIT_HEAD = list(range(N_DIL)) + [h for d in range(N_DIFF) for h in (None, N_DIL + d)]


def program(nc, I, out, table):
    ctx = ExitStack()
    with ctx:
        def sb(name, shape, scope=ctx, dt=F32):
            return scope.enter_context(nc.sbuf_tensor(name, shape, dt))

        M = Marks(nc, ctx, table)
        done, at = M.done, M.at

        ring = sb("weight_ring", [P, RING, 2048])
        X = sb("residual", [P, 2, D])
        KB = sb("const_base", [P, C_END])
        vec = sb("vectors", [P, 3, P])
        vT = sb("vectors_T", [P, 3, P])
        CS = sb("silu_c", [P, 16])
        ada = sb("ada", [P, 24, 2])
        adag = sb("ada_gain", [P, KD, 2])
        stat = sb("stat", [P, 64])
        eps = sb("eps", [P, 4])
        ada_row = sb("ada_rows", [34, 256])
        gain_row = sb("gain_row", [P, D])
        ytmp = sb("scaled_out", [P, 2, 512])
        lam_in = sb("lambda_in", [P, 2, 128])
        lamv = sb("lambda", [P, 2, 8])
        first = ctx.enter_context(ExitStack())
        XC = sb("residual_ctx", [P, 2, D], first)
        SG = sb("gated", [P, KD, TT], first)
        XN = SG[:, :, :].rearrange("p a b -> p (a b)").rearrange("p (t d) -> p t d", t=4)
        hT = sb("hT", [P, KD, TT], first)
        GB = hT[:, :, :].rearrange("p a b -> p (a b)").rearrange("p (v d) -> p v d", v=4)
        gate_diag = sb("gate_diag", [P, 2, 512], first)
        bsrow = sb("b_s_row", [1, 1024], first)[:, :].rearrange("p (l n) -> p l n", l=2)
        arena = sb("arena", [P, 19320], first)
        room = [0]

        def carve(n):
            a = room[0]
            room[0] += n
            assert room[0] <= 19320
            return arena[:, a:a + n]

        w_uq = carve(768).rearrange("p (j n) -> p j n", j=2)
        w_uqs = carve(256).rearrange("p (j n) -> p j n", j=2)
        w_ukv = carve(512)
        w_pw = carve(512).rearrange("p (j n) -> p j n", j=2)
        w_fo = carve(512).rearrange("p (j n) -> p j n", j=2)
        w_s = carve(512).rearrange("p (g n) -> p g n", g=4)
        wsT = carve(512).rearrange("p (g n) -> p g n", g=4)
        w_krs = carve(256).rearrange("p (k n) -> p k n", k=8)
        sgu_row = carve(512).rearrange("p (a n) -> p a n", a=2)
        qp = carve(1024).rearrange("p (j n) -> p j n", j=2)
        kvp = carve(512)
        sq = carve(1536).rearrange("p (j n) -> p j n", j=3)
        rq = carve(1024).rearrange("p (j n) -> p j n", j=2)
        krot = carve(512)
        CG = carve(4 * SEGP).rearrange("p (j s n) -> p j s n", j=2, s=2)
        cacc = carve(1024).rearrange("p (j n) -> p j n", j=2)
        csg = carve(1024).rearrange("p (j n) -> p j n", j=2)
        fT = carve(1024).rearrange("p (j n) -> p j n", j=2)
        FA = carve(2048).rearrange("p (t j n) -> p t j n", t=4, j=2)
        U = carve(1024).rearrange("p (j n) -> p j n", j=2)
        VN = carve(1024).rearrange("p (t n) -> p t n", t=4)
        Q = carve(2048).rearrange("p (h n) -> p h n", h=4)
        K = FA.rearrange("p t j n -> p (t j n)").rearrange("p (h n) -> p h n", h=4)
        V = fT.rearrange("p j n -> p (j n)").rearrange("p (t n) -> p t n", t=4)
        Pm = [w.rearrange("p t n -> p (t n)").rearrange("p (b n) -> p b n", b=2) for w in (VN, sq[:, 0:2, :])]
        PT = [w.rearrange("p j n -> p (j n)").rearrange("p (k n) -> p k n", k=4) for w in (U, csg)]
        ropet = gate_diag[:, 0, :]
        first.close()
        XN2 = sb("x_scaled_2", [P, 2, D])
        HH = sb("input_high", [P, KD, T], dt=F32R)
        HL = sb("input_low", [P, KD, T], dt=F32R)
        HBH = sb("hidden_high", [P, 2, T], dt=F32R)
        HBL = sb("hidden_low", [P, 2, T], dt=F32R)
        hbuf = sb("hidden", [P, 2, T])
        sgate = sb("silu_gate", [P, 2, T])
        alibi = sb("alibi", [P, 10, 384])
        FQ = sb("qk_feature_major", [P, 16, T])
        FV = sb("v_token_major", [P, 2, D])
        ZE = sb("mixer_maps", [P, 6, 384])
        SS, S2 = ZE[:, 0:4, :], ZE[:, 4:6, :]
        PT2 = sb("weights_T", [P, 2, 384])
        ZP = sb("softplus", [P, 6, 384])
        OB = sb("softmax_heads_out", [P, 5, T])
        OB2 = OB[:, 3:5, :]
        WH = sb("weights_high", [P, SPLIT, 1024], dt=F32R)
        WL = sb("weights_low", [P, SPLIT, 1024], dt=F32R)

        ident, ones = KB[:, C_ID:C_ID + P], KB[:, C_ONES:C_ONES + P]
        heads2, ntri, negones = (KB[:, c:c + P] for c in (C_H2, C_NTRI, C_NONE))
        dft_d = KB[:, C_DD:C_DD + 256]
        dft_n = KB[:, C_DN:C_DN + 1024].rearrange("p (s t n) -> p s t n", s=2, t=2)
        full, gap = KB[:, C_FULL:C_FULL + 384], KB[:, C_GAP:C_GAP + 384]
        rcos, rsin = KB[NOPE:QK, C_ROPE:C_ROPE + T], KB[NOPE:QK, C_ROPE + T:C_ROPE + 2 * T]

        B = [ctx.enter_context(nc.psum_tensor(f"bank{i}", [P, 512], F32)) for i in range(8)]

        slot_loaded = [M.sem(f"slot{i}_loaded") for i in range(RING)]
        s_silu, s_h, s_hh, s_hl = (M.sem(n) for n in ("silu_ready", "hidden_ready", "hidden_high_ready", "hidden_low_ready"))
        s_high, s_low, s_used = (M.sem(n) for n in ("unit_high_ready", "unit_low_ready", "unit_used"))

        def xt(t):
            return X[:, t, :] if t < 2 else XC[:, t - 2, :]

        def colslot(w, c0, n):
            return w.rearrange("(k p) n -> p k n", p=P)[:, :, c0:c0 + n], n

        SLOTS = []
        base = {}
        two_part = set()

        def add(name, items):
            base[name] = len(SLOTS)
            SLOTS.extend(items)

        def rows2(w, s):
            return w.rearrange("(s r p) n -> s p r n", r=2, p=P)[s], 0

        def ada_slots(L):
            return [colslot(I["w_ada"][L], 256 * s, 256) for s in range(ADA_SLOTS)]

        for L in range(2):
            if L == 0:
                add(("ada", 0), ada_slots(0))
            add(("win", L), [colslot(I["w_in"][L], c, n) for c, n in WIN_SLOTS])
            if L == 0:
                add(("ada", 1), ada_slots(1))
            add(("wout", L), [rows2(I["w_out"][L], s) for s in WOUT_ORDER[L]])
        SITES = [("ffn", 0), ("mix", 0), ("ffn", 1), ("ffn", 2), ("mix", 1), ("ffn", 3)]
        for kind, n in SITES:
            if kind == "ffn":
                add(("ffn", n), [None] * FFN_SLOTS)
            else:
                w = I["w_in_2"][n]
                two_part.update(len(SLOTS) + s for s, ((b0, b1), _, _) in enumerate(MIX_SLOTS) if b1 != b0 + 1)
                add(("win2", n), [colslot(w, P * b0, 256) if b1 == b0 + 1 else ((colslot(w, P * b0, P)[0], colslot(w, P * b1, P)[0]), P) for (b0, b1), _, _ in MIX_SLOTS])
                add(("wout2", n), [rows2(I["w_out_2"][n], s) for s in range(4)])

        UNITS2, unit_base = [], []
        for kind, n in SITES:
            unit_base.append(len(UNITS2))
            if kind == "ffn":
                b0 = base[("ffn", n)]
                for q in range(FFN_PAIRS):
                    m = b0 + 3 * q
                    UNITS2 += [(m, 0, "c"), (m + 1, 0, "c")] + ([(m - 1, 1, "r")] if q else []) + [(m, 1, "c"), (m + 1, 1, "c"), (m + 2, 0, "r")]
                UNITS2.append((b0 + FFN_SLOTS - 1, 1, "r"))
            else:
                UNITS2 += [(base[("win2", n)] + q // 2, q % 2, "c") for q in range(24)] + [(base[("wout2", n)] + q // 2, q % 2, "r") for q in range(8)]
        unit_base.append(len(UNITS2))
        last_unit = {m: U for U, (m, _, _) in enumerate(UNITS2)}

        LAST = {}
        for L in range(2):
            for s in range(ADA_SLOTS):
                LAST[base[("ada", L)] + s] = ("ada_rows", L, s)
            ends = [("q", 1), ("krs",), ("a", 1), ("g", 1), ("f", 1), ("u", 1), ("v", 3 if L == 0 else 1)] + [("gate", 2 * s + 1) for s in range(4)]
            for s, e in enumerate(ends):
                LAST[base[("win", L)] + s] = ("proj", L) + e
            for s in range(4):
                LAST[base[("wout", L)] + s] = ("wout_used", L, s) if s < 3 else ("y_ready", "b1", L, 3 if L == 0 else 1, 1)
        def slot(n):
            return ring[:, n % RING, :]

        def filled(n):
            return slot_loaded[n % RING], 16 * (n // RING + 1 + sum(m <= n and m % RING == n % RING for m in two_part))

        def cols(n, w=256):
            return slot(n)[:, 0:8 * w].rearrange("p (k n) -> p k n", k=8)

        def rows(n):
            return slot(n).rearrange("p (r n) -> p r n", r=2)

        def step(v, j, per):
            return v if j is None else j * per + v

        def y_out(i, t, hf):
            return (s_used, unit_base[i + 1]) if (t, hf) == (1, 1) else at("y_ready", "site", i, t, hf)

        def unit_source(U):
            n, half, kind = UNITS2[U]
            return cols(n)[:, :, half * P:(half + 1) * P] if kind == "c" else rows(n)[:, half, :]

        def unit_in(W, U):
            w = W[:, U % SPLIT, :]
            return w.rearrange("p (k n) -> p k n", k=8) if UNITS2[U][2] == "c" else w

        def at_slot(m, j=None):
            sem, count = filled(m)
            return sem, step(count, j, 16)

        block = ctx.enter_context(nc.Block())

        @block.sync
        def _(sp):
            def fill(n, src, w):
                if n - RING in last_unit:
                    sp.wait_ge(s_low, last_unit[n - RING] + 1)
                elif n >= RING:
                    sp.wait_ge(*at(*LAST[n - RING]))
                if n in two_part:
                    for q in range(2):
                        sp.dma_start(cols(n)[:, :, q * P:(q + 1) * P], src[q]).then_inc(slot_loaded[n % RING], 16)
                    return
                dst = cols(n, w) if w else rows(n)
                sp.dma_start(dst, src).then_inc(slot_loaded[n % RING], 16)

            sp.dma_start(vec[:, 0, :], I["k_vec1"][0]).then_inc(M.sem("vec_loaded"), 16)
            sp.dma_start(vec[:, 1, :], I["k_vec1"][1]).then_inc(M.sem("vec_loaded"), 16)
            sp.dma_start(vec[:, 2, :], I["k_vec2"]).then_inc(M.sem("vec_loaded"), 16)
            sp.dma_start(KB[:, 0:C_DD], I["k_base"][:, 0:C_DD]).then_inc(M.sem("vec_loaded"), 16)
            n_first = base[("ffn", 0)]
            for n in range(n_first):
                fill(n, *SLOTS[n])

            def ffn(idx):
                g = I["w_ffn_gate_2"][idx // 2, idx % 2].rearrange("(k p) (i n) -> i p k n", p=P, n=256)
                u = I["w_ffn_up_2"][idx // 2, idx % 2].rearrange("(k p) (i n) -> i p k n", p=P, n=256)
                d = I["w_ffn_down_2"][idx // 2, idx % 2].rearrange("(i r p) n -> i p r n", r=2, p=P)
                b0 = base[("ffn", idx)]
                for q, src in enumerate((g, u, d)):
                    fill(b0 + q, src[0], 0 if q == 2 else 256)
                with sp.Fori(0, FFN_PAIRS - 1) as j:
                    for q, src in enumerate((g, u, d)):
                        n = b0 + 3 + q
                        sp.wait_ge(s_low, j * 6 + (last_unit[n - RING] + 1))
                        s = src[bass.ds(j + 1, 1)]
                        dst = cols(n) if q < 2 else rows(n)
                        sp.dma_start(dst, s.rearrange("i p a n -> p (i a) n")).then_inc(slot_loaded[n % RING], 16)

            for kind, n in SITES:
                if kind == "ffn":
                    ffn(n)
                else:
                    for s in range(base[("win2", n)], base[("wout2", n)] + 4):
                        fill(s, *SLOTS[s])
            for t in range(2):
                sp.wait_ge(*at("x_updated", "site", 5, t, 0))
                sp.wait_ge(*at("x_updated_dve", "site", 5, t, 1))
                sp.dma_start(out[0].rearrange("(t p) d -> t p d", p=P)[t], X[:, t, :]).then_inc(M.sem("stored"), 16)
            sp.wait_ge(M.sem("stored"), 32)

        SW = 7 * 16

        @block.gpsimd
        def _(pool):
            def load(dst, src, stage):
                pool.dma_start(dst, src).then_inc(M.sem(stage), 16)

            pool.memset(eps[:, 0:1], RMS_EPS)
            pool.memset(eps[:, 1:2], LN_EPS)
            pool.memset(eps[:, 2:3], RMS_EPS * QK)
            pool.memset(eps[:, 3:4], 4 * RMS_EPS)
            pool.memset(CG, 0.0).then_inc(*done("set_up"))
            pool.wait_ge(*at("ada_rows", 0, 6))
            load(KB[:, C_DD:], I["k_base"][:, C_DD:], "base_loaded")
            load(lam_in[:, :, :], I["diff_lambda_2"].rearrange("l a b -> (l a b)").rearrange("(l n) -> l n", l=2).partition_broadcast(P), "base_loaded")
            load(bsrow, I["b_s"].rearrange("l g n -> (l g n)").rearrange("(a l n) -> a l n", a=1, l=2), "base_loaded")

            def small_weights(L):
                load(w_uq, I["w_uq"][L].rearrange("(j p) n -> p j n", p=P), "small_loaded")
                load(w_ukv, I["w_ukv"][L], "small_loaded")
                load(w_pw, I["w_pw"][L].rearrange("(j p) n -> p j n", p=P), "small_loaded")
                load(w_fo, I["w_fourier"][L].rearrange("(j p) n -> p j n", p=P), "small_loaded")
                load(w_s, I["w_s"][L].rearrange("g i j -> i g j"), "small_loaded")
                load(sgu_row[:, 0, :], I["sgu_ln_g"][L].partition_broadcast(P), "small_loaded")
                load(sgu_row[:, 1, :], I["sgu_ln_b"][L].partition_broadcast(P), "small_loaded")

            def layer(L):
                nq = TT if L == 0 else T
                if L:
                    pool.wait_ge(*at("conv_out", 0, 1))
                small_weights(L)
                pool.wait_ge(M.sem("small_loaded"), SW * (L + 1))
                for j in range(2):
                    for half in range(2):
                        src = w_uq[:, j, :].rearrange("p (h n) -> p h n", h=4)[:, :, NOPE:QK].rearrange("p h (a x f) -> p h a x f", a=2, x=2)[:, :, :, 1 - half, :]
                        dst = w_uqs[:, j, :].rearrange("p (h a x f) -> p h a x f", h=4, a=2, x=2)[:, :, :, half, :]
                        last = pool.tensor_copy(dst, src)
                last.then_inc(*done("uq_swapped", L))
                n = base[("win", L)] + 1
                pool.wait_ge(*filled(n))
                for half in range(2):
                    src = cols(n, 160)[:, :, P:P + ROPE].rearrange("p k (a x f) -> p k a x f", a=2, x=2)[:, :, :, 1 - half, :]
                    dst = w_krs.rearrange("p k (a x f) -> p k a x f", a=2, x=2)[:, :, :, half, :]
                    last = pool.tensor_copy(dst, src)
                last.then_inc(*done("kr_swapped", L))
                for j in range(2):
                    pool.wait_ge(*at("a_ready", L, j))
                    pool.wait_ge(*at("conv_gate_ready", L, j))
                    for s in range(nq // T):
                        last = pool.tensor_tensor(CG[:, j, s, PAD:PAD + T], CG[:, j, s, PAD:PAD + T], csg[:, j, s * T:(s + 1) * T], ALU.mult)
                    last.then_inc(*done("glu_ready", L, j))
                for t in range(nq // P):
                    pool.wait_ge(*at("v_normalised", L, t))
                    pool.tensor_tensor(VN[:, t, :], VN[:, t, :], sgu_row[:, 0, :], ALU.mult).then_inc(*done("v_gained", L, t))
                    pool.wait_ge(*at("v_gained", L, t))
                    pool.tensor_tensor(VN[:, t, :], VN[:, t, :], sgu_row[:, 1, :], ALU.add).then_inc(*done("v_ready", L, t))
                for m in range(2):
                    pool.wait_ge(*at("u_ready", L, m))
                    pool.wait_ge(*at("sg_ready", L, 6 + m))
                    pool.tensor_tensor(U[:, m, 0:nq], U[:, m, 0:nq], SG[:, 6 + m, 0:nq], ALU.mult).then_inc(*done("u_gated", L, m))
                pool.wait_ge(*at("u_gated", L, 1))
                pool.wait_ge(*at("kr_ready", L))
                pool.wait_ge(*at("fourier_tok", L, 1))
                for h in range(HEADS):
                    last = pool.tensor_copy(K[NOPE:QK, h, :], krot[NOPE:QK, :])
                last.then_inc(*done("k_rope_ready", L))
                pool.wait_ge(*at("k_rope_ready", L))
                for t in range(nq // P):
                    for n in range(2):
                        pool.wait_ge(*at("out_scaled", "b1", L, t, n))
                        x = xt(t)[:, n * 512:(n + 1) * 512]
                        pool.tensor_tensor(x, x, ytmp[:, n, :], ALU.add).then_inc(*done("x_updated", "b1", L, t, n))

            layer(0)
            layer(1)
            pool.wait_ge(*at("final_scaled", 1))
            load(gain_row[:, :], I["norm_gains_2"][0, 1].partition_broadcast(P), "gain_loaded")
            pool.wait_ge(*at("conv_out", 1, 1))
            load(alibi[:, :, :].rearrange("p h n -> p (h n)"), I["k_alibi"], "alibi_loaded")
            for i, (kind, n) in enumerate(SITES):
                if kind == "mix":
                    pool.wait_ge(M.sem("base_loaded"), 48)
                    for h in range(N_SB):
                        pool.wait_ge(*at("softplus_ready", n, h))
                        pool.tensor_tensor(ZP[:, h, :], ZP[:, h, :], full, ALU.mult).then_inc(*done("softplus_masked", n, h))
                for t in range(2):
                    pool.wait_ge(*at("out_scaled", "site", i, t, 0))
                    pool.tensor_tensor(X[:, t, 0:512], X[:, t, 0:512], ytmp[:, 0, :], ALU.add).then_inc(*done("x_updated", "site", i, t, 0))
                if i < 5:
                    pool.wait_ge(*at("out_scaled", "site", i, 1, 1))
                    nxt = i + 1
                    load(gain_row[:, :], I["norm_gains_2"][nxt // 3, 2 * (nxt % 3) + 1].partition_broadcast(P), "gain_loaded")

        @block.scalar
        def _(act):
            A = act.activation
            for t in range(2):
                act.dma_start(X[:, t, :], I["x"][0].rearrange("(t p) d -> t p d", p=P)[t]).then_inc(M.sem("x_loaded"), 16)
            for t in range(2):
                act.dma_start(XC[:, t, :], I["ctx"][0].rearrange("(t p) d -> t p d", p=P)[t]).then_inc(M.sem("x_loaded"), 16)
            act.dma_start(gain_row[:, :], I["final_g"].partition_broadcast(P)).then_inc(M.sem("final_loaded"), 16)
            act.wait_ge(*at("vec_T", 0))
            A(CS[:, :], vT[:, 0, R_C:R_C + 16], ACT.Silu).then_inc(*done("silu_c"))
            act.wait_ge(M.sem("x_loaded"), 64)
            act.wait_ge(*at("set_up"))

            def ada_copy(L, s):
                act.wait_ge(*at("ada_rows", L, s))
                A(ada_row[ADA_AT[s % 2], :], B[6][ADA_AT[s % 2], 0:T], ACT.Copy).then_inc(*done("ada_copied", L, s))

            def norm(site, tiles):
                for t in tiles:
                    if site == ("b1", 1):
                        for hf in range(2):
                            act.wait_ge(*at("x_updated", "b1", 0, t, hf))
                    A(XN[:, t, :], xt(t), ACT.Square, accum_out=stat[:, t:t + 1]).then_inc(*done("sum_squares", *site, t))
                    act.wait_ge(*at("sum_squares", *site, t))
                    A(stat[:, 8 + t:9 + t], stat[:, t:t + 1], ACT.Sqrt, bias=eps[:, 0:1], scale=1.0 / D).then_inc(*done("rms_ready", *site, t))
            def layer(L):
                nq = TT if L == 0 else T
                norm(("b1", L), range(4))
                if L == 0:
                    for s in range(ADA_SLOTS):
                        ada_copy(0, s)
                for c in range(0, KD, 2):
                    act.wait_ge(*at("x_T", "b1", L, c))
                    act.wait_ge(*at("ada_ready", L))
                    A(hT[:, c, 0:T], B[c % 4][:, 0:T], ACT.Identity, scale=adag[:, c, 0:1], bias=ada[:, c, 0:1])
                    A(hT[:, c, T:TT], B[c % 4][:, T:TT], ACT.Identity, scale=adag[:, c, 1:2], bias=ada[:, c, 1:2]).then_inc(*done("hT_ready_act", "b1", L, c))
                for j in range(2):
                    act.wait_ge(*at("proj", L, "q", j))
                    A(qp[:, j, 0:nq], B[PB[L]["q", j]][:, 0:nq], ACT.Copy)
                    A(sq[:, j, 0:nq], B[PB[L]["q", j]][:, 0:nq], ACT.Square).then_inc(*done("q_part_ready", L, j))
                act.wait_ge(*at("proj", L, "kv"))
                A(kvp, B[PB[L]["kv"]][:, :], ACT.Copy)
                A(sq[:, 2, :], B[PB[L]["kv"]][:, :], ACT.Square).then_inc(*done("kv_part_ready", L))
                for j in range(2):
                    act.wait_ge(*at("proj", L, "a", j))
                    if L:
                        act.wait_ge(*at("conv_tap", L - 1, j, CONV_K - 1))
                    else:
                        act.wait_ge(*at("set_up"))
                    src = B[PB[L]["a", j]][:, 0:nq].rearrange("p (s n) -> p s n", n=T)
                    A(CG[:, j, 0:nq // T, PAD:PAD + T], src, ACT.Copy).then_inc(*done("a_ready", L, j))
                act.wait_ge(*at("q_square_sum", L))
                A(rq[:, 0, 0:nq], B[6][:, 0:nq], ACT.Sqrt, bias=eps[:, 2:3], scale=float(QK) / 256).then_inc(*done("q_root", L))
                act.wait_ge(*at("kv_square_sum", L))
                A(rq[:, 1, :], B[7][:, :], ACT.Sqrt, bias=eps[:, 0:1], scale=1.0 / 128).then_inc(*done("kv_root", L))
                for j in range(2):
                    act.wait_ge(*at("proj", L, "g", j))
                    A(csg[:, j, 0:nq], B[PB[L]["g", j]][:, 0:nq], ACT.Sigmoid).then_inc(*done("conv_gate_ready", L, j))
                for j in range(2):
                    act.wait_ge(*at("proj", L, "f", j))
                    A(fT[:, j, 0:nq], B[PB[L]["f", j]][:, 0:nq], ACT.Copy).then_inc(*done("f_ready", L, j))
                for j in range(2):
                    act.wait_ge(*at("proj", L, "u", j))
                    A(U[:, j, 0:nq], B[PB[L]["u", j]][:, 0:nq], ACT.Copy).then_inc(*done("u_ready", L, j))
                act.wait_ge(*at("v_aggr", L, nq // P - 1))
                A(stat[:, 40:40 + nq // P], stat[:, 33:33 + 2 * (nq // P):2], ACT.Sqrt, bias=eps[:, 1:2]).then_inc(*done("v_root", L))
                for j in range(8):
                    act.wait_ge(*at("proj", L, "gate", j))
                    A(SG[:, j, 0:nq], B[PB[L]["gate", j]][:, 0:nq], ACT.Silu).then_inc(*done("sg_ready", L, j))
                for v in range(nq // T):
                    for hf in range(2):
                        act.wait_ge(*at("gate_rows", L, v, hf))
                        A(GB[:, v, hf * 512:(hf + 1) * 512], B[(2 * v + hf) % 4][:, :], ACT.Copy).then_inc(*done("gate_row_ready", L, v, hf))
                for h in range(HEADS):
                    act.wait_ge(*at("q_heads", L, h))
                    act.wait_ge(*at("glu_ready", L, 1))
                    A(Q[0:NOPE, h, 0:nq], B[h % 2][0:NOPE, 0:nq], ACT.Copy)
                    if L == 0:
                        A(Q[NOPE:QK, h, T:TT], B[h % 2][NOPE:QK, T:TT], ACT.Copy)
                    A(csg[NOPE:QK, h // 2, (h % 2) * T:(h % 2 + 1) * T], B[h % 2][NOPE:QK, 0:T], ACT.Copy).then_inc(*done("q_copied", L, h))
                for h in range(HEADS):
                    act.wait_ge(*at("k_heads", L, h))
                    act.wait_ge(*at("fourier_tok", L, 1))
                    A(K[0:NOPE, h, :], B[h % 2][0:NOPE, :], ACT.Copy).then_inc(*done("k_copied", L, h))
                def weights(i):
                    seg, h, par = UNITS[i] + (i % 2,)
                    keys = TT if seg == 0 else T
                    for qt in range(2):
                        act.wait_ge(*at("neg_max", L, seg, h, qt))
                        A(Pm[par][:, qt, 0:keys], B[qt][:, 0:keys], ACT.Exp, bias=stat[:, 16 + 2 * par + qt:17 + 2 * par + qt], accum_out=stat[:, 20 + 2 * par + qt:21 + 2 * par + qt]).then_inc(*done("exp_ready", L, seg, h, qt))

                def transposed(i):
                    seg, h, par = UNITS[i] + (i % 2,)
                    keys = TT if seg == 0 else T
                    for qt in range(2):
                        act.wait_ge(*at("p_T", L, seg, h, qt))
                        A(PT[par][:, 0:keys // P, qt * P:(qt + 1) * P], B[2 + qt][:, 0:keys].rearrange("p (k n) -> p k n", n=P), ACT.Copy).then_inc(*done("pT_ready", L, seg, h, qt))

                UNITS = [(seg, h) for seg in range(nq // T) for h in range(HEADS)]
                weights(0)
                for i in range(len(UNITS)):
                    if i + 1 < len(UNITS):
                        weights(i + 1)
                    if L == 0:
                        for sl in ADA_STEP[i]:
                            ada_copy(1, sl)
                    transposed(i)
                for j in range(2):
                    act.wait_ge(*at("conv_centred", L, j))
                    A(sq[:, j, 0:nq], cacc[:, j, 0:nq], ACT.Square).then_inc(*done("conv_square", L, j))
                A(stat[:, 60:61], eps[:, 0:1], ACT.Sqrt)
                act.wait_ge(*at("conv_var", L))
                A(rq[:, 0, 0:nq], B[1][:, 0:nq], ACT.Sqrt, bias=eps[:, 1:2], scale=1.0 / 256).then_inc(*done("conv_root", L))
                A(stat[:, 61:62], eps[:, 0:1], ACT.Silu)
                for j in range(2):
                    act.wait_ge(*at("conv_normalised", L, j))
                    A(csg[:, j, 0:nq], cacc[:, j, 0:nq], ACT.Silu, scale=vT[:, L, R_CLG + j:R_CLG + j + 1], bias=vT[:, L, R_CLB + j:R_CLB + j + 1]).then_inc(*done("conv_act", L, j))

            def high(U, j=None):
                act.wait_ge(*at_slot(UNITS2[U][0], j))
                if U >= SPLIT:
                    act.wait_ge(s_used, step(U - SPLIT + 1, j, 6))
                A(unit_in(WH, U), unit_source(U), ACT.Copy).then_inc(s_high, 1)

            layer(0)
            layer(1)
            A(stat[:, 60:61], eps[:, 0:1], ACT.Sqrt)
            act.wait_ge(*at("conv_out", 1, 1))
            for unit in range(3):
                high(unit)
            for t in range(2):
                for hf in range(2):
                    act.wait_ge(*at("x_updated", "b1", 1, t, hf))
                A(XN2[:, t, :], X[:, t, :], ACT.Square, accum_out=stat[:, t:t + 1]).then_inc(*done("final_squares", t))
                act.wait_ge(*at("final_squares", t))
                A(stat[:, 8 + t:9 + t], stat[:, t:t + 1], ACT.Sqrt, bias=eps[:, 0:1], scale=1.0 / D).then_inc(*done("final_root", t))

            def site_norm(i):
                for t in range(2):
                    if i == 0:
                        act.wait_ge(*at("final_scaled", t))
                    else:
                        for hf in range(2):
                            act.wait_ge(*at("x_updated" if hf == 0 else "x_updated_dve", "site", i - 1, t, hf))
                    A(XN2[:, t, :], X[:, t, :], ACT.Square, accum_out=stat[:, t:t + 1]).then_inc(*done("sum_squares", "site", i, t))
                    act.wait_ge(*at("sum_squares", "site", i, t))
                    A(stat[:, 8 + t:9 + t], stat[:, t:t + 1], ACT.Sqrt, bias=eps[:, 0:1], scale=1.0 / D).then_inc(*done("rms_ready", "site", i, t))
                for b in range(4):
                    act.wait_ge(*at("x_T", "site", i, b))
                    for q in range(2):
                        c = 2 * b + q
                        r = 8 * i + c
                        last = A(HH[:, c, :], B[b][:, q * T:(q + 1) * T], ACT.Identity, scale=vT[:, 2, r:r + 1])
                    last.then_inc(*done("input_high", i, b))

            def site_tail(i):
                for t in range(2):
                    e, by = (eps[:, 3:4], 4.0 / D) if SITES[i][0] == "ffn" else (eps[:, 0:1], 1.0 / D)
                    for hf in range(2):
                        act.wait_ge(*y_out(i, t, hf))
                        A(XN2[:, hf, 0:512], B[4 + 2 * t + hf][:, :], ACT.Square, accum_out=stat[:, 10 + 2 * t + hf:11 + 2 * t + hf]).then_inc(*done("y_squares", i, t, hf))
                        if hf == 0:
                            act.wait_ge(*at("y_squares", i, t, 0))
                            A(stat[:, 26 + t:27 + t], stat[:, 10 + 2 * t:11 + 2 * t], ACT.Identity, bias=e, scale=by).then_inc(*done("y_squares", i, t, "scaled"))
                    act.wait_ge(*at("y_squares", i, t, 1))
                    A(stat[:, 28 + t:29 + t], stat[:, 11 + 2 * t:12 + 2 * t], ACT.Sqrt, bias=stat[:, 26 + t:27 + t], scale=by).then_inc(*done("y_root", i, t))

            def ffn(i, n):
                f0 = n * FFN_CHUNKS

                def silu(par, ready, free):
                    act.wait_ge(s_used, ready)
                    if free is not None:
                        act.wait_ge(s_h, free)
                    A(sgate[:, par, :], B[par][:, 0:T], ACT.Silu).then_inc(s_silu, 1)

                def hidden_high(par, ready, used, j=None):
                    act.wait_ge(s_h, ready)
                    if used is not None:
                        act.wait_ge(s_used, step(used + 1, j, 6))
                    A(HBH[:, par, :], hbuf[:, par, :], ACT.Copy).then_inc(s_hh, 1)

                a = unit_base[i]
                silu(0, a + 2, f0 if n else None)
                high(a + 6)
                hidden_high(0, f0 + 1, None)
                high(a + 7)
                silu(1, a + 4, f0 if n else None)
                high(a + 8)
                hidden_high(1, f0 + 2, None)
                high(a + 9)
                high(a + 10)

                def pair(a, f, j=None):
                    split = [U for U in range(a + 6, a + 12) if U < min(len(UNITS2), unit_base[i + 1] + 3)]
                    silu(0, step(a + 2, j, 6), step(f - 1, j, 2))
                    if split:
                        high(split[0], j)
                    hidden_high(0, step(f + 1, j, 2), a - 1, j)
                    for U in split[1:3]:
                        high(U, j)
                    silu(1, step(a + 5, j, 6), step(f, j, 2))
                    for U in split[3:4]:
                        high(U, j)
                    hidden_high(1, step(f + 2, j, 2), a + 2, j)
                    for U in split[4:]:
                        high(U, j)

                with act.Fori(0, FFN_PAIRS - 2) as j:
                    pair(a + 5, f0 + 2, j)
                pair(a + 5 + 6 * (FFN_PAIRS - 2), f0 + FFN_CHUNKS - 2)
                A(stat[:, 60:61], eps[:, 0:1], ACT.Sqrt)

            def mix(i, n):
                u0 = unit_base[i]

                def projected(unit, kind, blocks, tiles):
                    if 1 not in tiles:
                        return
                    b = blocks[0]
                    if kind == "qk" and b % 2 == 0:
                        act.wait_ge(s_used, u0 + unit + 1)
                        A(FQ[:, b, :], B[PB2["qk", b]][:, 0:T], ACT.Copy, scale=QKSC[b]).then_inc(*done("qk_ready_act", n, b))
                    for q in range(len(blocks)):
                        high(u0 + unit + q + SPLIT)

                def numerators(u):
                    act.wait_ge(*at("neg_max2", n, u))
                    for qt, (a, w) in enumerate(((0, P), (P, T))):
                        last = A(SS[:, u % 4, a:a + w], S2[:, u % 2, a:a + w], ACT.Exp, scale=-1.0, bias=stat[:, 16 + 2 * (u % 2) + qt:17 + 2 * (u % 2) + qt], accum_out=stat[:, 20 + 2 * (u % 2) + qt:21 + 2 * (u % 2) + qt])
                    last.then_inc(*done("exp2_ready", n, u))

                def transposed(h):
                    act.wait_ge(*at("p2_T", n, h))
                    A(PT2[:, h % 2, :], B[2 + h % 2][:, 0:384], ACT.Copy).then_inc(*done("pT2_ready", n, h))

                for product in PROJ2_AHEAD:
                    projected(*product)
                for u in range(len(UNIT_HEAD) + 1):
                    if u and UNIT_HEAD[u - 1] is not None:
                        transposed(UNIT_HEAD[u - 1])
                    if u < len(UNIT_HEAD):
                        numerators(u)
                    for product in PROJ2_STEPS[u:u + 1]:
                        projected(*product)
                for b in range(2):
                    act.wait_ge(*at("ob_ready", n, 3 + b))
                    A(sgate[:, b, :], OB2[:, b, :], ACT.Square).then_inc(*done("ob_square", n, b))
                    act.wait_ge(*at("ob_sum", n, b))
                    A(sgate[:, b, :], B[4 + b][:, T:TT], ACT.Sqrt, bias=eps[:, 0:1]).then_inc(*done("ob_root", n, b))
                for group in SB_GROUPS:
                    for h in group:
                        act.wait_ge(*at("z_ready", n, h))
                        A(ZE[:, h, :], B[h % 4][:, 0:384], ACT.Abs).then_inc(*done("z_abs", n, h))
                    for h in group:
                        act.wait_ge(*at("z_abs", n, h))
                        A(ZE[:, h, :], ZE[:, h, :], ACT.Exp, scale=-1.0).then_inc(*done("z_exp", n, h))
                    for h in group:
                        act.wait_ge(*at("z_exp", n, h))
                        A(ZE[:, h, :], ZE[:, h, :], ACT.Ln, bias=1.0).then_inc(*done("z_ln", n, h))
                for h in range(N_SB):
                    act.wait_ge(*at("log_weight", n, h))
                    A(ZP[:, h, :], ZE[:, h, :], ACT.Exp).then_inc(*done("weight_ready", n, h))
                A(stat[:, 60:61], eps[:, 0:1], ACT.Sqrt)
                for U in range(u0 + 24, u0 + 29):
                    high(U + SPLIT)

            for i, (kind, n) in enumerate(SITES):
                site_norm(i)
                for unit in range(3, SPLIT):
                    high(unit_base[i] + unit)
                if i == 1:
                    for m in range(2):
                        act.wait_ge(*at("lambda_sums", m))
                        A(lamv[:, m, 2:4], lamv[:, m, 0:2], ACT.Exp).then_inc(*done("lambda_exp", m))
                (ffn if kind == "ffn" else mix)(i, n)
                site_tail(i)

        @block.vector
        def _(dve):
            TS, STT, TTn, CP = dve.tensor_scalar, dve.scalar_tensor_tensor, dve.tensor_tensor, dve.tensor_copy
            dve.wait_ge(*at("vec_transposed"))
            CP(vT[:, :, :], B[0][:, 0:384].rearrange("p (b n) -> p b n", b=3)).then_inc(*done("vec_T", 0))

            def scale_rows(site, tiles):
                for t in tiles:
                    dve.wait_ge(*at("rms_ready", *site, t))
                    dve.reciprocal(stat[:, 12 + t:13 + t], stat[:, 8 + t:9 + t]).then_inc(*done("inverse", "rms", *site, t))
                    dve.wait_ge(*at("inverse", "rms", *site, t))
                    TS(XN[:, t, :] if site[0] == "b1" else XN2[:, t, :], xt(t), stat[:, 12 + t:13 + t], None, ALU.mult).then_inc(*done("x_scaled", *site, t))

            def modulation(L):
                dve.wait_ge(*at("ada_T", L, ADA_SLOTS - 1))
                TTn(ada[:, :, :], B[7][:, 0:48].rearrange("p (b v) -> p b v", v=2), vT[:, L, 0:24].unsqueeze(2).to_broadcast([P, 24, 2]), ALU.add).then_inc(*done("ada_biased", L))
                dve.wait_ge(*at("ada_biased", L))
                STT(adag[:, :, :], ada[:, 8:16, :], 1.0, vT[:, L, R_NORM:R_NORM + 8].unsqueeze(2).to_broadcast([P, 8, 2]), ALU.add, ALU.mult).then_inc(*done("ada_ready", L))

            def layer(L):
                nq = TT if L == 0 else T
                nt = nq // P
                scale_rows(("b1", L), range(4))
                if L == 0:
                    modulation(0)
                dve.wait_ge(*at("ada_ready", L))
                for c in range(1, KD, 2):
                    dve.wait_ge(*at("x_T", "b1", L, c))
                    TS(hT[:, c, 0:T], B[c % 4][:, 0:T], adag[:, c, 0:1], ada[:, c, 0:1], ALU.mult, ALU.add)
                    TS(hT[:, c, T:TT], B[c % 4][:, T:TT], adag[:, c, 1:2], ada[:, c, 1:2], ALU.mult, ALU.add).then_inc(*done("hT_ready_dve", "b1", L, c))
                dve.wait_ge(*at("ws_transposed", L))
                CP(wsT, B[5][:, :].rearrange("p (g n) -> p g n", g=4)).then_inc(*done("wsT_ready", L))
                dve.wait_ge(*at("proj", L, "kr"))
                dve.wait_ge(M.sem("base_loaded"), 48)
                TTn(krot[NOPE:QK, 0:T], B[PB[L]["kr"]][NOPE:QK, 0:T], rcos, ALU.mult).then_inc(*done("kr_cos", L))
                CP(krot[NOPE:QK, T:TT], B[PB[L]["kr"]][NOPE:QK, T:TT]).then_inc(*done("kr_copied", L))
                dve.wait_ge(*at("proj", L, "krs"))
                TTn(ropet[NOPE:QK, 0:T], B[PB[L]["krs"]][NOPE:QK, 0:T], rsin, ALU.mult).then_inc(*done("kr_sin", L))
                dve.wait_ge(*at("kr_cos", L))
                dve.wait_ge(*at("kr_sin", L))
                TTn(krot[NOPE:QK, 0:T], krot[NOPE:QK, 0:T], ropet[NOPE:QK, 0:T], ALU.add).then_inc(*done("kr_ready", L))
                dve.wait_ge(*at("q_root", L))
                dve.reciprocal(rq[:, 0, 0:nq], rq[:, 0, 0:nq]).then_inc(*done("inverse", "q", L))
                dve.wait_ge(*at("kv_root", L))
                dve.reciprocal(rq[:, 1, :], rq[:, 1, :]).then_inc(*done("inverse", "kv", L))
                dve.wait_ge(*at("inverse", "q", L))
                for j in range(2):
                    dve.wait_ge(*at("q_part_ready", L, j))
                    STT(qp[:, j, 0:nq], qp[:, j, 0:nq], vT[:, L, R_QN + j:R_QN + j + 1], rq[:, 0, 0:nq], ALU.mult, ALU.mult).then_inc(*done("q_latent", L, j))
                dve.wait_ge(*at("inverse", "kv", L))
                STT(kvp, kvp, vT[:, L, R_KVN:R_KVN + 1], rq[:, 1, :], ALU.mult, ALU.mult).then_inc(*done("kv_latent", L))
                for t in range(nt):
                    dve.wait_ge(*at("fourier_feat", L, t))
                    CP(FA[:, t, :, :], B[6 + t % 2][:, :].rearrange("p (j n) -> p j n", j=2)).then_inc(*done("fa_ready", L, t))
                for t in range(nt):
                    dve.wait_ge(*at("proj", L, "v", t))
                    dve.bn_stats(stat[:, 44:50], B[PB[L]["v", t]][:, 0:256]).then_inc(*done("v_bn", L, t))
                    CP(VN[:, t, :], B[PB[L]["v", t]][:, 0:256]).then_inc(*done("v_copied", L, t))
                    dve.wait_ge(*at("v_bn", L, t))
                    dve.bn_aggr(stat[:, 32 + 2 * t:34 + 2 * t], stat[:, 44:50]).then_inc(*done("v_aggr", L, t))
                    dve.wait_ge(*at("v_aggr", L, t))
                for m in range(2):
                    dve.wait_ge(*at("fourier_tok", L, m))
                    CP(cacc[:, m, 0:nq], B[6 + m][:, 0:nq]).then_inc(*done("f_mixed", L, m))
                dve.wait_ge(*at("v_root", L))
                dve.reciprocal(stat[:, 40:40 + nt], stat[:, 40:40 + nt]).then_inc(*done("inverse", "v", L))
                dve.wait_ge(*at("inverse", "v", L))
                for t in range(nt):
                    dve.wait_ge(*at("v_copied", L, t))
                    TS(VN[:, t, :], VN[:, t, :], stat[:, 32 + 2 * t:33 + 2 * t], stat[:, 40 + t:41 + t], ALU.subtract, ALU.mult).then_inc(*done("v_normalised", L, t))
                for m in range(2):
                    dve.wait_ge(*at("fourier_out", L, m))
                    dve.wait_ge(*at("sg_ready", L, 4 + m))
                    STT(SG[:, 4 + m, 0:nq], B[4 + m][:, 0:nq], vT[:, L, R_BF + m:R_BF + m + 1], SG[:, 4 + m, 0:nq], ALU.add, ALU.mult).then_inc(*done("four_branch", L, m))
                conv = conv_steps(L)
                for _ in range(CONV_AHEAD):
                    next(conv)
                for m in range(2):
                    dve.wait_ge(*at("sgu_mixed", L, m))
                    dve.wait_ge(*at("u_gated", L, m))
                    TTn(SG[:, 6 + m, 0:nq], B[6 + m][:, 0:nq], U[:, m, 0:nq], ALU.mult).then_inc(*done("sgu_branch", L, m))
                for v in range(nq // T):
                    for hf in range(2):
                        if v:
                            dve.wait_ge(*at("gate_rows", L, v - 1, hf))
                        elif L:
                            dve.wait_ge(*at("gate_rows", 0, 1, hf))
                        for c in range(4):
                            last = TS(gate_diag[:, hf, c * P:(c + 1) * P], ident, ada[:, 16 + 4 * hf + c, v:v + 1], None, ALU.mult)
                        last.then_inc(*done("gate_diag_ready", L, v, hf))
                for h in range(HEADS):
                    dve.wait_ge(*at("q_copied", L, h))
                    qc = csg[NOPE:QK, h // 2, (h % 2) * T:(h % 2 + 1) * T]
                    TTn(Q[NOPE:QK, h, 0:T], qc, rcos, ALU.mult).then_inc(*done("q_cos", L, h))
                    dve.wait_ge(*at("q_swapped", L, h))
                    TTn(ropet[NOPE:QK, (h % 2) * T:(h % 2 + 1) * T], B[2 + h % 2][NOPE:QK, 0:T], rsin, ALU.mult).then_inc(*done("q_sin", L, h))
                    dve.wait_ge(*at("q_sin", L, h))
                    dve.wait_ge(*at("q_cos", L, h))
                    TTn(Q[NOPE:QK, h, 0:T], Q[NOPE:QK, h, 0:T], ropet[NOPE:QK, (h % 2) * T:(h % 2 + 1) * T], ALU.add).then_inc(*done("q_ready", L, h))
                for t in range(4):
                    dve.wait_ge(*at("v_heads", L, t))
                    CP(V[:, t, :], B[4 + t][:, 0:256]).then_inc(*done("v_heads_ready", L, t))
                UNITS = [(seg, h) for seg in range(nq // T) for h in range(HEADS)]

                def row_max(i):
                    seg, h, par = UNITS[i] + (i % 2,)
                    for qt in range(2):
                        dve.wait_ge(*at("scores", L, seg, h, qt))
                        dve.reduce_max(stat[:, 16 + 2 * par + qt:17 + 2 * par + qt], B[qt][:, 0:TT if seg == 0 else T], AXX, negate=True).then_inc(*done("neg_max", L, seg, h, qt))

                def row_scale(i):
                    seg, h, par = UNITS[i] + (i % 2,)
                    keys = TT if seg == 0 else T
                    for qt in range(2):
                        dve.wait_ge(*at("exp_ready", L, seg, h, qt))
                    dve.reciprocal(stat[:, 24 + 2 * par:26 + 2 * par], stat[:, 20 + 2 * par:22 + 2 * par]).then_inc(*done("inverse", "p", L, seg, h))
                    dve.wait_ge(*at("inverse", "p", L, seg, h))
                    for qt in range(2):
                        TS(Pm[par][:, qt, 0:keys], Pm[par][:, qt, 0:keys], stat[:, 24 + 2 * par + qt:25 + 2 * par + qt], None, ALU.mult).then_inc(*done("p_ready", L, seg, h, qt))

                def gated_heads(i):
                    seg, h = UNITS[i]
                    if h % 2:
                        dve.wait_ge(*at("attn", L, seg, h))
                        sl = SG[:, h // 2, seg * T:(seg + 1) * T]
                        TTn(sl, B[4 + h // 2][:, 0:T], sl, ALU.mult).then_inc(*done("attn_ready", L, h, seg))

                row_max(0)
                for i in range(len(UNITS)):
                    row_scale(i)
                    if i + 1 < len(UNITS):
                        row_max(i + 1)
                    if i:
                        gated_heads(i - 1)
                    for _ in range(-(-(CONV_K - CONV_AHEAD) // len(UNITS))):
                        next(conv, None)
                gated_heads(len(UNITS) - 1)
                for _ in conv:
                    pass
                if L == 0:
                    modulation(1)
                dve.wait_ge(*at("conv_mean", L))
                for j in range(2):
                    dve.wait_ge(*at("conv_tap", L, j, CONV_K - 1))
                    STT(cacc[:, j, 0:nq], B[0][:, 0:nq], -1.0 / 256, cacc[:, j, 0:nq], ALU.mult, ALU.add).then_inc(*done("conv_centred", L, j))
                dve.wait_ge(*at("conv_root", L))
                dve.reciprocal(rq[:, 0, 0:nq], rq[:, 0, 0:nq]).then_inc(*done("inverse", "conv", L))
                dve.wait_ge(*at("inverse", "conv", L))
                for j in range(2):
                    dve.wait_ge(*at("conv_square", L, j))
                    dve.wait_ge(*at("conv_centred", L, j))
                    TTn(cacc[:, j, 0:nq], cacc[:, j, 0:nq], rq[:, 0, 0:nq], ALU.mult).then_inc(*done("conv_normalised", L, j))
                for m in range(2):
                    dve.wait_ge(*at("conv_out", L, m))
                    STT(SG[:, 2 + m, 0:nq], B[2 + m][:, 0:nq], vT[:, L, R_BPW + m:R_BPW + m + 1], SG[:, 2 + m, 0:nq], ALU.add, ALU.mult).then_inc(*done("conv_branch", L, m))
                if L:
                    for unit in range(3):
                        low(unit)
                for t in range(nt):
                    for hf in range(2):
                        dve.wait_ge(*at("y_ready", "b1", L, t, hf))
                        dve.wait_ge(*at("gate_row_ready", L, t // 2, hf))
                        if t:
                            dve.wait_ge(*at("x_updated", "b1", L, t - 1, hf))
                        elif L:
                            dve.wait_ge(*at("x_updated", "b1", 0, 3, hf))
                        TTn(ytmp[:, hf, :], B[YB[L][t, hf]][:, :], GB[:, t // 2, hf * 512:(hf + 1) * 512], ALU.mult).then_inc(*done("out_scaled", "b1", L, t, hf))

            def conv_steps(L):
                nseg = 2 if L == 0 else 1
                for k in range(CONV_K):
                    for j in range(2):
                        accv = cacc[:, j, 0:nseg * T].rearrange("p (s n) -> p s n", n=T)
                        src = CG[:, j, 0:nseg, k:k + T]
                        w = vT[:, L, R_CW + 2 * k + j:R_CW + 2 * k + j + 1]
                        if k == 0:
                            dve.wait_ge(*at("glu_ready", L, j))
                            dve.wait_ge(*at("fourier_out", L, 1))
                            TS(accv, src, w, vT[:, L, R_CB + j:R_CB + j + 1], ALU.mult, ALU.add).then_inc(*done("conv_tap", L, j, k))
                        else:
                            dve.wait_ge(*at("conv_tap", L, j, k - 1))
                            STT(accv, src, w, accv, ALU.mult, ALU.add).then_inc(*done("conv_tap", L, j, k))
                    yield

            def low(U, j=None):
                dve.wait_ge(s_high, step(U + 1, j, 6))
                TTn(unit_in(WL, U), unit_source(U), unit_in(WH, U).bitcast(F32), ALU.subtract).then_inc(s_low, 1)

            layer(0)
            layer(1)
            dve.wait_ge(M.sem("final_loaded"), 16)
            for t in range(2):
                dve.wait_ge(*at("final_root", t))
                dve.reciprocal(stat[:, 12 + t:13 + t], stat[:, 8 + t:9 + t]).then_inc(*done("inverse", "final", t))
                dve.wait_ge(*at("inverse", "final", t))
                STT(X[:, t, :], X[:, t, :], stat[:, 12 + t:13 + t], gain_row[:, :], ALU.mult, ALU.mult).then_inc(*done("final_scaled", t))
            def lambdas():
                dve.wait_ge(M.sem("base_loaded"), 48)
                for m in range(2):
                    for q in range(2):
                        last = dve.tensor_tensor_reduce(out=S2[:, m, q * 32:q * 32 + 32], in0=lam_in[:, m, q * 64:q * 64 + 32], in1=lam_in[:, m, q * 64 + 32:q * 64 + 64], scale=1.0, scalar=0.0, op0=ALU.mult, op1=ALU.add, accum_out=lamv[:, m, q:q + 1])
                    last.then_inc(*done("lambda_sums", m))
                for m in range(2):
                    init = LAM_INIT[m]
                    dve.wait_ge(*at("lambda_exp", m))
                    STT(lamv[:, m, 4:5], lamv[:, m, 3:4], init, lamv[:, m, 2:3], ALU.subtract, ALU.subtract).then_inc(*done("lambda_ready", m))
                    TS(lamv[:, m, 5:6], vT[:, 2, R_SUB + m:R_SUB + m + 1], 1.0 - init, None, ALU.mult).then_inc(*done("sub_gain", m))

            def site_norm(i):
                if i == 0:
                    dve.wait_ge(*at("final_scaled", 1))
                scale_rows(("site", i), range(2))
                for b in range(4):
                    dve.wait_ge(*at("input_high", i, b))
                    for q in range(2):
                        c = 2 * b + q
                        r = 8 * i + c
                        last = STT(HL[:, c, :], B[b][:, q * T:(q + 1) * T], vT[:, 2, r:r + 1], HH[:, c, :].bitcast(F32), ALU.mult, ALU.subtract)
                    last.then_inc(*done("input_ready", i, b))

            def site_tail(i):
                kind, n = SITES[i]
                for t in range(2):
                    dve.wait_ge(*at("y_root", i, t))
                    sc = stat[:, 30 + t:31 + t]
                    dve.reciprocal(sc, stat[:, 28 + t:29 + t]).then_inc(*done("y_scale", "ready", i, t))
                    dve.wait_ge(*at("y_scale", "ready", i, t))
                    dve.wait_ge(M.sem("gain_loaded"), 16 * (i + 1))
                    for hf in range(2):
                        if t:
                            dve.wait_ge(*at("x_updated" if hf == 0 else "x_updated_dve", "site", i, 0, hf))
                        elif i:
                            dve.wait_ge(*at("x_updated" if hf == 0 else "x_updated_dve", "site", i - 1, 1, hf))
                        else:
                            dve.wait_ge(*at("x_updated", "b1", 1, 1, hf))
                        STT(ytmp[:, hf, :], B[4 + 2 * t + hf][:, :], sc, gain_row[:, hf * 512:(hf + 1) * 512], ALU.mult, ALU.mult).then_inc(*done("out_scaled", "site", i, t, hf))
                    dve.wait_ge(*at("out_scaled", "site", i, t, 1))
                    TTn(X[:, t, 512:D], X[:, t, 512:D], ytmp[:, 1, :], ALU.add).then_inc(*done("x_updated_dve", "site", i, t, 1))

            def ffn(i, n):
                f0 = n * FFN_CHUNKS

                def product(par, ready):
                    dve.wait_ge(s_silu, ready)
                    TTn(hbuf[:, par, :], B[par][:, T:TT], sgate[:, par, :], ALU.mult).then_inc(s_h, 1)

                def hidden_low(par, ready):
                    dve.wait_ge(s_hh, ready)
                    TTn(HBL[:, par, :], hbuf[:, par, :], HBH[:, par, :].bitcast(F32), ALU.subtract).then_inc(s_hl, 1)

                a = unit_base[i]
                product(0, f0 + 1)
                low(a + 6)
                hidden_low(0, f0 + 1)
                low(a + 7)
                product(1, f0 + 2)
                low(a + 8)
                hidden_low(1, f0 + 2)
                low(a + 9)
                low(a + 10)

                def pair(a, f, j=None):
                    split = [U for U in range(a + 6, a + 12) if U < min(len(UNITS2), unit_base[i + 1] + 3)]
                    product(0, step(f + 1, j, 2))
                    for U in split[0:1]:
                        low(U, j)
                    hidden_low(0, step(f + 1, j, 2))
                    for U in split[1:3]:
                        low(U, j)
                    product(1, step(f + 2, j, 2))
                    for U in split[3:4]:
                        low(U, j)
                    hidden_low(1, step(f + 2, j, 2))
                    for U in split[4:]:
                        low(U, j)

                with dve.Fori(0, FFN_PAIRS - 2) as j:
                    pair(a + 5, f0 + 2, j)
                pair(a + 5 + 6 * (FFN_PAIRS - 2), f0 + FFN_CHUNKS - 2)

            def mix(i, n):
                u0 = unit_base[i]

                def projected(unit, kind, blocks, tiles):
                    if 1 not in tiles:
                        return
                    b = blocks[0]
                    if kind == "v":
                        dve.wait_ge(s_used, u0 + unit + 2)
                        src = B[PB2["v", b]][:, :].rearrange("p (t b n) -> p t b n", t=2, b=2)
                        dst = FV[:, :, :].rearrange("p t (b n) -> p t b n", n=P)[:, :, b:blocks[1] + 1:blocks[1] - b, :]
                        for t in range(2):
                            last = CP(dst[:, t], src[:, t])
                        last.then_inc(*done("v2_ready", n, b))
                    elif b % 2:
                        dve.wait_ge(s_used, u0 + unit + 1)
                        TS(FQ[:, b, :], B[PB2["qk", b]][:, 0:T], QKSC[b], None, ALU.mult).then_inc(*done("qk_ready_dve", n, b))
                    for q in range(len(blocks)):
                        low(u0 + unit + q + SPLIT)

                for product in PROJ2_AHEAD:
                    projected(*product)
                if n == 0:
                    dve.wait_ge(M.sem("alibi_loaded"), 16)
                dve.wait_ge(*at("lambda_ready", n))

                def unit_bias(u):
                    hd = u if u < N_DIL else N_DIL + (u - N_DIL) // 2
                    dve.wait_ge(*at("scores2", n, u))
                    if u >= 2:
                        dve.wait_ge(*at("exp2_ready", n, u - 2))
                    for qt, (a, w) in enumerate(((0, P), (P, T))):
                        last = dve.tensor_tensor_reduce(out=S2[:, u % 2, a:a + w], in0=B[u % 2][:, a:a + w], in1=alibi[:, hd, a:a + w], scale=-1.0, scalar=-NEG, op0=ALU.add, op1=ALU.min, accum_out=stat[:, 16 + 2 * (u % 2) + qt:17 + 2 * (u % 2) + qt])
                    last.then_inc(*done("neg_max2", n, u))

                def unit_norm(u):
                    dve.wait_ge(*at("exp2_ready", n, u))
                    dve.reciprocal(stat[:, 54 + 2 * (u % 2):56 + 2 * (u % 2)], stat[:, 20 + 2 * (u % 2):22 + 2 * (u % 2)]).then_inc(*done("inverse2", n, u))
                    dve.wait_ge(*at("inverse2", n, u))
                    second = u >= N_DIL and (u - N_DIL) % 2
                    if second:
                        TS(stat[:, 58:60], stat[:, 54 + 2 * (u % 2):56 + 2 * (u % 2)], lamv[:, n, 4:5], None, ALU.mult).then_inc(*done("lambda_scaled", n, u))
                        dve.wait_ge(*at("lambda_scaled", n, u))
                        dve.wait_ge(*at("p2_ready", n, u - 1))
                        for qt, (a, w) in enumerate(((0, P), (P, T))):
                            last = STT(SS[:, u % 4, a:a + w], SS[:, u % 4, a:a + w], stat[:, 58 + qt:59 + qt], SS[:, (u - 1) % 4, a:a + w], ALU.mult, ALU.add)
                    else:
                        for qt, (a, w) in enumerate(((0, P), (P, T))):
                            last = TS(SS[:, u % 4, a:a + w], SS[:, u % 4, a:a + w], stat[:, 54 + 2 * (u % 2) + qt:55 + 2 * (u % 2) + qt], None, ALU.mult)
                    last.then_inc(*done("p2_ready", n, u))

                def split_out(b, src, stage):
                    CP(HH[:, b, :], src).then_inc(*done("o_part", n, "high", b))
                    dve.wait_ge(*at("o_part", n, "high", b))
                    TTn(HL[:, b, :], src, HH[:, b, :].bitcast(F32), ALU.subtract).then_inc(*done(stage, n, b))

                def head_out(h):
                    b = h // 2
                    dve.wait_ge(*at("attn2", n, h))
                    CP(OB[:, b, :], B[4 + b % 2][:, 0:T]).then_inc(*done("ob_ready", n, b))

                for u in range(len(UNIT_HEAD) + 1):
                    if u < len(UNIT_HEAD):
                        unit_bias(u)
                        unit_norm(u)
                    for product in PROJ2_STEPS[u:u + 1]:
                        projected(*product)
                    if u and UNIT_HEAD[u - 1] is not None and UNIT_HEAD[u - 1] % 2:
                        head_out(UNIT_HEAD[u - 1])
                for b in range(3):
                    dve.wait_ge(*at("ob_ready", n, b))
                    split_out(b, OB[:, b, :], "o_ready")
                for b in range(2):
                    dve.wait_ge(*at("ob_root", n, b))
                    dve.reciprocal(sgate[:, b, :], sgate[:, b, :]).then_inc(*done("ob_inverse", n, b))
                    dve.wait_ge(*at("ob_inverse", n, b))
                    dve.wait_ge(*at("sub_gain", n))
                    STT(OB2[:, b, :], OB2[:, b, :], lamv[:, n, 5:6], sgate[:, b, :], ALU.mult, ALU.mult).then_inc(*done("o_part", n, "normed", b))
                    dve.wait_ge(*at("o_part", n, "normed", b))
                    split_out(3 + b, OB2[:, b, :], "o_ready")
                for group in SB_GROUPS:
                    for h in group:
                        dve.wait_ge(*at("z_ln", n, h))
                        STT(ZP[:, h, :], B[h % 4][:, 0:384], 0.0, ZE[:, h, :], ALU.max, ALU.add).then_inc(*done("softplus_ready", n, h))
                    for h in group:
                        dve.wait_ge(*at("z_less_sum", n, h))
                        STT(ZE[:, h, :], B[h % 4][:, 0:384], 0.0, gap, ALU.min, ALU.add).then_inc(*done("log_weight", n, h))
                for b in range(3):
                    dve.wait_ge(*at("attn3", n, 2 * b + 1))
                    split_out(5 + b, B[SB_OUT[b]][:, 0:T], "o_ready")
                for U in range(u0 + 24, u0 + 29):
                    low(U + SPLIT)

            for i, (kind, n) in enumerate(SITES):
                site_norm(i)
                for unit in range(3, SPLIT):
                    low(unit_base[i] + unit)
                if i == 1:
                    lambdas()
                (ffn if kind == "ffn" else mix)(i, n)
                site_tail(i)

        @block.tensor
        def _(pe):
            mm, tr = pe.matmul, pe.transpose
            readers = {b: [] for b in range(8)}

            def hand_over(b, *reads):
                old, readers[b] = readers[b], list(reads)
                return old

            pe.wait_ge(M.sem("vec_loaded"), 64)
            for r in hand_over(0, ("vec_T", 0)):
                pe.wait_ge(*at(*r))
            b = B[0]
            for q in range(3):
                last = tr(b[:, q * P:(q + 1) * P], vec[:, q, :], ident)
            last.then_inc(*done("vec_transposed"))

            def ada_product(L, s):
                pe.wait_ge(*at("silu_c"))
                if s == 0:
                    for r in hand_over(6, ("ada_copied", L, ADA_SLOTS - 1)):
                        pe.wait_ge(*at(*r))
                if s >= 2:
                    pe.wait_ge(*at("ada_copied", L, s - 2))
                n = base[("ada", L)] + s
                pe.wait_ge(*filled(n))
                for k in range(KD):
                    last = mm(B[6][ADA_AT[s % 2], 0:T], CS[:, k:16:8], cols(n)[:, k, :], start=(k == 0), stop=(k == KD - 1), skip_group_check=True)
                last.then_inc(*done("ada_rows", L, s))

            def ada_transpose(L, s):
                if s == 0:
                    for r in hand_over(7, ("ada_biased", L)):
                        pe.wait_ge(*at(*r))
                else:
                    pe.wait_ge(*at("ada_T", L, s - 1))
                pe.wait_ge(*at("ada_copied", L, s))
                for q in range(2):
                    blk = 2 * s + q
                    last = tr(B[7][:, 2 * blk:2 * blk + 2], ada_row[ADA_AT[s % 2], q * P:(q + 1) * P], ident[ADA_AT[s % 2], ADA_AT[s % 2]])
                last.then_inc(*done("ada_T", L, s))

            def layer(L):
                nq = TT if L == 0 else T
                nt = nq // P
                if L == 0:
                    for sl in range(ADA_SLOTS):
                        ada_product(0, sl)
                        if sl:
                            ada_transpose(0, sl - 1)
                    ada_transpose(0, ADA_SLOTS - 1)
                for c in range(KD):
                    for t in range(4):
                        pe.wait_ge(*at("x_scaled", "b1", L, t))
                    for r in hand_over(c % 4, ("hT_ready_act" if c % 2 == 0 else "hT_ready_dve", "b1", L, c)):
                        pe.wait_ge(*at(*r))
                    b = B[c % 4]
                    for t in range(4):
                        last = tr(b[:, t * P:(t + 1) * P], XN[:, t, c * P:(c + 1) * P], ident)
                    last.then_inc(*done("x_T", "b1", L, c))
                pe.wait_ge(M.sem("small_loaded"), SW * (L + 1))
                for r in hand_over(5, ("wsT_ready", L)):
                    pe.wait_ge(*at(*r))
                b = B[5]
                for g in range(4):
                    last = tr(b[:, g * P:(g + 1) * P], w_s[:, g, :], ident)
                last.then_inc(*done("ws_transposed", L))
                for c in range(KD):
                    pe.wait_ge(*at("hT_ready_act" if c % 2 == 0 else "hT_ready_dve", "b1", L, c))

                n0 = base[("win", L)]

                def project(name, j, n, lhs, out_rows, ncol, reader):
                    key = (name,) if j is None else (name, j)
                    bank = PB[L][name if j is None else key]
                    for r in hand_over(bank, reader):
                        pe.wait_ge(*at(*r))
                    b = B[bank]
                    for k in range(KD):
                        last = mm(b[out_rows, 0:ncol], lhs(k), hT[:, k, 0:ncol], start=(k == 0), stop=(k == KD - 1))
                    last.then_inc(*done("proj", L, *key))
                    return last

                def col(n, w, a, m):
                    return lambda k: cols(n, w)[:, k, a:a + m]

                allp = slice(0, P)

                def sq_sums():
                    for r in hand_over(6, ("q_root", L)):
                        pe.wait_ge(*at(*r))
                    for j in range(2):
                        pe.wait_ge(*at("q_part_ready", L, j))
                        last = mm(B[6][:, 0:nq], ones, sq[:, j, 0:nq], start=(j == 0), stop=(j == 1))
                    last.then_inc(*done("q_square_sum", L))
                    for r in hand_over(7, ("kv_root", L)):
                        pe.wait_ge(*at(*r))
                    pe.wait_ge(*at("kv_part_ready", L))
                    mm(B[7][:, :], ones, sq[:, 2, :], start=True, stop=True).then_inc(*done("kv_square_sum", L))

                pe.wait_ge(*filled(n0))
                for j in range(2):
                    project("q", j, n0, col(n0, 256, j * P, P), allp, nq, ("q_part_ready", L, j))
                n = n0 + 1
                pe.wait_ge(*filled(n))
                project("kv", None, n, col(n, 160, 0, P), allp, TT, ("kv_part_ready", L))
                project("kr", None, n, col(n, 160, P, ROPE), slice(NOPE, QK), TT, ("kr_copied", L))
                pe.wait_ge(*at("kr_swapped", L))
                project("krs", None, n, lambda k: w_krs[:, k, :], slice(NOPE, QK), T, ("kr_sin", L))
                for name, s, rd in (("a", 2, "a_ready"), ("g", 3, "conv_gate_ready"), ("f", 4, "f_ready"), ("u", 5, "u_ready")):
                    n = n0 + s
                    pe.wait_ge(*filled(n))
                    for j in range(2):
                        project(name, j, n, col(n, 256, j * P, P), allp, nq, (rd, L, j))
                    if name == "a":
                        sq_sums()
                n = n0 + 6
                pe.wait_ge(*filled(n))
                for t in range(nt):
                    for r in hand_over(PB[L]["v", t], ("v_copied", L, t)):
                        pe.wait_ge(*at(*r))
                    b = B[PB[L]["v", t]]
                    for k in range(KD):
                        last = mm(b[:, 0:256], hT[:, k, t * P:(t + 1) * P], cols(n)[:, k, :], start=(k == 0), stop=(k == KD - 1))
                    last.then_inc(*done("proj", L, "v", t))
                pe.wait_ge(M.sem("base_loaded"), 48)
                for t in range(nt):
                    for r in hand_over(6 + t % 2, ("fa_ready", L, t)):
                        pe.wait_ge(*at(*r))
                    b = B[6 + t % 2]
                    for j in range(2):
                        pe.wait_ge(*at("f_ready", L, j))
                        last = mm(b[:, j * 256:(j + 1) * 256], fT[:, j, t * P:(t + 1) * P], dft_d, start=True, stop=True)
                    last.then_inc(*done("fourier_feat", L, t))
                for s in range(4):
                    n = n0 + 7 + s
                    pe.wait_ge(*filled(n))
                    for q in range(2):
                        j = 2 * s + q
                        project("gate", j, n, col(n, 256, q * P, P), allp, nq, ("sg_ready", L, j))
                    if s == 0:
                        for m in range(2):
                            for r in hand_over(6 + m, ("f_mixed", L, m)):
                                pe.wait_ge(*at(*r))
                            b = B[6 + m]
                            for sg in range(nq // T):
                                q = 0
                                for tl in range(2):
                                    pe.wait_ge(*at("fa_ready", L, 2 * sg + tl))
                                    for cs in range(2):
                                        last = mm(b[:, sg * T:(sg + 1) * T], FA[:, 2 * sg + tl, m, cs * P:(cs + 1) * P], dft_n[:, cs, tl, :], start=(q == 0), stop=(q == 3))
                                        q += 1
                            last.then_inc(*done("fourier_tok", L, m))
                    if s == 1:
                        for m in range(2):
                            for r in hand_over(4 + m, ("four_branch", L, m)):
                                pe.wait_ge(*at(*r))
                            b = B[4 + m]
                            for j in range(2):
                                pe.wait_ge(*at("f_mixed", L, j))
                                last = mm(b[:, 0:nq], w_fo[:, j, m * P:(m + 1) * P], cacc[:, j, 0:nq], start=(j == 0), stop=(j == 1))
                            last.then_inc(*done("fourier_out", L, m))
                pe.wait_ge(*at("wsT_ready", L))
                for m in range(2):
                    for r in hand_over(6 + m, ("sgu_branch", L, m)):
                        pe.wait_ge(*at(*r))
                    b = B[6 + m]
                    for t in range(nt):
                        pe.wait_ge(*at("v_ready", L, t))
                        for gg in range(2):
                            g = 2 * m + gg
                            o = b[gg * 64:(gg + 1) * 64, t * P:(t + 1) * P]
                            mm(o, VN[:, t, g * 64:(g + 1) * 64], wsT[:, g, :], start=True, stop=False)
                            last = mm(o, ones[0:1, 0:64], bsrow[0:1, L, g * P:(g + 1) * P], start=False, stop=True)
                    last.then_inc(*done("sgu_mixed", L, m))
                for v in range(nq // T):
                    for hf in range(2):
                        for r in hand_over((2 * v + hf) % 4, ("gate_row_ready", L, v, hf)):
                            pe.wait_ge(*at(*r))
                        b = B[(2 * v + hf) % 4]
                        pe.wait_ge(*at("gate_diag_ready", L, v, hf))
                        mm(b[:, :], ones, gate_diag[:, hf, :], start=True, stop=True).then_inc(*done("gate_rows", L, v, hf))
                pe.wait_ge(*at("uq_swapped", L))
                for h in range(HEADS):
                    for r in hand_over(h % 2, ("q_copied", L, h)):
                        pe.wait_ge(*at(*r))
                    b = B[h % 2]
                    for j in range(2):
                        pe.wait_ge(*at("q_latent", L, j))
                        last = mm(b[0:QK, 0:nq], w_uq[:, j, h * QK:(h + 1) * QK], qp[:, j, 0:nq], start=(j == 0), stop=(j == 1))
                    last.then_inc(*done("q_heads", L, h))
                    for r in hand_over(2 + h % 2, ("q_sin", L, h)):
                        pe.wait_ge(*at(*r))
                    b = B[2 + h % 2]
                    for j in range(2):
                        last = mm(b[NOPE:QK, 0:T], w_uqs[:, j, h * ROPE:(h + 1) * ROPE], qp[:, j, 0:T], start=(j == 0), stop=(j == 1))
                    last.then_inc(*done("q_swapped", L, h))
                pe.wait_ge(*at("kv_latent", L))
                for h in range(HEADS):
                    for r in hand_over(h % 2, ("k_copied", L, h)):
                        pe.wait_ge(*at(*r))
                    b = B[h % 2]
                    mm(b[0:NOPE, :], w_ukv[:, h * P:h * P + NOPE], kvp, start=True, stop=True).then_inc(*done("k_heads", L, h))
                vcols = w_ukv.rearrange("p (h n) -> p h n", h=4)[:, :, NOPE:P]
                for t in range(4):
                    for r in hand_over(4 + t, ("v_heads_ready", L, t)):
                        pe.wait_ge(*at(*r))
                    b = B[4 + t]
                    mm(b[:, 0:256].rearrange("p (h n) -> p h n", h=4), kvp[:, t * P:(t + 1) * P], vcols, start=True, stop=True).then_inc(*done("v_heads", L, t))
                pe.wait_ge(*at("k_rope_ready", L))
                UNITS = [(seg, h) for seg in range(nq // T) for h in range(HEADS)]

                def scores(i):
                    seg, h = UNITS[i]
                    k0, keys = (0, TT) if seg == 0 else (T, T)
                    pe.wait_ge(*at("k_copied", L, h))
                    pe.wait_ge(*at("q_ready", L, h))
                    for qt in range(2):
                        for r in hand_over(qt, ("exp_ready", L, seg, h, qt)):
                            pe.wait_ge(*at(*r))
                        b = B[qt]
                        mm(b[:, 0:keys], Q[0:QK, h, seg * T + qt * P:seg * T + (qt + 1) * P], K[0:QK, h, k0:k0 + keys], start=True, stop=True).then_inc(*done("scores", L, seg, h, qt))

                def transposes(i):
                    seg, h = UNITS[i]
                    for qt in range(2):
                        for r in hand_over(2 + qt, ("pT_ready", L, seg, h, qt)):
                            pe.wait_ge(*at(*r))
                        b = B[2 + qt]
                        pe.wait_ge(*at("p_ready", L, seg, h, qt))
                        for kt in range(4 if seg == 0 else 2):
                            last = tr(b[:, kt * P:(kt + 1) * P], Pm[i % 2][:, qt, kt * P:(kt + 1) * P], ident)
                        last.then_inc(*done("p_T", L, seg, h, qt))

                def weighted(i):
                    seg, h = UNITS[i]
                    k0, nk = (0, 4) if seg == 0 else (2, 2)
                    b = B[4 + h // 2]
                    if h % 2 == 0:
                        for r in hand_over(4 + h // 2, ("attn_ready", L, h + 1, seg)):
                            pe.wait_ge(*at(*r))
                    for qt in range(2):
                        pe.wait_ge(*at("pT_ready", L, seg, h, qt))
                    for kt in range(nk):
                        pe.wait_ge(*at("v_heads_ready", L, k0 + kt))
                        last = mm(b[(h % 2) * 64:(h % 2 + 1) * 64, 0:T], V[:, k0 + kt, h * 64:(h + 1) * 64], PT[i % 2][:, kt, :], start=(kt == 0), stop=(kt == nk - 1))
                    last.then_inc(*done("attn", L, seg, h))

                scores(0)
                for i in range(len(UNITS)):
                    if i + 1 < len(UNITS):
                        scores(i + 1)
                    if L == 0:
                        for sl in ADA_STEP[i]:
                            ada_product(1, sl)
                    transposes(i)
                    if L == 0:
                        for sl in ADA_STEP[i]:
                            ada_transpose(1, sl)
                    if i:
                        weighted(i - 1)
                weighted(len(UNITS) - 1)
                for j in range(2):
                    pe.wait_ge(*at("conv_tap", L, j, CONV_K - 1))
                for r in hand_over(0, ("conv_centred", L, 1)):
                    pe.wait_ge(*at(*r))
                b = B[0]
                for j in range(2):
                    last = mm(b[:, 0:nq], ones, cacc[:, j, 0:nq], start=(j == 0), stop=(j == 1))
                last.then_inc(*done("conv_mean", L))

                def conv_var():
                    for r in hand_over(1, ("conv_root", L)):
                        pe.wait_ge(*at(*r))
                    for j in range(2):
                        pe.wait_ge(*at("conv_square", L, j))
                        last = mm(B[1][:, 0:nq], ones, sq[:, j, 0:nq], start=(j == 0), stop=(j == 1))
                    last.then_inc(*done("conv_var", L))

                def conv_out():
                    for m in range(2):
                        for r in hand_over(2 + m, ("conv_branch", L, m)):
                            pe.wait_ge(*at(*r))
                        for j in range(2):
                            pe.wait_ge(*at("conv_act", L, j))
                            last = mm(B[2 + m][:, 0:nq], w_pw[:, j, m * P:(m + 1) * P], csg[:, j, 0:nq], start=(j == 0), stop=(j == 1))
                        last.then_inc(*done("conv_out", L, m))

                def out_banks():
                    for t in range(nt):
                        for hf in range(2):
                            for r in hand_over(YB[L][t, hf], ("out_scaled", "b1", L, t, hf)):
                                pe.wait_ge(*at(*r))
                    for stage in ("four_branch", "sgu_branch"):
                        pe.wait_ge(*at(stage, L, 1))
                    pe.wait_ge(*at("attn_ready", L, HEADS - 1, nq // T - 1))

                def out_rows(s):
                    n = base[("wout", L)] + s
                    pe.wait_ge(*filled(n))
                    for r in range(2):
                        k = 2 * WOUT_ORDER[L][s] + r
                        for t in range(nt):
                            for hf in range(2):
                                final = s == 3 and r == 1
                                last = mm(B[YB[L][t, hf]][:, :], SG[:, k, t * P:(t + 1) * P], rows(n)[:, r, hf * 512:(hf + 1) * 512], start=(s == 0 and r == 0), stop=final, skip_group_check=True)
                                if final:
                                    last.then_inc(*done("y_ready", "b1", L, t, hf))
                    if s < 3:
                        last.then_inc(*done("wout_used", L, s))

                if L == 0:
                    conv_var()
                    conv_out()
                    out_banks()
                    for s in range(3):
                        out_rows(s)
                else:
                    out_banks()
                    out_rows(0)
                    conv_var()
                    out_rows(1)
                    conv_out()
                    out_rows(2)
                pe.wait_ge(*at("conv_branch", L, 1))
                out_rows(3)

            def site_norm(i):
                for t in range(2):
                    pe.wait_ge(*at("x_scaled", "site", i, t))
                    for b in range(4):
                        if t == 0:
                            for r in hand_over(b, ("input_ready", i, b)):
                                pe.wait_ge(*at(*r))
                        for q in range(2):
                            c = 2 * b + q
                            last = tr(B[b][:, q * T + t * P:q * T + (t + 1) * P], XN2[:, t, c * P:(c + 1) * P], ident)
                        if t:
                            last.then_inc(*done("x_T", "site", i, b))

            def three(o, lhs, rhs, start, stop):
                for m, (x, y) in enumerate(((0, 0), (0, 1), (1, 0))):
                    last = mm(o, lhs(x), rhs(y), start=start and m == 0, stop=stop and m == 2, skip_group_check=True)
                return last

            W, H, HB = (WH, WL), (HH, HL), (HBH, HBL)

            def feature_major(o, U, site=None):
                for k in range(KD):
                    if site is not None and k % 2 == 0:
                        pe.wait_ge(*at("input_ready", site, k // 2))
                    last = three(o, lambda x: unit_in(W[x], U)[:, k, :], lambda y: H[y][:, k, :], k == 0, k == KD - 1)
                return last

            def ffn(i, n):
                f0 = n * FFN_CHUNKS
                for q in range(4):
                    for r in hand_over(q):
                        pe.wait_ge(*at(*r))
                for t in range(2):
                    for hf in range(2):
                        for r in hand_over(4 + 2 * t + hf, ("out_scaled", "site", i, t, hf)):
                            pe.wait_ge(*at(*r))

                def gate_up(par, U, free, j=None, site=None):
                    if free is not None:
                        pe.wait_ge(s_h, free)
                    for q in range(2):
                        pe.wait_ge(s_low, step(U + q + 1, j, 6))
                        feature_major(B[par][:, q * T:(q + 1) * T], U + q, site if q == 0 else None).then_inc(s_used, 1)

                def down(par, U, ready, first, final, j=None):
                    pe.wait_ge(s_hl, ready)
                    pe.wait_ge(s_low, step(U + 1, j, 6))
                    for t in range(2):
                        for hf in range(2):
                            last = three(B[4 + 2 * t + hf][:, :], lambda x: HB[x][:, par, t * P:(t + 1) * P], lambda y: W[y][:, U % SPLIT, hf * 512:(hf + 1) * 512], first, final)
                            if final and (t, hf) != (1, 1):
                                last.then_inc(*done("y_ready", "site", i, t, hf))
                    last.then_inc(s_used, 1)

                a = unit_base[i]
                gate_up(0, a, f0 if n else None, None, i)
                gate_up(1, a + 2, f0 if n else None)
                down(0, a + 4, f0 + 1, True, False)

                def pair(a, f, j=None):
                    gate_up(0, a, step(f - 1, j, 2), j)
                    down(1, a + 2, step(f, j, 2), False, False, j)
                    gate_up(1, a + 3, step(f, j, 2), j)
                    down(0, a + 5, step(f + 1, j, 2), False, False, j)

                with pe.Fori(0, FFN_PAIRS - 2) as j:
                    pair(a + 5, f0 + 2, j)
                pair(a + 5 + 6 * (FFN_PAIRS - 2), f0 + FFN_CHUNKS - 2)
                down(1, a + 6 * FFN_PAIRS - 1, f0 + FFN_CHUNKS, False, True)

            def mix(i, n):
                u0 = unit_base[i]

                def product(unit, kind, blocks, tiles):
                    U, b = u0 + unit, blocks[0]
                    if kind == "qk":
                        for r in hand_over(PB2[kind, b], ("qk_ready_act" if b % 2 == 0 else "qk_ready_dve", n, b)):
                            pe.wait_ge(*at(*r))
                        pe.wait_ge(s_low, U + 1)
                        feature_major(B[PB2[kind, b]][:, 0:T], U, i if unit == 0 else None).then_inc(s_used, 1)
                    else:
                        if 0 in tiles:
                            for r in hand_over(PB2[kind, b], ("v2_ready", n, b)):
                                pe.wait_ge(*at(*r))
                        pe.wait_ge(s_low, U + 2)
                        wide = [w[:, U % SPLIT:U % SPLIT + 2, :].rearrange("p u (k n) -> p k u n", k=8) for w in W]
                        for t in tiles:
                            o = B[PB2[kind, b]][:, t * T:(t + 1) * T].rearrange("p (u n) -> p u n", u=2)
                            for k in range(KD):
                                last = three(o, lambda x: H[x][:, k, t * P:(t + 1) * P], lambda y: wide[y][:, k], k == 0, k == KD - 1)
                        if 1 in tiles:
                            last.then_inc(s_used, 2)

                def score(u):
                    if u < N_DIL:
                        qb, kb, p0, kk = u // 2, 3 + u // 2, (u % 2) * 64, 64
                    else:
                        d = u - N_DIL
                        qb, kb, p0, kk = 6 + d // 4, 8 + d // 4, (d % 4) * 32, 32
                    for b in (qb, kb):
                        pe.wait_ge(*at("qk_ready_act" if b % 2 == 0 else "qk_ready_dve", n, b))
                    for r in hand_over(u % 2, ("neg_max2", n, u)):
                        pe.wait_ge(*at(*r))
                    b = B[u % 2]
                    mm(b[:, 0:P], FQ[p0:p0 + kk, qb, 0:P], FQ[p0:p0 + kk, kb, 0:P], start=True, stop=True)
                    mm(b[:, P:384], FQ[p0:p0 + kk, qb, P:T], FQ[p0:p0 + kk, kb, :], start=True, stop=True).then_inc(*done("scores2", n, u))

                def value(h, u):
                    for r in hand_over(2 + h % 2, ("pT2_ready", n, h)):
                        pe.wait_ge(*at(*r))
                    b = B[2 + h % 2]
                    pe.wait_ge(*at("p2_ready", n, u))
                    src = SS[:, u % 4, :]
                    tr(b[:, 0:P], src[:, 0:P], ident)
                    tr(b[:, P:T], src[:, P:T], ident)
                    tr(b[:, T:384], src[:, T:384], ident).then_inc(*done("p2_T", n, h))

                def weighted(h):
                    blk = h // 2
                    if h % 2 == 0:
                        for r in hand_over(4 + blk % 2, ("ob_ready", n, blk)):
                            pe.wait_ge(*at(*r))
                    o = B[4 + blk % 2][(h % 2) * 64:(h % 2 + 1) * 64, :]
                    pe.wait_ge(*at("pT2_ready", n, h))
                    pe.wait_ge(*at("v2_ready", n, 2 if h < N_DIL else 3))
                    mm(o[:, 0:T], FV[:, 0, h * 64:(h + 1) * 64], PT2[:, h % 2, 0:T], start=True, stop=False, skip_group_check=True)
                    mm(o[:, P:T], FV[:, 1, h * 64:(h + 1) * 64], PT2[:, h % 2, T:384], start=False, stop=True, skip_group_check=True).then_inc(*done("attn2", n, h))

                for step_product in PROJ2_AHEAD:
                    product(*step_product)
                for u in range(len(UNIT_HEAD) + 1):
                    h = UNIT_HEAD[u - 1] if u else None
                    if u < len(UNIT_HEAD):
                        score(u)
                    if h is not None:
                        value(h, u - 1)
                    for step_product in PROJ2_STEPS[u:u + 1]:
                        product(*step_product)
                    if h is not None:
                        weighted(h)
                def z(h):
                    for r in hand_over(h % 4, ("log_weight", n, h)):
                        pe.wait_ge(*at(*r))
                    b = B[h % 4]
                    p0, qb, kb = (h % 2) * 64, 10 + h // 2, 13 + h // 2
                    for blk in (qb, kb):
                        pe.wait_ge(*at("qk_ready_act" if blk % 2 == 0 else "qk_ready_dve", n, blk))
                    mm(b[:, 0:T], FQ[p0:p0 + 64, kb, 0:P], FQ[p0:p0 + 64, qb, :], start=True, stop=False, skip_group_check=True)
                    mm(b[:, T:384], FQ[p0:p0 + 64, kb, P:T], FQ[p0:p0 + 64, qb, P:T], start=False, stop=False, skip_group_check=True).then_inc(*done("z_ready", n, h))

                def less_sums(h):
                    pe.wait_ge(*at("softplus_masked", n, h))
                    mm(B[h % 4][:, 0:384], ntri, ZP[:, h, :], start=False, stop=False, skip_group_check=True)
                    mm(B[h % 4][:, P:T], negones, ZP[:, h, T:384], start=False, stop=True, skip_group_check=True).then_inc(*done("z_less_sum", n, h))

                def out_rows(k):
                    U = u0 + 24 + k
                    pe.wait_ge(s_low, U + 1)
                    pe.wait_ge(*at("o_ready", n, k))
                    for t in range(2):
                        for hf in range(2):
                            last = three(B[4 + 2 * t + hf][:, :], lambda x: H[x][:, k, t * P:(t + 1) * P], lambda y: W[y][:, U % SPLIT, hf * 512:(hf + 1) * 512], k == 0, k == KD - 1)
                            if k == KD - 1 and (t, hf) != (1, 1):
                                last.then_inc(*done("y_ready", "site", i, t, hf))
                    last.then_inc(s_used, 1)

                for h in SB_GROUPS[0]:
                    z(h)
                for b in range(2):
                    pe.wait_ge(*at("ob_square", n, b))
                    for r in hand_over(4 + b, ("ob_root", n, b)):
                        pe.wait_ge(*at(*r))
                    mm(B[4 + b][:, T:TT], heads2, sgate[:, b, :], start=True, stop=True).then_inc(*done("ob_sum", n, b))
                for t in range(2):
                    for hf in range(2):
                        for r in hand_over(4 + 2 * t + hf, ("out_scaled", "site", i, t, hf)):
                            pe.wait_ge(*at(*r))
                out_rows(0)
                out_rows(1)
                for h in SB_GROUPS[0]:
                    less_sums(h)
                out_rows(2)
                for h in SB_GROUPS[1]:
                    z(h)
                out_rows(3)
                out_rows(4)
                for h in SB_GROUPS[1]:
                    less_sums(h)
                for h in range(N_SB):
                    if h % 2 == 0:
                        for r in hand_over(SB_OUT[h // 2], ("o_ready", n, 5 + h // 2)):
                            pe.wait_ge(*at(*r))
                    o = B[SB_OUT[h // 2]][(h % 2) * 64:(h % 2 + 1) * 64, :]
                    pe.wait_ge(*at("weight_ready", n, h))
                    pe.wait_ge(*at("v2_ready", n, 5))
                    hv = N_DIL + N_DIFF + h
                    mm(o[:, 0:T], FV[:, 0, hv * 64:(hv + 1) * 64], ZP[:, h, 0:T], start=True, stop=False, skip_group_check=True)
                    mm(o[:, P:T], FV[:, 1, hv * 64:(hv + 1) * 64], ZP[:, h, T:384], start=False, stop=True, skip_group_check=True).then_inc(*done("attn3", n, h))
                for k in range(5, KD):
                    out_rows(k)

            layer(0)
            layer(1)
            for i, (kind, n) in enumerate(SITES):
                site_norm(i)
                (ffn if kind == "ffn" else mix)(i, n)


INPUTS = ["x", "c", "ctx", "c_ctx", "w_ada", "w_in", "w_uq", "w_ukv", "w_pw", "w_fourier", "sgu_ln_g", "sgu_ln_b", "w_s", "b_s",
          "w_out", "final_g", "norm_gains_2", "w_ffn_gate_2", "w_ffn_up_2", "w_ffn_down_2", "w_in_2", "w_out_2", "diff_lambda_2"]
VECTORS = ["b_ada", "norm_g", "q_norm_g", "kv_norm_g", "conv_w", "conv_b", "conv_ln_g", "conv_ln_b", "b_pw", "b_fourier"]


def kernel(**inputs):
    import numpy as _np
    import concourse.bacc as _bacc
    from contextlib import ExitStack as _ExitStack
    from concourse import mybir as _mybir
    from concourse.bass_utils import run_bass_kernel_spmd as _run

    a = {k: _np.asarray(v) for k, v in inputs.items()}
    arrays = {n: _np.ascontiguousarray(a[n]) for n in INPUTS if n not in ("c", "c_ctx")}
    banks = []
    for L in range(2):
        rows = [a[n][L].reshape(-1, 128) for n in VECTORS] + [a["c"].reshape(-1, 128), a["c_ctx"].reshape(-1, 128)]
        rows.append(_np.zeros((128 - sum(r.shape[0] for r in rows), 128), _np.float32))
        banks.append(_np.concatenate(rows))
    arrays["k_vec1"] = _np.stack(banks)
    rows = [a["norm_gains_2"][i // 3, 2 * (i % 3)].reshape(-1, 128) for i in range(6)]
    rows += [_np.concatenate([a["diff_subln_gain_2"][m]] * 2)[None] for m in range(2)]
    rows.append(_np.zeros((128 - 50, 128), _np.float32))
    arrays["k_vec2"] = _np.concatenate(rows)
    arrays.update(constants())

    def build(table):
        nc = _bacc.Bacc("TRN2", target_bir_lowering=False, num_devices=1)
        I = {n: nc.dram_tensor("in_" + n, v.shape, _mybir.dt.from_np(v.dtype), kind="ExternalInput").ap() for n, v in arrays.items()}
        out = nc.dram_tensor("out_0", (1, 256, 1024), _mybir.dt.float32, kind="ExternalOutput").ap()
        program(nc, I, out, table)
        return nc

    table = {}
    build(table)
    nc = build(table)
    r = _run(nc, [{"in_" + n: v for n, v in arrays.items()}], core_ids=[0])
    return r.results[0]["out_0"]
```
